# Optimizing a Trainium2 kernel written in Bass

```python
import math
import jax, jax.numpy as jnp
from jax import lax
import numpy as np

D_MODEL = 1024
BATCH = 1
SEQ = 256
DEPTH = 2

HEAD_DIM = 64
N_HEADS_SB = 8
N_HEADS_MOBA = 8
W_SB = N_HEADS_SB * HEAD_DIM
W_MOBA = N_HEADS_MOBA * HEAD_DIM
N_BRANCH = 2
IN_COLS = 3 * W_SB + 3 * W_MOBA + N_BRANCH * D_MODEL
SB_Q_BLOCK = 128
MOBA_BLOCK = 256
MOBA_TOPK = 3
MOBA_Q_CHUNK = 16
REL_BUCKETS = 32
REL_MAX_DIST = 128
D_FF = 3584
N_EXPERTS = 8
TOP_K = 2
D_FF_EXPERT = 3584
N_DENSE = (DEPTH + 1) // 2
N_MOE = DEPTH // 2
N_MOD = 6
EPS = 1e-6
NEG_INF = -1e30

kernel_name = 'hybrid_stickbreak_moba_moe_block'

def rms_norm(x, g):
    xf = x.astype(jnp.float32)
    y = xf * lax.rsqrt(jnp.mean(xf * xf, axis=-1, keepdims=True) + EPS)
    return (y * g.astype(jnp.float32)).astype(x.dtype)

def rel_bucket(dist):
    max_exact = REL_BUCKETS // 2
    n = jnp.maximum(dist, 0)
    nf = jnp.maximum(n, 1).astype(jnp.float32)
    large = max_exact + (jnp.log(nf / max_exact) / math.log(REL_MAX_DIST / max_exact)
                         * (REL_BUCKETS - max_exact)).astype(jnp.int32)
    large = jnp.minimum(large, REL_BUCKETS - 1)
    return jnp.where(n < max_exact, n, large)

def stick_breaking_attention(q, k, v):
    B, H, S, Dh = q.shape
    nq = S // SB_Q_BLOCK
    scale = Dh ** -0.5
    kpos = jnp.arange(S)
    qb = q.reshape(B, H, nq, SB_Q_BLOCK, Dh).transpose(2, 0, 1, 3, 4)

    def block(args):
        i, qi = args
        qpos = i * SB_Q_BLOCK + jnp.arange(SB_Q_BLOCK)
        z = jnp.einsum('bhqd,bhkd->bhqk', qi, k).astype(jnp.float32) * scale
        mask = kpos[None, :] < qpos[:, None]
        log_1m = jnp.where(mask, -jax.nn.softplus(z), 0.0)
        suffix = lax.cumsum(log_1m, axis=3, reverse=True) - log_1m
        att = jnp.where(mask, jnp.exp(jax.nn.log_sigmoid(z) + suffix), 0.0)
        return jnp.einsum('bhqk,bhkd->bhqd', att.astype(v.dtype), v)

    out = lax.map(block, (jnp.arange(nq), qb))
    return out.transpose(1, 2, 0, 3, 4).reshape(B, H, S, Dh)

def moba_attention(q, k, v, rel_bias):
    B, H, S, Dh = q.shape
    nb = -(-S // MOBA_BLOCK)
    sp = nb * MOBA_BLOCK
    pad = ((0, 0), (0, 0), (0, sp - S), (0, 0))
    kp = jnp.pad(k, pad)
    vp = jnp.pad(v, pad)
    kblk = kp.reshape(B, H, nb, MOBA_BLOCK, Dh)
    vblk = vp.reshape(B, H, nb, MOBA_BLOCK, Dh)
    kmean = jnp.mean(kblk, axis=3)
    n_sel = min(MOBA_TOPK, nb)
    scale = Dh ** -0.5
    nc = S // MOBA_Q_CHUNK
    qc = q.reshape(B, H, nc, MOBA_Q_CHUNK, Dh).transpose(2, 0, 1, 3, 4)
    bidx = jnp.arange(B)[:, None, None, None]
    hidx = jnp.arange(H)[None, :, None, None]
    hidx5 = jnp.arange(H)[None, :, None, None, None]
    blk_off = jnp.arange(MOBA_BLOCK)
    bias_t = rel_bias.T

    def chunk(args):
        i, qi = args
        qpos = i * MOBA_Q_CHUNK + jnp.arange(MOBA_Q_CHUNK)
        own = (i * MOBA_Q_CHUNK) // MOBA_BLOCK
        gate = jnp.einsum('bhqd,bhnd->bhqn', qi, kmean).astype(jnp.float32)
        gate = jnp.where(jnp.arange(nb) < own, gate, NEG_INF)
        _, sel = lax.top_k(gate, n_sel)
        sel_valid = sel < own
        ks = kblk[bidx, hidx, sel]
        vs = vblk[bidx, hidx, sel]
        s_sel = jnp.einsum('bhqd,bhqnkd->bhqnk', qi, ks).astype(jnp.float32) * scale
        spos_sel = sel[..., None] * MOBA_BLOCK + blk_off
        bias_sel = bias_t[hidx5, rel_bucket(qpos[:, None, None] - spos_sel)]
        s_sel = jnp.where(sel_valid[..., None], s_sel + bias_sel.astype(jnp.float32), NEG_INF)
        ko = lax.dynamic_slice_in_dim(kp, own * MOBA_BLOCK, MOBA_BLOCK, axis=2)
        vo = lax.dynamic_slice_in_dim(vp, own * MOBA_BLOCK, MOBA_BLOCK, axis=2)
        s_own = jnp.einsum('bhqd,bhkd->bhqk', qi, ko).astype(jnp.float32) * scale
        dist = qpos[:, None] - (own * MOBA_BLOCK + blk_off)[None, :]
        bias_own = bias_t[:, rel_bucket(dist)]
        s_own = jnp.where(dist >= 0, s_own + bias_own.astype(jnp.float32), NEG_INF)
        logits = jnp.concatenate([s_sel.reshape(B, H, MOBA_Q_CHUNK, n_sel * MOBA_BLOCK), s_own], axis=-1)
        p = jax.nn.softmax(logits, axis=-1).astype(v.dtype)
        p_sel = p[..., :n_sel * MOBA_BLOCK].reshape(B, H, MOBA_Q_CHUNK, n_sel, MOBA_BLOCK)
        p_own = p[..., n_sel * MOBA_BLOCK:]
        return (jnp.einsum('bhqnk,bhqnkd->bhqd', p_sel, vs)
                + jnp.einsum('bhqk,bhkd->bhqd', p_own, vo))

    out = lax.map(chunk, (jnp.arange(nc), qc))
    return out.transpose(1, 2, 0, 3, 4).reshape(B, H, S, Dh)

def hybrid_mixer(h, w_in, w_proj_sb, w_proj_moba, w_out, rel_bias):
    B, S, _ = h.shape
    proj = h @ w_in
    qkv_sb, qkv_moba, gates = jnp.split(proj, [3 * W_SB, 3 * W_SB + 3 * W_MOBA], axis=-1)

    def heads(t, nh):
        return t.reshape(B, S, 3, nh, HEAD_DIM).transpose(2, 0, 3, 1, 4)

    q_a, k_a, v_a = heads(qkv_sb, N_HEADS_SB)
    o_a = stick_breaking_attention(q_a, k_a, v_a)
    o_a = o_a.transpose(0, 2, 1, 3).reshape(B, S, W_SB) @ w_proj_sb
    q_b, k_b, v_b = heads(qkv_moba, N_HEADS_MOBA)
    o_b = moba_attention(q_b, k_b, v_b, rel_bias)
    o_b = o_b.transpose(0, 2, 1, 3).reshape(B, S, W_MOBA) @ w_proj_moba
    g_a, g_b = jnp.split(gates, 2, axis=-1)
    merged = jax.nn.sigmoid(g_a) * o_a + jax.nn.sigmoid(g_b) * o_b
    return merged @ w_out

def swiglu(h, w1, w3, w2):
    return (jax.nn.silu(h @ w1) * (h @ w3)) @ w2

def moe_swiglu(h, w_router, w1, w3, w2):
    logits = (h @ w_router).astype(jnp.float32)
    top_v, top_i = lax.top_k(logits, TOP_K)
    top_w = jax.nn.softmax(top_v, axis=-1)
    combine = jnp.sum(jax.nn.one_hot(top_i, N_EXPERTS, dtype=jnp.float32) * top_w[..., None], axis=-2)
    combine = combine.astype(h.dtype)
    out = jnp.zeros_like(h)
    for e in range(N_EXPERTS):
        out = out + combine[..., e:e + 1] * swiglu(h, w1[e], w3[e], w2[e])
    return out

def modulate_in(x, g_pre, shift, scale):
    return rms_norm(x, g_pre) * (1 + scale[:, None, :]) + shift[:, None, :]

def residual_out(x, y, g_post, gate):
    return x + gate[:, None, :] * rms_norm(y, g_post)

def setup_inputs(seed: int = 0) -> dict:
    key = jax.random.key(seed)
    ks = jax.random.split(key, 20)
    f32 = jnp.float32

    def w(k, shape, fan_in, mult=1.0):
        return jax.random.normal(k, shape, f32) * (mult * fan_in ** -0.5)

    def gain(k, shape):
        return 1.0 + 0.05 * jax.random.normal(k, shape, f32)

    return {
        'x': jax.random.normal(ks[0], (BATCH, SEQ, D_MODEL), f32),
        'c': jax.random.normal(ks[1], (BATCH, D_MODEL), f32),
        'w_mod': w(ks[2], (DEPTH, D_MODEL, N_MOD * D_MODEL), D_MODEL, 0.5),
        'b_mod': 0.01 * jax.random.normal(ks[3], (DEPTH, N_MOD * D_MODEL), f32),
        'g_mix_pre': gain(ks[4], (DEPTH, D_MODEL)),
        'g_mix_post': gain(ks[5], (DEPTH, D_MODEL)),
        'g_ffn_pre': gain(ks[6], (DEPTH, D_MODEL)),
        'g_ffn_post': gain(ks[7], (DEPTH, D_MODEL)),
        'w_in': w(ks[8], (DEPTH, D_MODEL, IN_COLS), D_MODEL),
        'w_proj_sb': w(ks[9], (DEPTH, W_SB, D_MODEL), W_SB),
        'w_proj_moba': w(ks[10], (DEPTH, W_MOBA, D_MODEL), W_MOBA),
        'w_out': w(ks[11], (DEPTH, D_MODEL, D_MODEL), D_MODEL),
        'rel_bias': 0.5 * jax.random.normal(ks[12], (REL_BUCKETS, N_HEADS_MOBA), f32),
        'w1_dense': w(ks[13], (N_DENSE, D_MODEL, D_FF), D_MODEL),
        'w3_dense': w(ks[14], (N_DENSE, D_MODEL, D_FF), D_MODEL),
        'w2_dense': w(ks[15], (N_DENSE, D_FF, D_MODEL), D_FF),
        'w_router': w(ks[16], (N_MOE, D_MODEL, N_EXPERTS), D_MODEL),
        'w1_moe': w(ks[17], (N_MOE, N_EXPERTS, D_MODEL, D_FF_EXPERT), D_MODEL),
        'w3_moe': w(ks[18], (N_MOE, N_EXPERTS, D_MODEL, D_FF_EXPERT), D_MODEL),
        'w2_moe': w(ks[19], (N_MOE, N_EXPERTS, D_FF_EXPERT, D_MODEL), D_FF_EXPERT),
    }

def reference(x, c, w_mod, b_mod, g_mix_pre, g_mix_post, g_ffn_pre, g_ffn_post, w_in, w_proj_sb,
              w_proj_moba, w_out, rel_bias, w1_dense, w3_dense, w2_dense, w_router, w1_moe, w3_moe,
              w2_moe):
    cond = jax.nn.silu(c)
    for l in range(DEPTH):
        mod = cond @ w_mod[l] + b_mod[l]
        sh_mix, sc_mix, gt_mix, sh_ffn, sc_ffn, gt_ffn = jnp.split(mod, N_MOD, axis=-1)
        h = modulate_in(x, g_mix_pre[l], sh_mix, sc_mix)
        y = hybrid_mixer(h, w_in[l], w_proj_sb[l], w_proj_moba[l], w_out[l], rel_bias)
        x = residual_out(x, y, g_mix_post[l], gt_mix)
        h = modulate_in(x, g_ffn_pre[l], sh_ffn, sc_ffn)
        if l % 2 == 0:
            y = swiglu(h, w1_dense[l // 2], w3_dense[l // 2], w2_dense[l // 2])
        else:
            y = moe_swiglu(h, w_router[l // 2], w1_moe[l // 2], w3_moe[l // 2], w2_moe[l // 2])
        x = residual_out(x, y, g_ffn_post[l], gt_ffn)
    return x


_drawn_inputs = setup_inputs


def setup_inputs(seed=0):
    import zlib

    import numpy as np

    out = dict(_drawn_inputs(seed))
    spreads = {}
    factors = {}
    for name, (base, spread) in spreads.items():
        noise = np.random.default_rng([zlib.crc32(name.encode()), seed]).standard_normal(out[name].shape)
        drawn = base * np.exp(spread * noise) if base else spread * noise
        out[name] = __import__('jax').numpy.asarray(drawn.astype(out[name].dtype))
    for name, factor in factors.items():
        out[name] = (out[name] * factor).astype(out[name].dtype)
    return out
```

```python
from contextlib import ExitStack

import concourse.bass as bass
from concourse import mybir

F32 = mybir.dt.float32
F32R = mybir.dt.float32r
I32 = mybir.dt.int32
ALU = mybir.AluOpType
ACT = mybir.ActivationFunctionType
AX = mybir.AxisListType.X

P = 128
D = 1024
KC = D // P
S = 256
C = S // P
DH = 64
HEADS = 8
DEPTH = 2
NB = 512
UNIT = 2048
FF = 3584
FBLK = FF // NB
E = 8
EXTRA = 3
ITEMS = E + EXTRA
BUCKETS = 32
BLK = 10
MIX_UNITS = 28
FFN_UNITS = 6 * FBLK
RAW = 6
SPLIT = 3
LEAD = 2
MODS = 48
MRAW = 2
EPS = 1e-6
NEG = -1e30
DIST = S + P - 1

MIX0 = 0
FFN0 = MIX0 + MIX_UNITS
MIX1 = FFN0 + FFN_UNITS
MOE0 = MIX1 + MIX_UNITS
FFN_BASE = [0, 2 * FBLK]


def build(nc, x_d, c_d, w_mod, b_mod, g_mix_pre, g_mix_post, g_ffn_pre, g_ffn_post, w_in, w_psb, w_pmo, w_out,
          rel_bias, w1_d, w3_d, w2_d, w_router, w1_m, w3_m, w2_m, onehot_d, dist_scratch, out_d):
    with ExitStack() as ctx:
        def sb(name, shape, dt=F32):
            return ctx.enter_context(nc.sbuf_tensor(name, shape, dt))

        def sem(name):
            return ctx.enter_context(nc.semaphore(name))

        raw = sb("raw", [P, RAW, UNIT])
        whi = sb("whi", [P, SPLIT, UNIT], F32R)
        wlo = sb("wlo", [P, SPLIT, UNIT], F32R)
        mraw = sb("mraw", [P, MRAW, KC, P])
        macc = sb("macc", [P, P])
        x = sb("x", [P, C, D])
        hhi = sb("hhi", [P, KC, S], F32R)
        hlo = sb("hlo", [P, KC, S], F32R)
        ohi = sb("ohi", [P, KC, S], F32R)
        olo = sb("olo", [P, KC, S], F32R)
        wide = sb("wide", [P, 2 * C * D])
        gates = wide[:].rearrange("p (c n) -> p c n", c=C)
        xn = wide[:, 0:C * D].rearrange("p (c n) -> p c n", c=C)
        yacc = wide[:, C * D:2 * C * D].rearrange("p (c n) -> p c n", c=C)
        vals = sb("vals", [P, 2, C, NB])
        h32 = vals[:].rearrange("p b c n -> p (b c n)").rearrange("p (k t) -> p k t", k=KC)
        gat = vals[:, 1, 0, 0:S].rearrange("p (c s) -> p c s", c=C)
        gatT = vals[:, 1, 0, S:2 * S]
        h32e = vals[:, 0, :, :].rearrange("p c n -> p (c n)").rearrange("p (k t) -> p k t", k=KC)
        qk = sb("qk", [P, 4 * 4 * S])
        qkT = qk[:].rearrange("p (b c t) -> p b c t", b=4, c=4)
        merged = qk[:, 0:C * D].rearrange("p (c n) -> p c n", c=C)
        mtmp = qk[:, 2048:3072].rearrange("p (c n) -> p c n", c=C)
        hid = qk[:, 0:C * NB].rearrange("p (c n) -> p c n", c=C)
        silu = qk[:, C * NB:2 * C * NB].rearrange("p (c n) -> p c n", c=C)
        ysb = qk[:, 2048:3072]
        gdiag = qk[:, 3072:4096]
        bias = sb("bias", [P, HEADS, S])
        gate = sb("gate", [P, D])
        eb = sb("eb", [P, 2, 384])
        at = sb("at", [P, 2, 384])
        ident = sb("ident", [P, P])
        upper = sb("upper", [P, P])
        lower = sb("lower", [P, P])
        ones = sb("ones", [P, P])
        iota = sb("iota", [P, P])
        modT = sb("modT", [P, DEPTH * MODS])
        colsB = sb("colsB", [P, 72])
        colsM = sb("colsM", [P, DEPTH * MODS])
        cond = sb("cond", [P, KC])
        wr = sb("wr", [P, KC, E])
        ss = sb("ss", [P, 8])
        rstd = sb("rstd", [P, 8])
        nhalf = sb("nhalf", [P, 8])
        A = sb("A", [P, KC])
        gcol = sb("gcol", [P, KC])
        nmx = sb("nmx", [P, 4])
        rs = sb("rs", [P, 4])
        rt = sb("rt", [P, 12, C, E])
        posI = sb("posI", [P, C, ITEMS + 1])
        wI = sb("wI", [P, C, ITEMS + 1])
        cur = sb("cur", [P, 2, C])
        ctl = sb("ctl", [P, 8])
        ctli = sb("ctli", [P, 8], I32)
        rowsM = raw[0:DEPTH * MODS, 5, 0:P]
        rowsB = raw[0:72, 5, P:2 * P]
        onehot = raw[0:BUCKETS + 1, 5, 256:256 + DIST]
        relx = raw[0:BUCKETS + 1, 5, 640:640 + HEADS]
        distb = raw[0:HEADS, 5, 704:704 + 384]
        flip = eb[:, 0, 0:P]
        hank = qk[:, 0:HEADS * S].rearrange("p (h j) -> p h j", h=HEADS)

        bank = [ctx.enter_context(nc.psum_tensor(f"bank{i}", [P, NB], F32)) for i in range(8)]
        MODB = bank[7]

        raw_full = [sem(f"raw_full{i}") for i in range(RAW)]
        mraw_full = [sem(f"mraw_full{i}") for i in range(MRAW)]
        hi_done = sem("hi_done")
        lo_done = sem("lo_done")
        unit_used = sem("unit_used")
        mod_link = sem("mod_link")
        mod_acc = sem("mod_acc")
        mod_col = sem("mod_col")
        mod_evac = sem("mod_evac")
        small_in = sem("small_in")
        x_in = sem("x_in")
        rel_in = sem("rel_in")
        hank_in = sem("hank_in")
        dist_out = sem("dist_out")
        x_out = sem("x_out")
        const = sem("const")
        relx_set = sem("relx_set")
        cols_ps = sem("cols_ps")
        cols_sb = sem("cols_sb")
        cond_done = sem("cond_done")
        dist_ps = sem("dist_ps")
        dist_sb = sem("dist_sb")
        flip_ps = sem("flip_ps")
        bias_sb = sem("bias_sb")
        dve_link = sem("dve_link")
        pool_link = sem("pool_link")
        sq_done = sem("sq_done")
        rstd_done = sem("rstd_done")
        xn_done = sem("xn_done")
        xT_done = sem("xT_done")
        ab_done = sem("ab_done")
        h32a = sem("h32a")
        h32b = sem("h32b")
        hhi_done = sem("hhi_done")
        hlo_done = sem("hlo_done")
        blk_evac = sem("blk_evac")
        z_done = sem("z_done")
        z_abs = sem("z_abs")
        z_relu = sem("z_relu")
        sb_exp1 = sem("sb_exp1")
        sb_ln = sem("sb_ln")
        sb_sum = sem("sb_sum")
        sb_lm = sem("sb_lm")
        arg_done = sem("arg_done")
        sb_att = sem("sb_att")
        mo_max = sem("mo_max")
        mo_exp = sem("mo_exp")
        mo_p = sem("mo_p")
        bank_free = sem("bank_free")
        at_done = sem("at_done")
        pv_done = sem("pv_done")
        ohi_done = sem("ohi_done")
        olo_done = sem("olo_done")
        sig_done = sem("sig_done")
        mg_evac = sem("mg_evac")
        mT_done = sem("mT_done")
        mhi_done = sem("mhi_done")
        mlo_done = sem("mlo_done")
        gd_done = sem("gd_done")
        gps_done = sem("gps_done")
        gate_sb = sem("gate_sb")
        ysq_done = sem("ysq_done")
        ry_done = sem("ry_done")
        x_done = sem("x_done")
        silu_done = sem("silu_done")
        g_done = sem("g_done")
        gT_done = sem("gT_done")
        gh_done = sem("gh_done")
        gl_done = sem("gl_done")
        yp_done = sem("yp_done")
        yadd_done = sem("yadd_done")
        lg_done = sem("lg_done")
        rexp_in = sem("rexp_in")
        rexp = sem("rexp")
        mem_done = sem("mem_done")
        pos_done = sem("pos_done")
        ctl_done = sem("ctl_done")
        cur_done = sem("cur_done")
        gat_done = sem("gat_done")
        gath_done = sem("gath_done")
        h32e_done = sem("h32e_done")
        ehi_done = sem("ehi_done")
        elo_done = sem("elo_done")
        gatT_ps = sem("gatT_ps")
        gatT_sb = sem("gatT_sb")
        ysb_done = sem("ysb_done")
        yzero = sem("yzero")
        comb_ps = sem("comb_ps")
        comb_add = sem("comb_add")

        def dma_value(s, r):
            return 16 * (s // RAW + 1) + r * 16

        def number(s, r):
            return s + r * 6

        def wait_at_least(eng, semaphore, value):
            if not isinstance(value, int) or value > 0:
                eng.wait_ge(semaphore, value)

        def split_hi(act, s, r=0):
            act.wait_ge(raw_full[s % RAW], dma_value(s, r))
            wait_at_least(act, unit_used, number(s, r) - SPLIT + 1)
            nc.scalar.activation(whi[:, s % SPLIT, :], raw[:, s % RAW, :], ACT.Copy).then_inc(hi_done, 1)

        def split_lo(dve, s, r=0):
            dve.wait_ge(hi_done, number(s, r) + 1)
            wait_at_least(dve, unit_used, number(s, r) - SPLIT + 1)
            nc.vector.tensor_tensor(wlo[:, s % SPLIT, :], raw[:, s % RAW, :], whi[:, s % SPLIT, :].bitcast(F32),
                                    ALU.subtract).then_inc(lo_done, 1)

        def mod_chain(dve, m, slot):
            dve.wait_ge(mraw_full[slot], (m // MRAW + 1) * 16 if isinstance(m, int) else m * (16 // MRAW) + (16 - slot * (16 // MRAW)))
            nc.vector.tensor_scalar(macc[:], mraw[:, slot, 0, :], cond[:, 0:1], None, ALU.mult).then_inc(mod_link, 1)
            for k in range(1, KC):
                dve.wait_ge(mod_link, m * (KC - 1) + k)
                ins = nc.vector.scalar_tensor_tensor(macc[:], mraw[:, slot, k, :], cond[:, k:k + 1], macc[:],
                                                     ALU.mult, ALU.add)
                ins.then_inc(mod_link if k < KC - 1 else mod_acc, 1)

        def mod_take(dve, m):
            dve.wait_ge(mod_col, m + 1)
            col = modT[:, m:m + 1] if isinstance(m, int) else modT[:, bass.ds(m, 1)]
            nc.vector.tensor_copy(col, MODB[:, 0:1]).then_inc(mod_evac, 1)

        def mod_column(pe, m):
            pe.wait_ge(mod_acc, m + 1)
            nc.tensor.matmul(MODB[:, 0:1], macc[:], ones[:, 0:1], start=True, stop=True).then_inc(mod_col, 1)

        def mods_of_step(phase, u):
            if phase == 0:
                first = 16 + (2 * u if u < 4 else 4 + u)
                return list(range(first, first + (2 if u < 4 else 1)))
            return [90 + u] if u < 6 else []

        G_PRE = [0, 32, 8, 40]
        G_POST = [16, 48, 24, 56]
        C_COL = 64
        SH = [0, 24, 48, 72]
        SC = [8, 32, 56, 80]
        GT = [16, 40, 64, 88]

        block = ctx.enter_context(nc.Block())

        @block.sync
        def _(sp):
            def load_mix(l, u):
                if u < 20:
                    j, kh = divmod(u, 2)
                    return w_in[l, kh * 512:(kh + 1) * 512, j * NB:(j + 1) * NB].rearrange("(k p) n -> p k n", p=P)
                if u < 24:
                    w = w_psb if u < 22 else w_pmo
                    half = u % 2
                    return w[l, :, half * NB:(half + 1) * NB].rearrange("(k p) n -> p k n", p=P)
                half, kh = divmod(u - 24, 2)
                return w_out[l, kh * 512:(kh + 1) * 512, half * NB:(half + 1) * NB].rearrange("(k p) n -> p k n", p=P)

            def load_up(w, kh, b):
                cols = slice(b * NB, (b + 1) * NB) if isinstance(b, int) else bass.ds(b * NB, NB)
                return w.rearrange("(k p) n -> p k n", p=P)[:, kh * 4:kh * 4 + 4, cols]

            def load_down(w, part, b):
                rows = w.rearrange("(b q k p) n -> b q p k n", q=2, k=2, p=P)
                return rows[b, part]

            def load(s, r, src):
                wait_at_least(sp, lo_done, number(s, r) - RAW + 1)
                n = src.shape[-1]
                sp.dma_start(raw[:, s % RAW, :].rearrange("p (k n) -> p k n", n=n), src)\
                    .then_inc(raw_full[s % RAW], 16)

            def load_mod(m, slot, l, col):
                wait_at_least(sp, mod_acc, m - MRAW + 1)
                cols = slice(col * P, col * P + P) if isinstance(col, int) else bass.ds(col * P, P)
                sp.dma_start(mraw[:, slot, :, :], w_mod[l].rearrange("(k p) n -> p k n", p=P)[:, :, cols])\
                    .then_inc(mraw_full[slot], 16)

            def ffn_unit(ws, b, j):
                if j < 4:
                    return load_up(ws[j // 2], j % 2, b)
                return load_down(ws[2], j - 4, b - 1)

            sp.dma_start(rowsM, b_mod.rearrange("l (m p) -> (l m) p", p=P)).then_inc(small_in, 16)
            for i, g in enumerate([g_mix_pre, g_mix_post, g_ffn_pre, g_ffn_post]):
                sp.dma_start(raw[16 * i:16 * i + 16, 5, P:2 * P], g.rearrange("l (m p) -> (l m) p", p=P))\
                    .then_inc(small_in, 16)
            sp.dma_start(raw[64:72, 5, P:2 * P], c_d.rearrange("b (m p) -> (b m) p", p=P)).then_inc(small_in, 16)
            sp.dma_start(x[:], x_d.rearrange("b (c p) n -> p (b c) n", p=P)).then_inc(x_in, 16)
            sp.dma_start(onehot, onehot_d).then_inc(rel_in, 16)
            sp.wait_ge(relx_set, 1)
            sp.dma_start(relx[0:BUCKETS, :], rel_bias).then_inc(rel_in, 16)
            sp.dma_start(wr[:], w_router[0].rearrange("(k p) e -> p k e", p=P)).then_inc(small_in, 16)
            for m in range(16):
                load_mod(m, m % MRAW, 0, m)
                if m == 3:
                    sp.wait_ge(dist_sb, 1)
                    sp.dma_start(dist_scratch[:, 0:DIST], distb[:, 0:DIST]).then_inc(dist_out, 16)
                    sp.wait_ge(dist_out, 16)
                    sp.dma_start(hank, bass.AP(dist_scratch.tensor, 0, [[1, P], [384, HEADS], [1, S]]))\
                        .then_inc(hank_in, 16)

            def phase_unit(n):
                if n < FFN0:
                    return load_mix(0, n)
                if n < MIX1:
                    u = n - FFN0
                    return ffn_unit(dense, 0, u) if u < 4 else ffn_unit(dense, FBLK, u - FFN_UNITS + 6)
                return load_mix(1, n - MIX1)

            dense = (w1_d[0], w3_d[0], w2_d[0])

            for s in range(LEAD):
                load(s, 0, phase_unit(s))
            for u in range(MIX_UNITS):
                load(u + LEAD, 0, phase_unit(u + LEAD))
                for m in mods_of_step(0, u):
                    load_mod(m, m % MRAW, 0, m)
            for j in range(4):
                s = FFN0 + j + LEAD
                load(s, 0, ffn_unit(dense, 0, j + LEAD) if j + LEAD < 4 else ffn_unit(dense, 1, j + LEAD - 4))
                load_mod(MODS + j, j % MRAW, 1, j)
            with sp.Fori(0, FBLK - 2) as t:
                for j in range(6):
                    jj = j + LEAD
                    src = ffn_unit(dense, t + 1, jj) if jj < 6 else ffn_unit(dense, t + 2, jj - 6)
                    load(FFN0 + 4 + jj, t, src)
                    load_mod(t * 6 + (MODS + 4 + j), j % MRAW, 1, t * 6 + (4 + j))
            for j in range(6):
                jj = j + LEAD
                src = ffn_unit(dense, FBLK - 1, jj) if jj < 6 else ffn_unit(dense, FBLK, jj - 2)
                load(FFN0 + 4 + jj + 6 * (FBLK - 2), 0, src)
                m = MODS + 4 + 6 * (FBLK - 2) + j
                load_mod(m, m % MRAW, 1, m - MODS)
            for j in range(2):
                load(MIX1 + j, 0, load_mix(1, j))
                m = MODS + 4 + 6 * (FBLK - 1) + j
                load_mod(m, m % MRAW, 1, m - MODS)
            for u in range(MIX_UNITS - LEAD):
                load(MIX1 + u + LEAD, 0, load_mix(1, u + LEAD))
                for m in mods_of_step(1, u):
                    load_mod(m, m % MRAW, 1, m - MODS)

            def load_expert(e, item):
                ws = (w1_m[0, e], w3_m[0, e], w2_m[0, e])
                for j in range(4):
                    load(MOE0 + j, item * FBLK, ffn_unit(ws, 0, j))
                with sp.Fori(0, FBLK - 1) as t:
                    for j in range(6):
                        load(MOE0 + 4 + j, item * FBLK + t, ffn_unit(ws, t + 1, j))
                for j in range(2):
                    load(MOE0 + FFN_UNITS - 2 + j, item * FBLK, load_down(ws[2], j, FBLK - 1))

            with sp.Fori(0, E) as e:
                load_expert(e, e)
            sp.wait_ge(ctl_done, 1)
            over = sp.value_load(ctli[0:1, 1:2], min_val=0, max_val=EXTRA)
            with sp.If(over > 0):
                with sp.Fori(0, over) as i:
                    e = sp.value_load(ctli[0:1, bass.ds(i + 2, 1)], min_val=0, max_val=E - 1)
                    load_expert(e, i + E)
            items = sp.value_load(ctli[0:1, 0:1], min_val=E, max_val=ITEMS)
            for j in range(LEAD):
                load(MOE0 + j, items * FBLK, load_mix(0, j))
            for j in range(LEAD):
                sp.wait_ge(raw_full[(MOE0 + j) % RAW], dma_value(MOE0 + j, items * FBLK))
            sp.wait_ge(x_done, 4 * 4)
            sp.dma_start(out_d.rearrange("b (c p) n -> p (b c) n", p=P), x[:]).then_inc(x_out, 16)
            sp.wait_ge(x_out, 16)

        @block.scalar
        def _(act):
            def norm(q):
                for c in range(C):
                    if q:
                        act.wait_ge(x_done, 4 * (q - 1) + 2 * c + 2)
                        act.wait_ge(rstd_done, C * q)
                        act.wait_ge(xT_done, 4 * q)
                        act.wait_ge(ysq_done, squares[0])
                    elif c == 0:
                        act.wait_ge(x_in, 16)
                    scr = h32[:].rearrange("p k t -> p (k t)")[:, c * D:(c + 1) * D]
                    nc.scalar.activation(scr, x[:, c, :], ACT.Square, accum_out=ss[:, c:c + 1]).then_inc(sq_done, 1)
                act.wait_ge(xT_done, 4 * q + 2)
                act.wait_ge(ab_done, q + 1)
                act.wait_ge(sq_done, C * (q + 1))
                for k in range(KC):
                    src = bank[k // 4][:, (k % 4) * P:(k % 4 + 1) * P]
                    nc.scalar.activation(h32[:, k, 0:P], src, ACT.Identity, scale=A[:, k:k + 1],
                                         bias=modT[:, SH[q] + k:SH[q] + k + 1]).then_inc(h32a, 1)
                if q < 3:
                    act.wait_ge(h32a, KC * (q + 1))
                    nc.scalar.activation(hhi[:, :, 0:P], h32[:, :, 0:P], ACT.Copy).then_inc(hhi_done, 1)
                    act.wait_ge(h32b, KC * (q + 1))
                    nc.scalar.activation(hhi[:, :, P:S], h32[:, :, P:S], ACT.Copy).then_inc(hhi_done, 1)

            def mixer(l):
                base = MIX1 if l else MIX0

                def block_out(j):
                    act.wait_ge(unit_used, base + 2 * j + 2)
                    for i in range(2):
                        src = bank[2 * (j % 2) + i]
                        if j in (0, 1, 3, 4):
                            b = [0, 1, None, 2, 3][j]
                            nc.scalar.activation(qkT[:, b, 2 * i:2 * i + 2, :].rearrange("p c t -> p (c t)"), src[:],
                                                 ACT.Copy, scale=DH ** -0.5 if b % 2 == 0 else 1.0)\
                                .then_inc(blk_evac, 1)
                        elif j in (2, 5):
                            nc.scalar.activation(vals[:, j // 4, i, :], src[:], ACT.Copy).then_inc(blk_evac, 1)
                        else:
                            nc.scalar.activation(gates[:, i, (j - 6) * NB:(j - 5) * NB], src[:], ACT.Copy)\
                                .then_inc(blk_evac, 1)

                def after_scores(p):
                    for s in range(2):
                        n = 16 * l + 2 * p + s
                        if p < 4:
                            nsb = 8 * l + 2 * p + s
                            act.wait_ge(z_abs, nsb + 1)
                            nc.scalar.activation(eb[:, s, :], eb[:, s, :], ACT.Exp).then_inc(sb_exp1, 1)
                            act.wait_ge(sb_exp1, nsb + 1)
                            nc.scalar.activation(eb[:, s, :], eb[:, s, :], ACT.Ln, bias=1.0).then_inc(sb_ln, 1)
                        else:
                            nmo = 8 * l + 2 * (p - 4) + s
                            act.wait_ge(mo_max, 2 * (nmo + 1))
                            nc.scalar.activation(eb[:, s, 0:S], eb[:, s, 0:S], ACT.Exp, bias=nmx[:, 2 * s:2 * s + 1],
                                                 accum_out=rs[:, 2 * s:2 * s + 1]).then_inc(mo_exp, 1)
                            nc.scalar.activation(eb[:, s, S:384], eb[:, s, S:384], ACT.Exp,
                                                 bias=nmx[:, 2 * s + 1:2 * s + 2],
                                                 accum_out=rs[:, 2 * s + 1:2 * s + 2]).then_inc(mo_exp, 1)

                def after_arg(p):
                    for s in range(2):
                        n = 16 * l + 2 * p + s
                        act.wait_ge(arg_done, n + 1)
                        if p < 4:
                            nc.scalar.activation(at[:, s, :], bank[4 + s][:, 0:384], ACT.Exp).then_inc(sb_att, 1)
                        else:
                            nc.scalar.activation(at[:, s, :], bank[4 + s][:, 0:384], ACT.Copy).then_inc(at_done, 1)

                def after_pv(p):
                    act.wait_ge(pv_done, 8 * l + p + 1)
                    nc.scalar.activation(ohi[:, p, :], bank[6][:, 0:S], ACT.Copy).then_inc(ohi_done, 1)

                for u in range(MIX_UNITS):
                    split_hi(act, base + u + LEAD)
                    if u < 20 and u % 2 == 1:
                        block_out(u // 2)
                    if 7 <= u < 23 and (u - 7) % 2 == 0:
                        after_pv((u - 7) // 2)
                    if 5 <= u < 21 and (u - 5) % 2 == 0:
                        after_scores((u - 5) // 2)
                    if 6 <= u < 22 and (u - 6) % 2 == 0:
                        after_arg((u - 6) // 2)
                    if u == 19:
                        act.wait_ge(blk_evac, 2 * BLK * (l + 1))
                        for c in range(C):
                            nc.scalar.activation(gates[:, c, :], gates[:, c, :], ACT.Sigmoid).then_inc(sig_done, 1)
                    if u == 23:
                        for i in range(4):
                            half, c = divmod(i, 2)
                            act.wait_ge(mT_done, 4 * l + i + 1)
                            nc.scalar.activation(hhi[:, 4 * half:4 * half + 4, c * P:(c + 1) * P],
                                                 bank[[2, 3, 6, 4][i]][:].rearrange("p (k t) -> p k t", k=4),
                                                 ACT.Copy).then_inc(mhi_done, 1)

            def out_squares(q):
                for c in range(C):
                    act.wait_ge(rstd_done, C * (q + 1))
                    if q % 2 == 0:
                        for half in range(2):
                            act.wait_ge(unit_used, (MIX1 if q else MIX0) + 26 + 2 * half)
                            scr = eb[:].rearrange("p a n -> p (a n)")[:, 0:NB]
                            act.wait_ge(at_done, 16 * (q // 2 + 1))
                            if c or half:
                                act.wait_ge(ysq_done, squares[0])
                            squares[0] += 1
                            nc.scalar.activation(scr, bank[2 * half + c][:], ACT.Square,
                                                 accum_out=ss[:, 2 * c + half:2 * c + half + 1]).then_inc(ysq_done, 1)
                    else:
                        if q == 1:
                            act.wait_ge(yadd_done, 4 * FBLK + 1)
                        else:
                            act.wait_ge(comb_add, items4[0])
                        if c:
                            act.wait_ge(ysq_done, squares[0])
                        squares[0] += 1
                        nc.scalar.activation(h32[:].rearrange("p k t -> p (k t)")[:, 0:D] if q == 1 else hid[:].rearrange("p c n -> p (c n)"),
                                             yacc[:, c, :], ACT.Square, accum_out=ss[:, c:c + 1]).then_inc(ysq_done, 1)

            squares = [0]
            items4 = [0]

            def ffn_silu(n, t, units):
                for c in range(n):
                    act.wait_ge(unit_used, units)
                    wait_at_least(act, g_done, t * n + base_of[n])
                    nc.scalar.activation(silu[:, c, :], bank[c][:], ACT.Silu).then_inc(silu_done, 1)

            def ffn_ghi(n, t, c):
                act.wait_ge(gT_done, t * n + (base_of[n] + c + 1))
                nc.scalar.activation(ohi[:, 0:4, c * P:(c + 1) * P], bank[6][:].rearrange("p (k t) -> p k t", k=4),
                                     ACT.Copy).then_inc(gh_done, 1)

            base_of = {2: FFN_BASE[0], 1: FFN_BASE[1]}

            act.wait_ge(cols_sb, 2)
            nc.scalar.activation(cond[:], colsB[:, C_COL:C_COL + KC], ACT.Silu).then_inc(cond_done, 1)
            norm(0)
            for s in range(LEAD):
                split_hi(act, s)
            mixer(0)
            out_squares(0)
            norm(1)
            for j in range(4):
                split_hi(act, FFN0 + j + LEAD)
                if j == 1:
                    ffn_silu(2, 0, FFN0 + 2)

            def block_steps(n, s0, r, t):
                for j in range(6):
                    split_hi(act, s0 + j + LEAD, r)
                    if j == 1:
                        ffn_silu(n, t, number(s0, r) + 2)
                        ffn_ghi(n, t - 1, 0)
                    if j == 2 and n == 2:
                        ffn_ghi(n, t - 1, 1)

            with act.Fori(0, FBLK - 1) as t:
                block_steps(2, FFN0 + 4, t, t + 1)
            for c in range(C):
                ffn_ghi(2, FBLK - 1, c)
            for j in range(2):
                split_hi(act, MIX1 + j)
            out_squares(1)
            norm(2)
            mixer(1)
            out_squares(2)
            norm(3)
            act.wait_ge(rexp_in, 1)
            nc.scalar.activation(rt[:, 9, :, 0], rt[:, 8, :, 0], ACT.Exp).then_inc(rexp, 1)

            def expert_h(item):
                act.wait_ge(gath_done, item * 2 + 2)
                wait_at_least(act, elo_done, item)
                for k in range(KC):
                    src = bank[2 + k // 4][:, (k % 4) * P:(k % 4 + 1) * P]
                    nc.scalar.activation(h32e[:, k, :], src, ACT.Identity, scale=A[:, k:k + 1],
                                         bias=modT[:, SH[3] + k:SH[3] + k + 1]).then_inc(h32e_done, 1)
                act.wait_ge(h32e_done, item * KC + KC)
                nc.scalar.activation(hhi[:, :, 0:P], h32e[:], ACT.Copy).then_inc(ehi_done, 1)

            act.wait_ge(lg_done, 1)
            expert_h(0)
            act.wait_ge(ctl_done, 1)
            items = act.value_load(ctli[0:1, 0:1], min_val=E, max_val=ITEMS)
            with act.Fori(0, items) as i:
                for j in range(4):
                    split_hi(act, MOE0 + j + LEAD, i * FBLK)
                    if j == 1:
                        ffn_silu(1, i * FBLK, i * FFN_UNITS + (MOE0 + 2))
                with act.Fori(0, FBLK - 1) as t:
                    block_steps(1, MOE0 + 4, i * FBLK + t, i * FBLK + t + 1)
                ffn_ghi(1, i * FBLK + (FBLK - 1), 0)
                expert_h(i + 1)
                for j in range(2):
                    split_hi(act, MOE0 + FFN_UNITS + j, i * FBLK)
                act.wait_ge(unit_used, i * FFN_UNITS + (MOE0 + FFN_UNITS))
                act.wait_ge(comb_ps, i * 4 + 1)
                for half in range(2):
                    nc.scalar.activation(ysb[:, half * NB:(half + 1) * NB], bank[4 + half][:], ACT.Copy)\
                        .then_inc(ysb_done, 1)
            items4[0] = items * 4 + 1
            out_squares(3)

        @block.vector
        def _(dve):
            links = [0]

            def link(ins):
                links[0] += 1
                ins.then_inc(dve_link, 1)
                dve.wait_ge(dve_link, links[0])

            def norm(q):
                link(nc.vector.tensor_tensor(modT[:, SH[q]:SH[q] + 16], modT[:, SH[q]:SH[q] + 16],
                                             colsM[:, SH[q]:SH[q] + 16], ALU.add))
                nc.vector.scalar_tensor_tensor(A[:], modT[:, SC[q]:SC[q] + KC], 1.0,
                                               colsB[:, G_PRE[q]:G_PRE[q] + KC], ALU.add, ALU.mult)\
                    .then_inc(ab_done, 1)
                for c in range(C):
                    dve.wait_ge(rstd_done, C * q + c + 1)
                    nc.vector.tensor_scalar(xn[:, c, :], x[:, c, :], rstd[:, c:c + 1], None, ALU.mult)\
                        .then_inc(xn_done, 1)
                dve.wait_ge(xT_done, 4 * q + 4)
                dve.wait_ge(sq_done, C * (q + 1))
                dve.wait_ge(ab_done, q + 1)
                for k in range(KC):
                    src = bank[2 + k // 4][:, (k % 4) * P:(k % 4 + 1) * P]
                    nc.vector.tensor_scalar(h32[:, k, P:S], src, A[:, k:k + 1], modT[:, SH[q] + k:SH[q] + k + 1],
                                            ALU.mult, ALU.add).then_inc(h32b, 1)
                if q < 3:
                    for c in range(C):
                        dve.wait_ge(hhi_done, C * q + c + 1)
                        if c:
                            dve.wait_ge(h32b, KC * (q + 1))
                        nc.vector.tensor_tensor(hlo[:, :, c * P:(c + 1) * P], h32[:, :, c * P:(c + 1) * P],
                                                hhi[:, :, c * P:(c + 1) * P].bitcast(F32), ALU.subtract)\
                            .then_inc(hlo_done, 1)

            def gate_diag(q):
                link(nc.vector.tensor_tensor(gcol[:], modT[:, GT[q]:GT[q] + KC], colsM[:, GT[q]:GT[q] + KC], ALU.add))
                link(nc.vector.tensor_tensor(gcol[:], gcol[:], colsB[:, G_POST[q]:G_POST[q] + KC], ALU.mult))
                for k in range(KC):
                    nc.vector.tensor_scalar(gdiag[:, k * P:(k + 1) * P], ident[:], gcol[:, k:k + 1], None, ALU.mult)\
                        .then_inc(gd_done, 1)

            def gate_take(q):
                for half in range(2):
                    dve.wait_ge(gps_done, 2 * q + half + 1)
                    nc.vector.tensor_copy(gate[:, half * NB:(half + 1) * NB], bank[4 + half][:]).then_inc(gate_sb, 1)

            def residual(q):
                dve.wait_ge(gate_sb, 2 * (q + 1))
                for c in range(C):
                    dve.wait_ge(ry_done, C * q + c + 1)
                    tmp = [None] * 2
                    for half in range(2):
                        cols = slice(half * NB, (half + 1) * NB)
                        src = bank[2 * half + c][:] if q % 2 == 0 else yacc[:, c, cols]
                        if c == 0 and half == 0 and q % 2 == 0:
                            dve.wait_ge(ysq_done, [4, 0, 10][q])
                        if q == 3 and c == 0 and half == 0:
                            dve.wait_ge(ysq_done, 12)
                        links[0] += 1
                        nc.vector.scalar_tensor_tensor(mtmp[:, half, :], src, rstd[:, 4 + c:5 + c], gate[:, cols],
                                                       ALU.mult, ALU.mult).then_inc(dve_link, 1)
                        tmp[half] = links[0]
                    for half in range(2):
                        cols = slice(half * NB, (half + 1) * NB)
                        dve.wait_ge(dve_link, tmp[half])
                        nc.vector.tensor_tensor(x[:, c, cols], x[:, c, cols], mtmp[:, half, :], ALU.add)\
                            .then_inc(x_done, 1)
                    dve.wait_ge(x_done, 4 * q + 2 * c + 2)

            taken = set()

            def take_once(m):
                if m >= 0 and m not in taken:
                    taken.add(m)
                    mod_take(dve, m)

            def mods(phase, u):
                for m in mods_of_step(phase, u):
                    take_once(m - 1)
                    dve.wait_ge(mod_evac, m)
                    mod_chain(dve, m, m % MRAW)

            def mixer(l):
                base = MIX1 if l else MIX0
                q = 2 * l

                def after_scores(p):
                    for s in range(2):
                        n = 16 * l + 2 * p + s
                        z = bank[4 + s]
                        dve.wait_ge(z_done, n + 1)
                        if p < 4:
                            nc.vector.tensor_scalar(at[:, s, :], z[:, 0:384], 0.0, None, ALU.max).then_inc(z_relu, 1)
                            dve.wait_ge(z_relu, 8 * l + 2 * p + s + 1)
                            nc.vector.scalar_tensor_tensor(eb[:, s, :], at[:, s, :], -2.0, z[:, 0:384], ALU.mult,
                                                           ALU.add).then_inc(z_abs, 1)
                        else:
                            h = 2 * (p - 4) + s
                            links[0] += 2
                            nc.vector.tensor_tensor(eb[:, s, 0:S], z[:, 0:S], bias[:, h, :], ALU.add)\
                                .then_inc(dve_link, 1)
                            nc.vector.tensor_tensor(eb[:, s, S:384], z[:, S:384], bias[:, h, P:S], ALU.add)\
                                .then_inc(dve_link, 1)
                            dve.wait_ge(dve_link, links[0])
                            nc.vector.tensor_reduce(nmx[:, 2 * s:2 * s + 1], eb[:, s, 0:S], AX, ALU.max, negate=True)\
                                .then_inc(mo_max, 1)
                            nc.vector.tensor_reduce(nmx[:, 2 * s + 1:2 * s + 2], eb[:, s, S:384], AX, ALU.max,
                                                    negate=True).then_inc(mo_max, 1)
                    for s in range(2):
                        if p < 4:
                            nsb = 8 * l + 2 * p + s
                            dve.wait_ge(sb_ln, nsb + 1)
                            dve.wait_ge(z_relu, nsb + 1)
                            nc.vector.scalar_tensor_tensor(at[:, s, :], eb[:, s, :], -1.0, at[:, s, :], ALU.mult,
                                                           ALU.subtract).then_inc(sb_sum, 1)
                        else:
                            nmo = 8 * l + 2 * (p - 4) + s
                            dve.wait_ge(mo_exp, 2 * (nmo + 1))
                            link(nc.vector.reciprocal(rs[:, 2 * s:2 * s + 2], rs[:, 2 * s:2 * s + 2]))
                            nc.vector.tensor_scalar(eb[:, s, 0:S], eb[:, s, 0:S], rs[:, 2 * s:2 * s + 1], None,
                                                    ALU.mult).then_inc(mo_p, 1)
                            nc.vector.tensor_scalar(eb[:, s, S:384], eb[:, s, S:384], rs[:, 2 * s + 1:2 * s + 2],
                                                    None, ALU.mult).then_inc(mo_p, 1)

                def after_pv(p):
                    dve.wait_ge(ohi_done, 8 * l + p + 1)
                    nc.vector.tensor_tensor(olo[:, p, :], bank[6][:, 0:S], ohi[:, p, :].bitcast(F32), ALU.subtract)\
                        .then_inc(olo_done, 1)

                for u in range(MIX_UNITS):
                    split_lo(dve, base + u + LEAD)
                    if 7 <= u < 23 and (u - 7) % 2 == 0:
                        after_pv((u - 7) // 2)
                    if 5 <= u < 21 and (u - 5) % 2 == 0:
                        after_scores((u - 5) // 2)
                    mods(l, u)
                    if u == 7 and l == 1:
                        take_once(95)
                    if 20 <= u < 22:
                        half = u - 20
                        dve.wait_ge(sig_done, C * (l + 1))
                        for c in range(C):
                            dve.wait_ge(unit_used, base + u + 1)
                            nc.vector.tensor_tensor(merged[:, c, half * NB:(half + 1) * NB], bank[2 * half + c][:],
                                                    gates[:, c, half * NB:(half + 1) * NB], ALU.mult)\
                                .then_inc(mg_evac, 1)
                    if 22 <= u < 24:
                        half = u - 22
                        for c in range(C):
                            dve.wait_ge(unit_used, base + u + 1)
                            link(nc.vector.tensor_tensor(mtmp[:, c, :], bank[(4 if half == 0 else 0) + c][:],
                                                         gates[:, c, D + half * NB:D + (half + 1) * NB], ALU.mult))
                            dve.wait_ge(mg_evac, 8 * l + 2 * half + c + 1)
                            cols = slice(half * NB, (half + 1) * NB)
                            nc.vector.tensor_tensor(merged[:, c, cols], merged[:, c, cols], mtmp[:, c, :], ALU.add)\
                                .then_inc(mg_evac, 1)
                    if u == 23:
                        for i in range(4):
                            half, c = divmod(i, 2)
                            dve.wait_ge(mhi_done, 4 * l + i + 1)
                            nc.vector.tensor_tensor(hlo[:, 4 * half:4 * half + 4, c * P:(c + 1) * P],
                                                    bank[[2, 3, 6, 4][i]][:].rearrange("p (k t) -> p k t", k=4),
                                                    hhi[:, 4 * half:4 * half + 4, c * P:(c + 1) * P].bitcast(F32),
                                                    ALU.subtract).then_inc(mlo_done, 1)
                        gate_diag(q)
                    if u == 25:
                        gate_take(q)

            def ffn_g(n, t, units):
                for c in range(n):
                    dve.wait_ge(unit_used, units)
                    dve.wait_ge(silu_done, t * n + (base_of[n] + c + 1))
                    wait_at_least(dve, gT_done, t * n + base_of[n])
                    nc.vector.tensor_tensor(hid[:, c, :], silu[:, c, :], bank[(2 if n == 2 else 1) + c][:], ALU.mult)\
                        .then_inc(g_done, 1)

            def ffn_glo(n, t, c):
                dve.wait_ge(gh_done, t * n + (base_of[n] + c + 1))
                nc.vector.tensor_tensor(olo[:, 0:4, c * P:(c + 1) * P], bank[6][:].rearrange("p (k t) -> p k t", k=4),
                                        ohi[:, 0:4, c * P:(c + 1) * P].bitcast(F32), ALU.subtract)\
                    .then_inc(gl_done, 1)

            def dense_add(t, c, units):
                if True:
                    for half in range(2):
                        k = 2 * c + half
                        if k < 3:
                            dve.wait_ge(yp_done, t * 3 + (k + 1))
                        else:
                            dve.wait_ge(unit_used, units)
                        dve.wait_ge(yadd_done, t * 4 + 1)
                        cols = slice(half * NB, (half + 1) * NB)
                        nc.vector.tensor_tensor(yacc[:, c, cols], yacc[:, c, cols], bank[4 + half][:], ALU.add)\
                            .then_inc(yadd_done, 1)

            base_of = {2: FFN_BASE[0], 1: FFN_BASE[1]}

            nc.vector.memset(ones[:], 1.0).then_inc(const, 1)
            nc.vector.memset(posI[:], -1.0).then_inc(const, 1)
            nc.vector.memset(wI[:], 0.0).then_inc(const, 1)
            dve.wait_ge(cols_ps, 2)
            nc.vector.tensor_copy(colsM[:], bank[6][:, 0:DEPTH * MODS]).then_inc(cols_sb, 1)
            nc.vector.tensor_copy(colsB[:], bank[6][:, P:P + 72]).then_inc(cols_sb, 1)
            dve.wait_ge(dist_ps, 1)
            nc.vector.tensor_copy(distb[:, 0:DIST], bank[5][0:HEADS, 0:DIST]).then_inc(dist_sb, 1)
            dve.wait_ge(cond_done, 1)
            for m in range(16):
                take_once(m - 1)
                if m:
                    dve.wait_ge(mod_evac, m)
                mod_chain(dve, m, m % MRAW)
                if m == 8:
                    for i in range(4):
                        dve.wait_ge(flip_ps, i + 1)
                        nc.vector.tensor_copy(bias[:, 2 * i:2 * i + 2, :].rearrange("p h j -> p (h j)"), bank[i][:])\
                            .then_inc(bias_sb, 1)
            take_once(15)
            dve.wait_ge(mod_evac, 16)
            norm(0)
            for s in range(LEAD):
                split_lo(dve, s)
            mixer(0)
            residual(0)
            take_once(47)
            dve.wait_ge(mod_evac, 48)
            norm(1)
            gate_diag(1)
            nc.vector.memset(yacc[:], 0.0).then_inc(yadd_done, 1)
            for j in range(4):
                split_lo(dve, FFN0 + j + LEAD)
                if j:
                    mod_take(dve, MODS + j - 1)
                dve.wait_ge(mod_evac, MODS + j)
                mod_chain(dve, MODS + j, j % MRAW)
                if j == 3:
                    gate_take(1)
                    ffn_g(2, 0, FFN0 + 4)
            with dve.Fori(0, FBLK - 1) as t:
                for j in range(6):
                    split_lo(dve, FFN0 + 4 + j + LEAD, t)
                    if j == 1:
                        ffn_glo(2, t, 0)
                    if j == 2:
                        ffn_glo(2, t, 1)
                    m = t * 6 + (MODS + 4 + j)
                    mod_take(dve, m - 1)
                    dve.wait_ge(mod_evac, m)
                    mod_chain(dve, m, j % MRAW)
                    if j == 3:
                        ffn_g(2, t + 1, t * 6 + (FFN0 + 8))
                    if j == 4:
                        dense_add(t, 0, None)
                dense_add(t, 1, t * 6 + (FFN0 + 10))
            for c in range(C):
                ffn_glo(2, FBLK - 1, c)
            for j in range(2):
                split_lo(dve, MIX1 + j)
                m = MODS + 4 + 6 * (FBLK - 1) + j
                mod_take(dve, m - 1)
                dve.wait_ge(mod_evac, m)
                mod_chain(dve, m, m % MRAW)
                dense_add(FBLK - 1, j, MIX1)
            taken.update(range(MODS, MODS + 41))
            take_once(89)
            dve.wait_ge(mod_evac, 90)
            residual(1)
            norm(2)
            mixer(1)
            residual(2)
            norm(3)
            gate_diag(3)

            lg, cand, oh1, oh2, t5, pos, comb, mem = (rt[:, i, :, :] for i in range(8))
            m1, m2, i1, w1, w2 = (rt[:, 10, :, i:i + 1] for i in range(5))
            dlt = rt[:, 8, :, 0:1]
            ex = rt[:, 9, :, 0:1]
            cnt = rt[:, 11, 0, :]
            pre = rt[:, 11, 1, :]

            def wide8(v):
                return v.broadcast_to([P, C, E])

            iota8 = iota[:, 0:E].rearrange("p (a e) -> p a e", a=1).broadcast_to([P, C, E])

            def first_of_largest(values, top, onehot_out):
                link(nc.vector.tensor_reduce(top, values, AX, ALU.max))
                link(nc.vector.tensor_tensor(cand, values, wide8(top), ALU.is_lt))
                link(nc.vector.tensor_scalar(cand, cand, 100.0, None, ALU.mult))
                link(nc.vector.tensor_tensor(cand, cand, iota8, ALU.add))
                link(nc.vector.tensor_reduce(i1, cand, AX, ALU.min))
                link(nc.vector.tensor_tensor(onehot_out, iota8, wide8(i1), ALU.is_equal))

            dve.wait_ge(lg_done, 1)
            link(nc.vector.tensor_copy(lg, bank[4][:, 0:C * E].rearrange("p (c e) -> p c e", c=C)))
            first_of_largest(lg, m1, oh1)
            link(nc.vector.tensor_scalar(t5, oh1, NEG, None, ALU.mult))
            link(nc.vector.tensor_tensor(t5, t5, lg, ALU.add))
            first_of_largest(t5, m2, oh2)
            nc.vector.tensor_tensor(dlt, m2, m1, ALU.subtract).then_inc(rexp_in, 1)
            nc.vector.tensor_tensor(mem, oh1, oh2, ALU.add).then_inc(mem_done, 1)
            dve.wait_ge(rexp, 1)
            link(nc.vector.tensor_scalar(w1, ex, 1.0, None, ALU.add))
            link(nc.vector.reciprocal(w1, w1))
            link(nc.vector.tensor_tensor(w2, ex, w1, ALU.mult))
            link(nc.vector.tensor_tensor(comb, oh1, wide8(w1), ALU.mult))
            link(nc.vector.tensor_tensor(t5, oh2, wide8(w2), ALU.mult))
            link(nc.vector.tensor_tensor(comb, comb, t5, ALU.add))
            link(nc.vector.tensor_copy(wI[:, :, 0:E], comb))
            dve.wait_ge(pos_done, 1)
            link(nc.vector.tensor_scalar(pos, bank[5][:, 0:C * E].rearrange("p (c e) -> p c e", c=C), 1.0, None, ALU.add))
            link(nc.vector.tensor_tensor(pos, pos, mem, ALU.mult))
            link(nc.vector.tensor_scalar(pos, pos, -1.0, None, ALU.add))
            link(nc.vector.tensor_copy(posI[:, :, 0:E], pos))
            link(nc.vector.tensor_scalar(cnt, bank[5][:, C * E:C * E + E], float(P), None, ALU.is_gt))
            link(nc.vector.memset(pre[:, 0:1], 0.0))
            for e in range(1, E):
                link(nc.vector.tensor_tensor(pre[:, e:e + 1], pre[:, e - 1:e], cnt[:, e - 1:e], ALU.add))
            link(nc.vector.tensor_reduce(ctl[:, 1:2], cnt, AX, ALU.add))
            link(nc.vector.tensor_scalar(ctl[:, 0:1], ctl[:, 1:2], float(E), None, ALU.add))
            for i in range(EXTRA):
                sel = rt[:, 8, 0, :]
                link(nc.vector.tensor_scalar(sel, pre, float(i), None, ALU.is_equal))
                link(nc.vector.tensor_tensor(sel, sel, cnt, ALU.mult))
                for c in range(C):
                    link(nc.vector.tensor_tensor(cand[:, c, :], pos[:, c, :], sel, ALU.mult))
                    link(nc.vector.tensor_tensor(t5[:, c, :], comb[:, c, :], sel, ALU.mult))
                link(nc.vector.tensor_reduce(posI[:, :, E + i:E + i + 1], cand, AX, ALU.add))
                link(nc.vector.tensor_scalar(posI[:, :, E + i], posI[:, :, E + i], -float(P), None, ALU.add))
                link(nc.vector.tensor_reduce(wI[:, :, E + i:E + i + 1], t5, AX, ALU.add))
                link(nc.vector.tensor_tensor(sel, sel, iota[:, 0:E], ALU.mult))
                link(nc.vector.tensor_reduce(ctl[:, 2 + i:3 + i], sel, AX, ALU.add))
            nc.vector.tensor_copy(ctli[:, 0:5], ctl[:, 0:5]).then_inc(ctl_done, 1)

            def expert_slots(item):
                col = slice(item, item + 1) if isinstance(item, int) else bass.ds(item, 1)
                nc.vector.tensor_copy(cur[:, 0, :], posI[:, :, col].rearrange("p c o -> p (c o)")).then_inc(cur_done, 1)
                dve.wait_ge(cur_done, 1 if isinstance(item, int) else item * 2)
                for c in range(C):
                    nc.vector.tensor_scalar(gat[:, c, :], iota[:], cur[:, 0, c:c + 1], None, ALU.is_equal)\
                        .then_inc(gat_done, 1)

            def expert_lo(item):
                dve.wait_ge(ehi_done, item + 1)
                nc.vector.tensor_tensor(hlo[:, :, 0:P], h32e[:], hhi[:, :, 0:P].bitcast(F32), ALU.subtract)\
                    .then_inc(elo_done, 1)

            dve.wait_ge(lg_done, 1)
            expert_slots(0)
            gate_take(3)
            nc.vector.memset(yacc[:], 0.0).then_inc(comb_add, 1)
            expert_lo(0)
            dve.wait_ge(gatT_ps, 1)
            nc.vector.tensor_copy(gatT, bank[7][:, 0:S]).then_inc(gatT_sb, 1)
            dve.wait_ge(ctl_done, 1)
            items = dve.value_load(ctli[0:1, 0:1], min_val=E, max_val=ITEMS)
            with dve.Fori(0, items) as i:
                dve.wait_ge(gate_sb, 8)
                for half in range(2):
                    nc.vector.memset(bank[4 + half][:], 0.0).then_inc(yzero, 1)
                for j in range(4):
                    split_lo(dve, MOE0 + j + LEAD, i * FBLK)
                    if j == 3:
                        ffn_g(1, i * FBLK, i * FFN_UNITS + (MOE0 + 4))
                with dve.Fori(0, FBLK - 1) as t:
                    for j in range(6):
                        split_lo(dve, MOE0 + 4 + j + LEAD, i * FBLK + t)
                        if j == 1:
                            ffn_glo(1, i * FBLK + t, 0)
                        if j == 3:
                            ffn_g(1, i * FBLK + t + 1, i * FFN_UNITS + t * 6 + (MOE0 + 8))
                dve.wait_ge(gatT_ps, i + 1)
                expert_slots(i + 1)
                ffn_glo(1, i * FBLK + (FBLK - 1), 0)
                expert_lo(i + 1)
                for j in range(2):
                    split_lo(dve, MOE0 + FFN_UNITS + j, i * FBLK)
                nc.vector.tensor_copy(cur[:, 1, :], wI[:, :, bass.ds(i, 1)].rearrange("p c o -> p (c o)"))\
                    .then_inc(cur_done, 1)
                dve.wait_ge(cur_done, i * 2 + 3)
                for c in range(C):
                    for half in range(2):
                        k = 2 * c + half
                        dve.wait_ge(comb_ps, i * 4 + (k + 1) + 1)
                        dve.wait_ge(comb_add, i * 4 + 1)
                        cols = slice(half * NB, (half + 1) * NB)
                        nc.vector.scalar_tensor_tensor(yacc[:, c, cols], bank[2 + half][:], cur[:, 1, c:c + 1],
                                                       yacc[:, c, cols], ALU.mult, ALU.add).then_inc(comb_add, 1)
                dve.wait_ge(gatT_ps, i + 2)
                nc.vector.tensor_copy(gatT, bank[7][:, 0:S]).then_inc(gatT_sb, 1)
            dve.wait_ge(comb_add, items * 4 + 1)
            residual(3)

        @block.gpsimd
        def _(pool):
            links = [0]

            def link(ins):
                links[0] += 1
                ins.then_inc(pool_link, 1)
                pool.wait_ge(pool_link, links[0])

            nc.gpsimd.memset(relx, NEG).then_inc(relx_set, 1)
            nc.gpsimd.iota(iota[:], pattern=[[1, P]], base=0, channel_multiplier=0,
                           allow_small_or_imprecise_dtypes=True).then_inc(const, 1)
            for tile in (ident, upper, lower):
                nc.gpsimd.memset(tile[:], 0.0 if tile is ident else 1.0).then_inc(pool_link, 1)
                links[0] += 1
            nc.gpsimd.memset(flip, 0.0).then_inc(pool_link, 1)
            nc.gpsimd.memset(nhalf[:], -0.5).then_inc(pool_link, 1)
            links[0] += 2
            pool.wait_ge(pool_link, links[0])

            def select(tile, op, step, channel, base, fill):
                return nc.gpsimd.affine_select(out=tile, in_=tile, compare_op=op, fill=fill, base=base,
                                               pattern=[[step, P]], channel_multiplier=channel)

            select(ident[:], ALU.not_equal, -1, 1, 0, 1.0).then_inc(const, 1)
            select(upper[:], ALU.is_gt, 1, -1, 0, 0.0).then_inc(const, 1)
            select(lower[:], ALU.is_ge, -1, 1, 0, 0.0).then_inc(const, 1)
            select(flip, ALU.not_equal, 1, 1, -(P - 1), 1.0).then_inc(const, 1)

            def inv_rms(done, wait_sem, wait_val, col, parts, at_col, free):
                pool.wait_ge(wait_sem, wait_val)
                src = ss[:, col:col + 1]
                if parts == 2:
                    link(nc.gpsimd.tensor_tensor(src, src, ss[:, col + 1:col + 2], ALU.add))
                link(nc.gpsimd.tensor_scalar(src, src, 1.0 / D, EPS, ALU.mult, ALU.add))
                nc.gpsimd.tensor_tensor(rstd[:, at_col:at_col + 1], src, nhalf[:, 0:1], ALU.pow).then_inc(done, 1)

            def norm(q):
                for c in range(C):
                    if q:
                        pool.wait_ge(xn_done, C * q)
                    inv_rms(rstd_done, sq_done, C * q + c + 1, c, 1, c, None)

            def after(q, count):
                for c in range(C):
                    if q:
                        pool.wait_ge(x_done, 4 * q)
                    if q % 2 == 0:
                        inv_rms(ry_done, ysq_done, count + 2 * c + 2, 2 * c, 2, 4 + c, None)
                    else:
                        inv_rms(ry_done, ysq_done, count + c + 1, c, 1, 4 + c, None)

            def keep_earlier(s, fill_done):
                select(at[:, s, 0:P], ALU.is_gt, 1, -1, 0, 0.0)
                select(at[:, s, S:384], ALU.is_gt, 1, -1, 0, 0.0).then_inc(fill_done, 1)

            def mixer(l):
                for p in range(4):
                    for s in range(2):
                        pool.wait_ge(sb_sum, 8 * l + 2 * p + s + 1)
                        keep_earlier(s, sb_lm)
                    for s in range(2):
                        pool.wait_ge(sb_att, 8 * l + 2 * p + s + 1)
                        keep_earlier(s, at_done)

            norm(0)
            mixer(0)
            after(0, 0)
            norm(1)
            after(1, 4)
            norm(2)
            mixer(1)
            after(2, 6)
            norm(3)
            after(3, 10)

        @block.tensor
        def _(pe):
            def three(out, a_hi, a_lo, b_hi, b_lo, first, last, check=True):
                kw = {} if check else {"skip_group_check": True}
                nc.tensor.matmul(out, a_hi, b_hi, start=first, stop=False, **kw)
                nc.tensor.matmul(out, a_lo, b_hi, start=False, stop=False, **kw)
                return nc.tensor.matmul(out, a_hi, b_lo, start=False, stop=last, **kw)

            def unit(s, n):
                hi = whi[:, s % SPLIT, :].rearrange("p (k n) -> p k n", n=n)
                lo = wlo[:, s % SPLIT, :].rearrange("p (k n) -> p k n", n=n)
                return hi, lo

            def use(s, r=0):
                pe.wait_ge(lo_done, number(s, r) + 1)

            def transposes(q):
                for c in range(C):
                    pe.wait_ge(xn_done, C * q + c + 1)
                    if q == 0 and c == 0:
                        pe.wait_ge(bias_sb, 4)
                    for half in range(2):
                        for k in range(4):
                            kk = 4 * half + k
                            ins = nc.tensor.transpose(bank[2 * c + half][:, k * P:(k + 1) * P],
                                                      xn[:, c, kk * P:(kk + 1) * P], ident[:])
                        ins.then_inc(xT_done, 1)

            def gate_rows(q):
                pe.wait_ge(gd_done, KC * (q + 1))
                for half in range(2):
                    nc.tensor.matmul(bank[4 + half][:], ones[:], gdiag[:, half * NB:(half + 1) * NB], start=True,
                                     stop=True).then_inc(gps_done, 1)

            def mixer(l):
                base = MIX1 if l else MIX0

                def rows_step(s, a_hi, a_lo, kcs, banks, first, last):
                    w_hi, w_lo = unit(s, NB)
                    for c in range(C):
                        cs = slice(c * P, (c + 1) * P)
                        for k in range(4):
                            ins = three(bank[banks[c]][:], a_hi[:, kcs + k, cs], a_lo[:, kcs + k, cs], w_hi[:, k, :],
                                        w_lo[:, k, :], first and k == 0, last and k == 3)
                    return ins

                def scores(p):
                    for s in range(2):
                        z = bank[4 + s]
                        rows = slice(s * DH, (s + 1) * DH)
                        b = 0 if p < 4 else 2
                        qT = qkT[rows, b, p % 4, :]
                        kT = qkT[rows, b + 1, p % 4, :]
                        if p or l:
                            pe.wait_ge(at_done, 16 * l + 2 * p)
                        if p < 4:
                            nc.tensor.matmul(z[:, 0:S], kT[:, 0:P], qT, start=True, stop=True)
                            nc.tensor.matmul(z[:, S:384], kT[:, P:S], qT[:, P:S], start=False, stop=True,
                                             skip_group_check=True).then_inc(z_done, 1)
                        else:
                            nc.tensor.matmul(z[:, 0:S], qT[:, P:S], kT, start=True, stop=True)
                            nc.tensor.matmul(z[:, S:384], qT[:, 0:P], kT[:, 0:P], start=True, stop=True)\
                                .then_inc(z_done, 1)

                def arguments(p):
                    for s in range(2):
                        z = bank[4 + s]
                        if p < 4:
                            pe.wait_ge(sb_lm, 8 * l + 2 * p + s + 1)
                            nc.tensor.matmul(z[:, 0:384], lower[:], at[:, s, :], start=False, stop=True,
                                             skip_group_check=True)
                            nc.tensor.matmul(z[:, P:S], ones[:], at[:, s, S:384], start=False, stop=True,
                                             skip_group_check=True).then_inc(arg_done, 1)
                        else:
                            pe.wait_ge(mo_p, 2 * (8 * l + 2 * (p - 4) + s + 1))
                            nc.tensor.transpose(z[:, 0:P], eb[:, s, S:384], ident[:])
                            nc.tensor.transpose(z[:, P:S], eb[:, s, 0:P], ident[:])
                            nc.tensor.transpose(z[:, S:384], eb[:, s, P:S], ident[:]).then_inc(arg_done, 1)

                def weighted(p):
                    if p or l:
                        pe.wait_ge(olo_done, 8 * l + p)
                    for s in range(2):
                        pe.wait_ge(at_done, 16 * l + 2 * p + s + 1)
                        out = bank[6][s * DH:(s + 1) * DH, :]
                        cols = slice((2 * (p % 4) + s) * DH, (2 * (p % 4) + s + 1) * DH)
                        nc.tensor.matmul(out[:, 0:S], vals[:, p // 4, 0, cols], at[:, s, 0:S], start=True, stop=True)
                        ins = nc.tensor.matmul(out[:, P:S], vals[:, p // 4, 1, cols], at[:, s, S:384], start=False,
                                               stop=True, skip_group_check=True)
                    ins.then_inc(pv_done, 1)

                for u in range(MIX_UNITS):
                    s = base + u
                    use(s)
                    if u == 0:
                        pe.wait_ge(hlo_done, C * (2 * l + 1))
                        pe.wait_ge(h32b, KC * (2 * l + 1))
                    if u < 20:
                        j, kh = divmod(u, 2)
                        if kh == 0 and (j >= 2):
                            pe.wait_ge(blk_evac, 2 * (BLK * l + j - 1))
                        if j in (0, 1, 3, 4):
                            w_hi, w_lo = unit(s, NB)
                            for cc in range(4):
                                out = bank[2 * (j % 2) + cc // 2][:, (cc % 2) * S:(cc % 2 + 1) * S]
                                cols = slice(cc * P, (cc + 1) * P)
                                for k in range(4):
                                    kk = 4 * kh + k
                                    ins = three(out, w_hi[:, k, cols], w_lo[:, k, cols], hhi[:, kk, :], hlo[:, kk, :],
                                                kh == 0 and k == 0 and cc % 2 == 0, kh == 1 and k == 3, check=False)
                        else:
                            b2 = 2 * (j % 2)
                            ins = rows_step(s, hhi, hlo, 4 * kh, (b2, b2 + 1), kh == 0, kh == 1)
                        ins.then_inc(unit_used, 1)
                    elif u < 24:
                        half = u % 2
                        branch = (u - 20) // 2
                        if u == 20:
                            pe.wait_ge(blk_evac, 2 * BLK * (l + 1))
                            pe.wait_ge(olo_done, 8 * l + 4)
                        if u == 22:
                            pe.wait_ge(olo_done, 8 * l + 8)
                        if u == 23:
                            pe.wait_ge(mg_evac, 8 * l + 2)
                        banks = [(0, 1), (2, 3), (4, 5), (0, 1)][u - 20]
                        rows_step(s, ohi, olo, 4 * branch, banks, True, True).then_inc(unit_used, 1)
                    else:
                        half, kh = divmod(u - 24, 2)
                        if u == 24:
                            pe.wait_ge(mlo_done, 4 * l + 2)
                            pe.wait_ge(mg_evac, 8 * (l + 1))
                        if u == 25:
                            pe.wait_ge(mlo_done, 4 * l + 4)
                        banks = [(0, 1), (2, 3)][half]
                        rows_step(s, hhi, hlo, 4 * kh, banks, kh == 0, kh == 1).then_inc(unit_used, 1)
                    if 7 <= u < 23 and (u - 7) % 2 == 0:
                        weighted((u - 7) // 2)
                    if 6 <= u < 22 and (u - 6) % 2 == 0:
                        arguments((u - 6) // 2)
                    if 5 <= u < 21 and (u - 5) % 2 == 0:
                        if u == 5:
                            pe.wait_ge(blk_evac, 2 * (BLK * l + 2))
                        if u == 7:
                            pass
                        if u == 13:
                            pe.wait_ge(blk_evac, 2 * (BLK * l + 5))
                        scores((u - 5) // 2)
                    if u in (6, 14):
                        pe.wait_ge(blk_evac, 2 * (BLK * l + (3 if u == 6 else 6)))
                    for m in mods_of_step(l, u):
                        mod_column(pe, m)
                    if u == 23:
                        for i in range(4):
                            half, c = divmod(i, 2)
                            pe.wait_ge(mg_evac, 8 * l + 4 + 2 * half + c + 1)
                            for k in range(4):
                                kk = 4 * half + k
                                ins = nc.tensor.transpose(bank[[2, 3, 6, 4][i]][:, k * P:(k + 1) * P],
                                                          merged[:, c, kk * P:(kk + 1) * P], ident[:])
                            ins.then_inc(mT_done, 1)
                    if u == 25:
                        gate_rows(2 * l)

            def up(n, s, r, kh, banks):
                use(s, r)
                w_hi, w_lo = unit(s, NB)
                for c in range(n):
                    cs = slice(c * P, (c + 1) * P)
                    for k in range(4):
                        ins = three(bank[banks + c][:], hhi[:, 4 * kh + k, cs], hlo[:, 4 * kh + k, cs], w_hi[:, k, :],
                                    w_lo[:, k, :], kh == 0 and k == 0, kh == 1 and k == 3)
                ins.then_inc(unit_used, 1)

            def hidden_T(n, t, c):
                pe.wait_ge(g_done, t * n + (base_of[n] + c + 1))
                wait_at_least(pe, gl_done, t * n + (base_of[n] + c))
                for k in range(4):
                    ins = nc.tensor.transpose(bank[6][:, k * P:(k + 1) * P], hid[:, c, k * P:(k + 1) * P], ident[:])
                ins.then_inc(gT_done, 1)

            def dense_down(t, s, r):
                pe.wait_ge(gl_done, t * 2 + 2)
                use(s, r)
                use(s + 1, r)
                for c in range(C):
                    cs = slice(c * P, (c + 1) * P)
                    for half in range(2):
                        if c:
                            pe.wait_ge(yadd_done, t * 4 + (half + 1) + 1)
                        else:
                            pe.wait_ge(yadd_done, t * 4 + 1)
                        for k in range(4):
                            w_hi, w_lo = unit(s + k // 2, D)
                            cols = slice(half * NB, (half + 1) * NB)
                            ins = three(bank[4 + half][:], ohi[:, k, cs], olo[:, k, cs], w_hi[:, k % 2, cols],
                                        w_lo[:, k % 2, cols], k == 0, k == 3)
                            if k % 2 and c and half:
                                ins.then_inc(unit_used, 1)
                        if not (c and half):
                            ins.then_inc(yp_done, 1)

            def expert_down(t, s, r, part, last=False):
                use(s, r)
                w_hi, w_lo = unit(s, D)
                for k in range(2):
                    kk = 2 * part + k
                    for half in range(2):
                        cols = slice(half * NB, (half + 1) * NB)
                        ins = three(bank[4 + half][:], ohi[:, kk, 0:P], olo[:, kk, 0:P], w_hi[:, k, cols],
                                    w_lo[:, k, cols], False, last and k == 1, check=False)
                ins.then_inc(unit_used, 1)

            base_of = {2: FFN_BASE[0], 1: FFN_BASE[1]}

            pe.wait_ge(const, 8)
            pe.wait_ge(small_in, 16 * 7)
            nc.tensor.transpose(bank[6][:, 0:DEPTH * MODS], rowsM, ident[0:DEPTH * MODS, 0:DEPTH * MODS])\
                .then_inc(cols_ps, 1)
            nc.tensor.transpose(bank[6][:, P:P + 72], rowsB, ident[0:72, 0:72]).then_inc(cols_ps, 1)
            pe.wait_ge(rel_in, 32)
            nc.tensor.matmul(bank[5][0:HEADS, 0:DIST], relx, onehot, start=True, stop=True).then_inc(dist_ps, 1)
            for m in range(16):
                mod_column(pe, m)
                if m == 7:
                    pe.wait_ge(hank_in, 16)
                    for i in range(4):
                        nc.tensor.matmul(bank[i][:], flip, hank[:, 2 * i:2 * i + 2, :].rearrange("p h j -> p (h j)"),
                                         start=True, stop=True).then_inc(flip_ps, 1)
            transposes(0)
            mixer(0)
            transposes(1)
            pe.wait_ge(hlo_done, C * 2)
            for j in range(4):
                up(2, FFN0 + j, 0, j % 2, 2 * (j // 2))
                if j == 2:
                    gate_rows(1)
                mod_column(pe, MODS + j)
            pe.wait_ge(gate_sb, 4)
            with pe.Fori(0, FBLK - 1) as t:
                for j in range(6):
                    if j == 0:
                        pe.wait_ge(silu_done, t * 2 + 2)
                    if j == 2:
                        pe.wait_ge(g_done, t * 2 + 2)
                    if j < 4:
                        up(2, FFN0 + 4 + j, t, j % 2, 2 * (j // 2))
                    if j == 1:
                        hidden_T(2, t, 0)
                    if j == 2:
                        hidden_T(2, t, 1)
                    if j == 4:
                        dense_down(t, FFN0 + 8, t)
                    mod_column(pe, t * 6 + (MODS + 4 + j))
            for c in range(C):
                hidden_T(2, FBLK - 1, c)
            dense_down(FBLK - 1, FFN0 + 4 + 6 * (FBLK - 1), 0)
            for j in range(2):
                mod_column(pe, MODS + 4 + 6 * (FBLK - 1) + j)
            transposes(2)
            mixer(1)
            transposes(3)

            pe.wait_ge(h32a, KC * 4)
            pe.wait_ge(h32b, KC * 4)
            pe.wait_ge(gate_sb, 6)
            for c in range(C):
                for k in range(KC):
                    ins = nc.tensor.matmul(bank[4][:, c * E:(c + 1) * E], h32[:, k, c * P:(c + 1) * P], wr[:, k, :],
                                           start=k == 0, stop=k == KC - 1)
            ins.then_inc(lg_done, 1)
            pe.wait_ge(mem_done, 1)
            mem = rt[:, 7, :, :]
            b5 = bank[5]
            nc.tensor.matmul(b5[:, 0:E], upper[:], mem[:, 0, :], start=True, stop=True)
            nc.tensor.matmul(b5[:, E:2 * E], ones[:], mem[:, 0, :], start=True, stop=False)
            nc.tensor.matmul(b5[:, E:2 * E], upper[:], mem[:, 1, :], start=False, stop=True)
            nc.tensor.matmul(b5[:, 2 * E:3 * E], ones[:], mem[:, 0, :], start=True, stop=False)
            nc.tensor.matmul(b5[:, 2 * E:3 * E], ones[:], mem[:, 1, :], start=False, stop=True).then_inc(pos_done, 1)

            def gather(item):
                pe.wait_ge(gat_done, item * 2 + 2)
                for half in range(2):
                    for k in range(4):
                        kk = 4 * half + k
                        for c in range(C):
                            ins = nc.tensor.matmul(bank[2 + half][:, k * P:(k + 1) * P], xn[:, c, kk * P:(kk + 1) * P],
                                                   gat[:, c, :], start=c == 0, stop=c == C - 1)
                    ins.then_inc(gath_done, 1)

            def slots_T(item):
                for c in range(C):
                    ins = nc.tensor.transpose(bank[7][:, c * P:(c + 1) * P], gat[:, c, :], ident[:])
                ins.then_inc(gatT_ps, 1)

            gather(0)
            slots_T(0)
            pe.wait_ge(ctl_done, 1)
            gate_rows(3)
            nc.tensor.matmul(bank[6][0:1, 0:1], ones[:, 0:1], ones[:, 0:1], start=True, stop=True).then_inc(comb_ps, 1)
            items = pe.value_load(ctli[0:1, 0:1], min_val=E, max_val=ITEMS)
            with pe.Fori(0, items) as i:
                pe.wait_ge(elo_done, i + 1)
                pe.wait_ge(gatT_sb, i + 1)
                for j in range(4):
                    if j == 0:
                        pe.wait_ge(silu_done, i * FBLK + base_of[1])
                    if j == 2:
                        pe.wait_ge(g_done, i * FBLK + base_of[1])
                    up(1, MOE0 + j, i * FBLK, j % 2, j // 2)
                with pe.Fori(0, FBLK - 1) as t:
                    for j in range(6):
                        if j == 0:
                            pe.wait_ge(silu_done, i * FBLK + t + (base_of[1] + 1))
                        if j == 2:
                            pe.wait_ge(g_done, i * FBLK + t + (base_of[1] + 1))
                        if j < 4:
                            up(1, MOE0 + 4 + j, i * FBLK + t, j % 2, j // 2)
                        if j == 1:
                            hidden_T(1, i * FBLK + t, 0)
                        if j == 4:
                            pe.wait_ge(gl_done, i * FBLK + t + (base_of[1] + 1))
                            pe.wait_ge(yzero, i * 2 + 2)
                        if j >= 4:
                            expert_down(t, MOE0 + 4 + j, i * FBLK + t, j - 4)
                pe.wait_ge(comb_add, i * 4 + 1)
                gather(i + 1)
                hidden_T(1, i * FBLK + (FBLK - 1), 0)
                pe.wait_ge(gl_done, i * FBLK + (base_of[1] + FBLK))
                for j in range(2):
                    expert_down(None, MOE0 + FFN_UNITS - 2 + j, i * FBLK, j, last=j == 1)
                pe.wait_ge(h32e_done, i * KC + 2 * KC)
                for c in range(C):
                    for half in range(2):
                        pe.wait_ge(ysb_done, i * 2 + half + 1)
                        if c:
                            pe.wait_ge(comb_add, i * 4 + (half + 1) + 1)
                        nc.tensor.matmul(bank[2 + half][:], gatT[:, c * P:(c + 1) * P],
                                         ysb[:, half * NB:(half + 1) * NB], start=True, stop=True)\
                            .then_inc(comb_ps, 1)
                slots_T(i + 1)


def _bucket_onehot():
    import numpy as np
    table = np.zeros((BUCKETS + 1, DIST), np.float32)
    exact = BUCKETS // 2
    for i in range(DIST):
        dist = S - 1 - i
        if dist < 0:
            table[BUCKETS, i] = 1
        elif dist < exact:
            table[dist, i] = 1
        else:
            large = exact + int(np.float32(np.log(np.float32(dist) / np.float32(exact)))
                                / np.float32(np.log(128 / exact)) * np.float32(BUCKETS - exact))
            table[min(large, BUCKETS - 1), i] = 1
    return table


_INS = ["x", "c", "w_mod", "b_mod", "g_mix_pre", "g_mix_post", "g_ffn_pre", "g_ffn_post", "w_in", "w_proj_sb",
        "w_proj_moba", "w_out", "rel_bias", "w1_dense", "w3_dense", "w2_dense", "w_router", "w1_moe", "w3_moe",
        "w2_moe"]


def kernel(**inputs):
    import numpy as np
    import concourse.bacc as bacc
    from concourse.bass_utils import run_bass_kernel_spmd as run

    nc = bacc.Bacc("TRN2", target_bir_lowering=False, num_devices=1)
    arrays = {f"in_{name}": np.ascontiguousarray(inputs[name]) for name in _INS}
    arrays["in_bucket_onehot"] = _bucket_onehot()
    args = [nc.dram_tensor(k, a.shape, mybir.dt.from_np(a.dtype), kind="ExternalInput").ap()
            for k, a in arrays.items()]
    scratch = nc.dram_tensor("dist_scratch", (HEADS, 384), F32, kind="Internal").ap()
    out = nc.dram_tensor("out_0", (1, S, D), F32, kind="ExternalOutput").ap()
    build(nc, *args, scratch, out)
    r = run(nc, [arrays], core_ids=[0])
    return r.results[0]["out_0"]
```

```python
from contextlib import ExitStack

import concourse.bass as bass
from concourse import mybir

F32 = mybir.dt.float32
F32R = mybir.dt.float32r
I32 = mybir.dt.int32
ALU = mybir.AluOpType
ACT = mybir.ActivationFunctionType
AX = mybir.AxisListType.X

P = 128
D = 1024
KC = D // P
S = 256
C = S // P
DH = 64
HEADS = 8
DEPTH = 2
NB = 512
UNIT = 2048
FF = 3584
FBLK = FF // NB
E = 8
EXTRA = 3
ITEMS = E + EXTRA
BUCKETS = 32
BLK = 10
MIX_UNITS = 28
FFN_UNITS = 6 * FBLK
RAW = 6
SPLIT = 3
LEAD = 2
MODS = 48
MOD_FIRST = 16
MOD_UNITS = 8
MRAW = 2
MOD_LAG = 4
EPS = 1e-6
NEG = -1e30
DIST = S + P - 1

MIX0 = 0
FFN0 = MIX0 + MIX_UNITS
MIX1 = FFN0 + FFN_UNITS
MOE0 = MIX1 + MIX_UNITS
FFN_BASE = [0, 2 * FBLK]


def build(nc, x_d, c_d, w_mod, b_mod, g_mix_pre, g_mix_post, g_ffn_pre, g_ffn_post, w_in, w_psb, w_pmo, w_out,
          rel_bias, w1_d, w3_d, w2_d, w_router, w1_m, w3_m, w2_m, onehot_d, dist_scratch, out_d):
    with ExitStack() as ctx:
        def sb(name, shape, dt=F32):
            return ctx.enter_context(nc.sbuf_tensor(name, shape, dt))

        def sem(name):
            return ctx.enter_context(nc.semaphore(name))

        raw = sb("raw", [P, RAW, UNIT])
        whi = sb("whi", [P, SPLIT, UNIT], F32R)
        wlo = sb("wlo", [P, SPLIT, UNIT], F32R)
        mraw = sb("mraw", [P, MRAW, KC, P])
        macc = sb("macc", [P, 2, P])
        x = sb("x", [P, C, D])
        hhi = sb("hhi", [P, KC, S], F32R)
        hlo = sb("hlo", [P, KC, S], F32R)
        ohi = sb("ohi", [P, KC, S], F32R)
        olo = sb("olo", [P, KC, S], F32R)
        wide = sb("wide", [P, 2 * C * D])
        gates = wide[:].rearrange("p (c n) -> p c n", c=C)
        xn = wide[:, 0:C * D].rearrange("p (c n) -> p c n", c=C)
        yacc = wide[:, C * D:2 * C * D].rearrange("p (c n) -> p c n", c=C)
        vals = sb("vals", [P, 2, C, NB])
        h32 = vals[:].rearrange("p b c n -> p (b c n)").rearrange("p (k t) -> p k t", k=KC)
        gat = vals[:, 1, 0, 0:S].rearrange("p (c s) -> p c s", c=C)
        gatT = vals[:, 1, 0, S:2 * S]
        h32e = vals[:, 0, :, :].rearrange("p c n -> p (c n)").rearrange("p (k t) -> p k t", k=KC)
        qk = sb("qk", [P, 4 * 4 * S])
        qkT = qk[:].rearrange("p (b c t) -> p b c t", b=4, c=4)
        merged = qk[:, 0:C * D].rearrange("p (c n) -> p c n", c=C)
        mtmp = qk[:, 2048:3072].rearrange("p (c n) -> p c n", c=C)
        hid = qk[:, 0:C * NB].rearrange("p (c n) -> p c n", c=C)
        silu = qk[:, C * NB:2 * C * NB].rearrange("p (c n) -> p c n", c=C)
        ysb = qk[:, 2048:3072]
        gdiag = qk[:, 3072:4096]
        bias = sb("bias", [P, HEADS, S])
        gate = sb("gate", [P, D])
        eb = sb("eb", [P, 2, 384])
        at = sb("at", [P, 2, 384])
        ident = sb("ident", [P, P])
        upper = sb("upper", [P, P])
        lower = sb("lower", [P, P])
        ones = sb("ones", [P, P])
        iota = sb("iota", [P, P])
        modT = sb("modT", [P, DEPTH * MODS])
        colsB = sb("colsB", [P, 72])
        colsM = sb("colsM", [P, DEPTH * MODS])
        cond = sb("cond", [P, KC])
        wr = sb("wr", [P, KC, E])
        ss = sb("ss", [P, 8])
        rstd = sb("rstd", [P, 8])
        nhalf = sb("nhalf", [P, 8])
        A = sb("A", [P, KC])
        gcol = sb("gcol", [P, KC])
        nmx = sb("nmx", [P, 4])
        rs = sb("rs", [P, 4])
        rt = at[:, 1, 0:192].rearrange("p (n c e) -> p n c e", n=12, c=C)
        ex = at[:, 0, 0:64].rearrange("p (n c e) -> p n c e", n=4, c=C)
        posI = sb("posI", [P, C, ITEMS + 1])
        wI = sb("wI", [P, C, ITEMS + 1])
        cur = sb("cur", [P, 2, C])
        ctl = sb("ctl", [P, 8])
        ctli = sb("ctli", [P, 8], I32)
        rowsM = qk[0:DEPTH * MODS, 2048:2048 + P]
        rowsB = qk[0:72, 2176:2176 + P]
        onehot = qk[0:BUCKETS + 1, 2304:2304 + DIST]
        relx = qk[0:BUCKETS + 1, 2690:2690 + HEADS]
        distb = qk[0:HEADS, 2700:2700 + 384]
        modrow = wide[0:1, C * D:2 * C * D]
        flip = eb[:, 0, 0:P]
        hank = qk[:, 0:HEADS * S].rearrange("p (h j) -> p h j", h=HEADS)

        bank = [ctx.enter_context(nc.psum_tensor(f"bank{i}", [P, NB], F32)) for i in range(8)]
        MODB = bank[7]

        raw_full = [sem(f"raw_full{i}") for i in range(RAW)]
        mraw_full = [sem(f"mraw_full{i}") for i in range(MRAW)]
        hi_done = sem("hi_done")
        lo_done = sem("lo_done")
        unit_used = sem("unit_used")
        mod_link = sem("mod_link")
        mod_acc = sem("mod_acc")
        mod_col = sem("mod_col")
        mod_evac = sem("mod_evac")
        mod_prod = sem("mod_prod")
        mod_unit = sem("mod_unit")
        mod_row = sem("mod_row")
        mod_first = sem("mod_first")
        cnt_sb = sem("cnt_sb")
        ex_done = sem("ex_done")
        small_in = sem("small_in")
        x_in = sem("x_in")
        rel_in = sem("rel_in")
        hank_in = sem("hank_in")
        dist_out = sem("dist_out")
        x_out = sem("x_out")
        const = sem("const")
        relx_set = sem("relx_set")
        cols_ps = sem("cols_ps")
        cols_sb = sem("cols_sb")
        cond_done = sem("cond_done")
        dist_ps = sem("dist_ps")
        dist_sb = sem("dist_sb")
        flip_ps = sem("flip_ps")
        bias_sb = sem("bias_sb")
        dve_link = sem("dve_link")
        pool_link = sem("pool_link")
        sq_done = sem("sq_done")
        rstd_done = sem("rstd_done")
        xn_done = sem("xn_done")
        xT_done = sem("xT_done")
        ab_done = sem("ab_done")
        h32a = sem("h32a")
        h32b = sem("h32b")
        hhi_done = sem("hhi_done")
        hlo_done = sem("hlo_done")
        blk_evac = sem("blk_evac")
        z_done = sem("z_done")
        z_abs = sem("z_abs")
        z_relu = sem("z_relu")
        sb_exp1 = sem("sb_exp1")
        sb_ln = sem("sb_ln")
        sb_sum = sem("sb_sum")
        sb_lm = sem("sb_lm")
        arg_done = sem("arg_done")
        sb_att = sem("sb_att")
        mo_max = sem("mo_max")
        mo_exp = sem("mo_exp")
        mo_p = sem("mo_p")
        bank_free = sem("bank_free")
        at_done = sem("at_done")
        pv_done = sem("pv_done")
        ohi_done = sem("ohi_done")
        olo_done = sem("olo_done")
        sig_done = sem("sig_done")
        mg_evac = sem("mg_evac")
        mT_done = sem("mT_done")
        mhi_done = sem("mhi_done")
        mlo_done = sem("mlo_done")
        gd_done = sem("gd_done")
        gps_done = sem("gps_done")
        gate_sb = sem("gate_sb")
        ysq_done = sem("ysq_done")
        ry_done = sem("ry_done")
        x_done = sem("x_done")
        silu_done = sem("silu_done")
        g_done = sem("g_done")
        gT_done = sem("gT_done")
        gh_done = sem("gh_done")
        gl_done = sem("gl_done")
        yp_done = sem("yp_done")
        yadd_done = sem("yadd_done")
        lg_done = sem("lg_done")
        rexp_in = sem("rexp_in")
        rexp = sem("rexp")
        mem_done = sem("mem_done")
        pos_done = sem("pos_done")
        ctl_done = sem("ctl_done")
        cur_done = sem("cur_done")
        gat_done = sem("gat_done")
        gath_done = sem("gath_done")
        h32e_done = sem("h32e_done")
        ehi_done = sem("ehi_done")
        elo_done = sem("elo_done")
        gatT_ps = sem("gatT_ps")
        gatT_sb = sem("gatT_sb")
        ysb_done = sem("ysb_done")
        yzero = sem("yzero")
        comb_ps = sem("comb_ps")
        comb_add = sem("comb_add")

        def dma_value(s, r):
            return 16 * ((s + MOD_UNITS) // RAW + 1) + r * 16

        def slot(s):
            return (s + MOD_UNITS) % RAW

        def number(s, r):
            return s + r * 6

        def wait_at_least(eng, semaphore, value):
            if not isinstance(value, int) or value > 0:
                eng.wait_ge(semaphore, value)

        def split_hi(act, s, r=0):
            act.wait_ge(raw_full[slot(s)], dma_value(s, r))
            wait_at_least(act, unit_used, number(s, r) - SPLIT + 1)
            nc.scalar.activation(whi[:, s % SPLIT, :], raw[:, slot(s), :], ACT.Copy).then_inc(hi_done, 1)

        def split_lo(dve, s, r=0):
            dve.wait_ge(hi_done, number(s, r) + 1)
            wait_at_least(dve, unit_used, number(s, r) - SPLIT + 1)
            nc.vector.tensor_tensor(wlo[:, s % SPLIT, :], raw[:, slot(s), :], whi[:, s % SPLIT, :].bitcast(F32),
                                    ALU.subtract).then_inc(lo_done, 1)

        def mod_product(dve, m, ms):
            dve.wait_ge(mraw_full[ms], 16 * ((m - MOD_FIRST) // MRAW + 1) if isinstance(m, int)
                        else m * (16 // MRAW) + (16 - (MOD_FIRST + ms) * (16 // MRAW)))
            nc.vector.tensor_tensor(mraw[:, ms, :, :], mraw[:, ms, :, :],
                                    cond[:].rearrange("p (k a) -> p k a", a=1).broadcast_to([P, KC, P]), ALU.mult)\
                .then_inc(mod_prod, 1)

        def mod_sum(pool, m, ms):
            pool.wait_ge(mod_prod, m - (MOD_FIRST - 1))
            nc.gpsimd.tensor_tensor(mraw[:, ms, 0:4, :], mraw[:, ms, 0:4, :], mraw[:, ms, 4:8, :], ALU.add)\
                .then_inc(mod_link, 1)
            pool.wait_ge(mod_link, m * 2 - (2 * MOD_FIRST - 1))
            nc.gpsimd.tensor_tensor(mraw[:, ms, 0:2, :], mraw[:, ms, 0:2, :], mraw[:, ms, 2:4, :], ALU.add)\
                .then_inc(mod_link, 1)
            pool.wait_ge(mod_link, m * 2 - (2 * MOD_FIRST - 2))
            wait_at_least(pool, mod_col, m - (MOD_FIRST + 1))
            nc.gpsimd.tensor_tensor(macc[:, ms, :], mraw[:, ms, 0, :], mraw[:, ms, 1, :], ALU.add)\
                .then_inc(mod_acc, 1)

        def mod_column(pe, m, ms):
            pe.wait_ge(mod_acc, m - (MOD_FIRST - 1))
            out = MODB[:, m:m + 1] if isinstance(m, int) else MODB[:, bass.ds(m, 1)]
            nc.tensor.matmul(out, macc[:, ms, :], ones[:, 0:1], start=True, stop=True).then_inc(mod_col, 1)

        def mod_take(dve, first, end, col_count):
            wait_at_least(dve, mod_col, col_count)
            nc.vector.tensor_copy(modT[:, first:end], MODB[:, first:end]).then_inc(mod_evac, 1)

        def mods_of_step(phase, u):
            if phase == 0:
                first = 16 + (2 * u if u < 4 else 4 + u)
                return list(range(first, first + (2 if u < 4 else 1)))
            return [90 + u] if u < 6 else []

        G_PRE = [0, 32, 8, 40]
        G_POST = [16, 48, 24, 56]
        C_COL = 64
        SH = [0, 24, 48, 72]
        SC = [8, 32, 56, 80]
        GT = [16, 40, 64, 88]

        block = ctx.enter_context(nc.Block())

        @block.sync
        def _(sp):
            def load_mix(l, u):
                if u < 20:
                    j, kh = divmod(u, 2)
                    return w_in[l, kh * 512:(kh + 1) * 512, j * NB:(j + 1) * NB].rearrange("(k p) n -> p k n", p=P)
                if u < 24:
                    w = w_psb if u < 22 else w_pmo
                    half = u % 2
                    return w[l, :, half * NB:(half + 1) * NB].rearrange("(k p) n -> p k n", p=P)
                half, kh = divmod(u - 24, 2)
                return w_out[l, kh * 512:(kh + 1) * 512, half * NB:(half + 1) * NB].rearrange("(k p) n -> p k n", p=P)

            def load_up(w, kh, b):
                cols = slice(b * NB, (b + 1) * NB) if isinstance(b, int) else bass.ds(b * NB, NB)
                return w.rearrange("(k p) n -> p k n", p=P)[:, kh * 4:kh * 4 + 4, cols]

            def load_down(w, part, b):
                rows = w.rearrange("(b q k p) n -> b q p k n", q=2, k=2, p=P)
                return rows[b, part]

            def load(s, r, src):
                if isinstance(s, int) and isinstance(r, int) and s + 6 * r < RAW:
                    wait_at_least(sp, mod_unit, s + MOD_UNITS - RAW + 1)
                wait_at_least(sp, lo_done, number(s, r) - RAW + 1)
                n = src.shape[-1]
                sp.dma_start(raw[:, slot(s), :].rearrange("p (k n) -> p k n", n=n), src)\
                    .then_inc(raw_full[slot(s)], 16)

            def load_mod(m, ms, l, col):
                wait_at_least(sp, mod_acc, m - (MOD_FIRST + MRAW - 1))
                cols = slice(col * P, col * P + P) if isinstance(col, int) else bass.ds(col * P, P)
                sp.dma_start(mraw[:, ms, :, :], w_mod[l].rearrange("(k p) n -> p k n", p=P)[:, :, cols])\
                    .then_inc(mraw_full[ms], 16)

            def ffn_unit(ws, b, j):
                if j < 4:
                    return load_up(ws[j // 2], j % 2, b)
                return load_down(ws[2], j - 4, b - 1)

            sp.dma_start(rowsM, b_mod.rearrange("l (m p) -> (l m) p", p=P)).then_inc(small_in, 16)
            for i, g in enumerate([g_mix_pre, g_mix_post, g_ffn_pre, g_ffn_post]):
                sp.dma_start(rowsB[16 * i:16 * i + 16, :], g.rearrange("l (m p) -> (l m) p", p=P))\
                    .then_inc(small_in, 16)
            sp.dma_start(rowsB[64:72, :], c_d.rearrange("b (m p) -> (b m) p", p=P)).then_inc(small_in, 16)
            sp.dma_start(x[:], x_d.rearrange("b (c p) n -> p (b c) n", p=P)).then_inc(x_in, 16)
            sp.dma_start(onehot, onehot_d).then_inc(rel_in, 16)
            sp.wait_ge(relx_set, 1)
            sp.dma_start(relx[0:BUCKETS, :], rel_bias).then_inc(rel_in, 16)
            sp.dma_start(wr[:], w_router[0].rearrange("(k p) e -> p k e", p=P)).then_inc(small_in, 16)
            for i in range(MOD_UNITS):
                cb, kh = divmod(i, 2)
                if i >= RAW:
                    sp.wait_ge(mod_unit, i - RAW + 1)
                sp.dma_start(raw[:, i % RAW, :].rearrange("p (k n) -> p k n", n=NB),
                             w_mod[0, kh * 512:(kh + 1) * 512, cb * NB:(cb + 1) * NB]
                             .rearrange("(k p) n -> p k n", p=P)).then_inc(raw_full[i % RAW], 16)
                if i == 3:
                    sp.wait_ge(dist_sb, 1)
                    sp.dma_start(dist_scratch[:, 0:DIST], distb[:, 0:DIST]).then_inc(dist_out, 16)
                    sp.wait_ge(dist_out, 16)
                    sp.dma_start(hank, bass.AP(dist_scratch.tensor, 0, [[1, P], [384, HEADS], [1, S]]))\
                        .then_inc(hank_in, 16)

            def phase_unit(n):
                if n < FFN0:
                    return load_mix(0, n)
                if n < MIX1:
                    u = n - FFN0
                    return ffn_unit(dense, 0, u) if u < 4 else ffn_unit(dense, FBLK, u - FFN_UNITS + 6)
                return load_mix(1, n - MIX1)

            dense = (w1_d[0], w3_d[0], w2_d[0])

            for s in range(LEAD):
                load(s, 0, phase_unit(s))
            for u in range(MIX_UNITS):
                load(u + LEAD, 0, phase_unit(u + LEAD))
                if u >= MOD_LAG:
                    for m in mods_of_step(0, u - MOD_LAG):
                        load_mod(m, m % MRAW, 0, m)
            for j in range(4):
                s = FFN0 + j + LEAD
                load(s, 0, ffn_unit(dense, 0, j + LEAD) if j + LEAD < 4 else ffn_unit(dense, 1, j + LEAD - 4))
                m = MODS + j - MOD_LAG
                load_mod(m, m % MRAW, 0, m)
            with sp.Fori(0, FBLK - 2) as t:
                for j in range(6):
                    jj = j + LEAD
                    src = ffn_unit(dense, t + 1, jj) if jj < 6 else ffn_unit(dense, t + 2, jj - 6)
                    load(FFN0 + 4 + jj, t, src)
                    load_mod(t * 6 + (MODS + 4 + j - MOD_LAG), j % MRAW, 1, t * 6 + (4 + j - MOD_LAG))
            for j in range(6):
                jj = j + LEAD
                src = ffn_unit(dense, FBLK - 1, jj) if jj < 6 else ffn_unit(dense, FBLK, jj - 2)
                load(FFN0 + 4 + jj + 6 * (FBLK - 2), 0, src)
                m = MODS + 4 + 6 * (FBLK - 2) + j - MOD_LAG
                load_mod(m, m % MRAW, 1, m - MODS)
            for j in range(2):
                load(MIX1 + j, 0, load_mix(1, j))
                m = MODS + 4 + 6 * (FBLK - 1) + j - MOD_LAG
                load_mod(m, m % MRAW, 1, m - MODS)
            for u in range(MIX_UNITS - LEAD):
                load(MIX1 + u + LEAD, 0, load_mix(1, u + LEAD))
                m = 90 + u - MOD_LAG
                if m < DEPTH * MODS:
                    load_mod(m, m % MRAW, 1, m - MODS)

            def load_expert(e, item):
                ws = (w1_m[0, e], w3_m[0, e], w2_m[0, e])
                for j in range(4):
                    load(MOE0 + j, item * FBLK, ffn_unit(ws, 0, j))
                with sp.Fori(0, FBLK - 1) as t:
                    for j in range(6):
                        load(MOE0 + 4 + j, item * FBLK + t, ffn_unit(ws, t + 1, j))
                for j in range(2):
                    load(MOE0 + FFN_UNITS - 2 + j, item * FBLK, load_down(ws[2], j, FBLK - 1))

            with sp.Fori(0, E) as e:
                load_expert(e, e)
            sp.wait_ge(ctl_done, 1)
            over = sp.value_load(ctli[0:1, 1:2], min_val=0, max_val=EXTRA)
            with sp.If(over > 0):
                with sp.Fori(0, over) as i:
                    e = sp.value_load(ctli[0:1, bass.ds(i + 2, 1)], min_val=0, max_val=E - 1)
                    load_expert(e, i + E)
            items = over + E
            for j in range(LEAD):
                load(MOE0 + j, items * FBLK, load_mix(0, j))
            for j in range(LEAD):
                sp.wait_ge(raw_full[slot(MOE0 + j)], dma_value(MOE0 + j, items * FBLK))
            sp.wait_ge(x_done, 4 * 4)
            sp.dma_start(out_d.rearrange("b (c p) n -> p (b c) n", p=P), x[:]).then_inc(x_out, 16)
            sp.wait_ge(x_out, 16)

        @block.scalar
        def _(act):
            def squares_of_x(q):
                for c in range(C):
                    if q:
                        act.wait_ge(x_done, 4 * (q - 1) + 2 * c + 2)
                        act.wait_ge(rstd_done, C * q)
                        act.wait_ge(xT_done, 4 * q)
                        act.wait_ge(ysq_done, squares[0])
                    elif c == 0:
                        act.wait_ge(x_in, 16)
                    scr = h32[:].rearrange("p k t -> p (k t)")[:, c * D:(c + 1) * D]
                    nc.scalar.activation(scr, x[:, c, :], ACT.Square, accum_out=ss[:, c:c + 1]).then_inc(sq_done, 1)

            def norm(q):
                if q:
                    squares_of_x(q)
                act.wait_ge(xT_done, 4 * q + 2)
                act.wait_ge(ab_done, q + 1)
                act.wait_ge(sq_done, C * (q + 1))
                for k in range(KC):
                    src = bank[k // 4][:, (k % 4) * P:(k % 4 + 1) * P]
                    nc.scalar.activation(h32[:, k, 0:P], src, ACT.Identity, scale=A[:, k:k + 1],
                                         bias=modT[:, SH[q] + k:SH[q] + k + 1]).then_inc(h32a, 1)
                if q < 3:
                    act.wait_ge(h32a, KC * (q + 1))
                    nc.scalar.activation(hhi[:, :, 0:P], h32[:, :, 0:P], ACT.Copy).then_inc(hhi_done, 1)
                    act.wait_ge(h32b, KC * (q + 1))
                    nc.scalar.activation(hhi[:, :, P:S], h32[:, :, P:S], ACT.Copy).then_inc(hhi_done, 1)

            def mixer(l):
                base = MIX1 if l else MIX0

                def block_out(j):
                    act.wait_ge(unit_used, base + 2 * j + 2)
                    for i in range(2):
                        src = bank[2 * (j % 2) + i]
                        if j in (0, 1, 3, 4):
                            b = [0, 1, None, 2, 3][j]
                            nc.scalar.activation(qkT[:, b, 2 * i:2 * i + 2, :].rearrange("p c t -> p (c t)"), src[:],
                                                 ACT.Copy, scale=DH ** -0.5 if b % 2 == 0 else 1.0)\
                                .then_inc(blk_evac, 1)
                        elif j in (2, 5):
                            nc.scalar.activation(vals[:, j // 4, i, :], src[:], ACT.Copy).then_inc(blk_evac, 1)
                        else:
                            nc.scalar.activation(gates[:, i, (j - 6) * NB:(j - 5) * NB], src[:], ACT.Copy)\
                                .then_inc(blk_evac, 1)

                def after_scores(p):
                    if p < 4:
                        pair = 4 * l + p
                        act.wait_ge(z_abs, 2 * pair + 2)
                        nc.scalar.activation(eb[:], eb[:], ACT.Exp).then_inc(sb_exp1, 1)
                        act.wait_ge(sb_exp1, pair + 1)
                        nc.scalar.activation(eb[:], eb[:], ACT.Ln, bias=1.0).then_inc(sb_ln, 1)
                        return
                    for s in range(2):
                        nmo = 8 * l + 2 * (p - 4) + s
                        act.wait_ge(mo_max, 2 * (nmo + 1))
                        nc.scalar.activation(eb[:, s, 0:S], eb[:, s, 0:S], ACT.Exp, bias=nmx[:, 2 * s:2 * s + 1],
                                             accum_out=rs[:, 2 * s:2 * s + 1]).then_inc(mo_exp, 1)
                        nc.scalar.activation(eb[:, s, S:384], eb[:, s, S:384], ACT.Exp,
                                             bias=nmx[:, 2 * s + 1:2 * s + 2],
                                             accum_out=rs[:, 2 * s + 1:2 * s + 2]).then_inc(mo_exp, 1)

                def after_arg(p):
                    for s in range(2):
                        n = 16 * l + 2 * p + s
                        act.wait_ge(arg_done, n + 1)
                        if p < 4:
                            nc.scalar.activation(at[:, s, :], bank[4 + s][:, 0:384], ACT.Exp).then_inc(sb_att, 1)
                        else:
                            nc.scalar.activation(at[:, s, :], bank[4 + s][:, 0:384], ACT.Copy).then_inc(at_done, 1)

                def after_pv(p):
                    act.wait_ge(pv_done, 8 * l + p + 1)
                    nc.scalar.activation(ohi[:, p, :], bank[6][:, 0:S], ACT.Copy).then_inc(ohi_done, 1)

                for u in range(MIX_UNITS):
                    split_hi(act, base + u + LEAD)
                    if u < 20 and u % 2 == 1:
                        block_out(u // 2)
                    if 7 <= u < 23 and (u - 7) % 2 == 0:
                        after_pv((u - 7) // 2)
                    if 5 <= u < 21 and (u - 5) % 2 == 0:
                        after_scores((u - 5) // 2)
                    if 6 <= u < 22 and (u - 6) % 2 == 0:
                        after_arg((u - 6) // 2)
                    if u == 19:
                        act.wait_ge(blk_evac, 2 * BLK * (l + 1))
                        for c in range(C):
                            nc.scalar.activation(gates[:, c, :], gates[:, c, :], ACT.Sigmoid).then_inc(sig_done, 1)
                    if u == 23:
                        for i in range(4):
                            half, c = divmod(i, 2)
                            act.wait_ge(mT_done, 4 * l + i + 1)
                            nc.scalar.activation(hhi[:, 4 * half:4 * half + 4, c * P:(c + 1) * P],
                                                 bank[[2, 3, 6, 4][i]][:].rearrange("p (k t) -> p k t", k=4),
                                                 ACT.Copy).then_inc(mhi_done, 1)

            def out_squares(q):
                for c in range(C):
                    act.wait_ge(rstd_done, C * (q + 1))
                    if q % 2 == 0:
                        for half in range(2):
                            act.wait_ge(unit_used, (MIX1 if q else MIX0) + 26 + 2 * half)
                            scr = eb[:].rearrange("p a n -> p (a n)")[:, 0:NB]
                            act.wait_ge(at_done, 16 * (q // 2 + 1))
                            if c or half:
                                act.wait_ge(ysq_done, squares[0])
                            squares[0] += 1
                            nc.scalar.activation(scr, bank[2 * half + c][:], ACT.Square,
                                                 accum_out=ss[:, 2 * c + half:2 * c + half + 1]).then_inc(ysq_done, 1)
                    else:
                        if q == 1:
                            act.wait_ge(yadd_done, 4 * FBLK + 1)
                        else:
                            act.wait_ge(comb_add, items4[0])
                        if c:
                            act.wait_ge(ysq_done, squares[0])
                        squares[0] += 1
                        nc.scalar.activation(h32[:].rearrange("p k t -> p (k t)")[:, 0:D] if q == 1 else hid[:].rearrange("p c n -> p (c n)"),
                                             yacc[:, c, :], ACT.Square, accum_out=ss[:, c:c + 1]).then_inc(ysq_done, 1)

            squares = [0]
            items4 = [0]

            def ffn_silu(n, t, units):
                for c in range(n):
                    act.wait_ge(unit_used, units)
                    wait_at_least(act, g_done, t * n + base_of[n])
                    nc.scalar.activation(silu[:, c, :], bank[c][:], ACT.Silu).then_inc(silu_done, 1)

            def ffn_ghi(n, t, c):
                act.wait_ge(gT_done, t * n + (base_of[n] + c + 1))
                nc.scalar.activation(ohi[:, 0:4, c * P:(c + 1) * P], bank[6][:].rearrange("p (k t) -> p k t", k=4),
                                     ACT.Copy).then_inc(gh_done, 1)

            base_of = {2: FFN_BASE[0], 1: FFN_BASE[1]}

            act.wait_ge(cols_sb, 2)
            nc.scalar.activation(cond[:], colsB[:, C_COL:C_COL + KC], ACT.Silu).then_inc(cond_done, 1)
            squares_of_x(0)
            for cb in range(4):
                act.wait_ge(mod_unit, 2 * cb + 2)
                nc.scalar.activation(modrow[:, cb * NB:(cb + 1) * NB], bank[6 + cb % 2][0:1, :], ACT.Copy)\
                    .then_inc(mod_row, 1)
            norm(0)
            for s in range(LEAD):
                split_hi(act, s)
            mixer(0)
            out_squares(0)
            norm(1)
            for j in range(4):
                split_hi(act, FFN0 + j + LEAD)
                if j == 1:
                    ffn_silu(2, 0, FFN0 + 2)

            def block_steps(n, s0, r, t):
                for j in range(6):
                    split_hi(act, s0 + j + LEAD, r)
                    if j == 1:
                        ffn_silu(n, t, number(s0, r) + 2)
                        ffn_ghi(n, t - 1, 0)
                    if j == 2 and n == 2:
                        ffn_ghi(n, t - 1, 1)

            with act.Fori(0, FBLK - 1) as t:
                block_steps(2, FFN0 + 4, t, t + 1)
            for c in range(C):
                ffn_ghi(2, FBLK - 1, c)
            for j in range(2):
                split_hi(act, MIX1 + j)
            out_squares(1)
            norm(2)
            mixer(1)
            out_squares(2)
            norm(3)
            act.wait_ge(rexp_in, 1)
            nc.scalar.activation(rt[:, 9, :, 0], rt[:, 8, :, 0], ACT.Exp).then_inc(rexp, 1)

            def expert_h(item):
                act.wait_ge(gath_done, item * 2 + 2)
                wait_at_least(act, elo_done, item)
                for k in range(KC):
                    src = bank[2 + k // 4][:, (k % 4) * P:(k % 4 + 1) * P]
                    nc.scalar.activation(h32e[:, k, :], src, ACT.Identity, scale=A[:, k:k + 1],
                                         bias=modT[:, SH[3] + k:SH[3] + k + 1]).then_inc(h32e_done, 1)
                act.wait_ge(h32e_done, item * KC + KC)
                nc.scalar.activation(hhi[:, :, 0:P], h32e[:], ACT.Copy).then_inc(ehi_done, 1)

            act.wait_ge(lg_done, 1)
            expert_h(0)

            def expert(i):
                for j in range(4):
                    split_hi(act, MOE0 + j + LEAD, i * FBLK)
                    if j == 1:
                        ffn_silu(1, i * FBLK, i * FFN_UNITS + (MOE0 + 2))
                with act.Fori(0, FBLK - 1) as t:
                    block_steps(1, MOE0 + 4, i * FBLK + t, i * FBLK + t + 1)
                ffn_ghi(1, i * FBLK + (FBLK - 1), 0)
                expert_h(i + 1)
                for j in range(2):
                    split_hi(act, MOE0 + FFN_UNITS + j, i * FBLK)
                act.wait_ge(unit_used, i * FFN_UNITS + (MOE0 + FFN_UNITS))
                act.wait_ge(comb_ps, i * 4 + 1)
                for half in range(2):
                    nc.scalar.activation(ysb[:, half * NB:(half + 1) * NB], bank[4 + half][:], ACT.Copy)\
                        .then_inc(ysb_done, 1)

            with act.Fori(0, E) as i:
                expert(i)
            act.wait_ge(ctl_done, 1)
            over = act.value_load(ctli[0:1, 1:2], min_val=0, max_val=EXTRA)
            with act.If(over > 0):
                with act.Fori(0, over) as i:
                    expert(i + E)
            items4[0] = (over + E) * 4 + 1
            out_squares(3)

        @block.vector
        def _(dve):
            links = [0]

            def link(ins):
                links[0] += 1
                ins.then_inc(dve_link, 1)
                dve.wait_ge(dve_link, links[0])

            def normed(q):
                for c in range(C):
                    dve.wait_ge(rstd_done, C * q + c + 1)
                    nc.vector.tensor_scalar(xn[:, c, :], x[:, c, :], rstd[:, c:c + 1], None, ALU.mult)\
                        .then_inc(xn_done, 1)

            def norm(q):
                link(nc.vector.tensor_tensor(modT[:, SH[q]:SH[q] + 16], modT[:, SH[q]:SH[q] + 16],
                                             colsM[:, SH[q]:SH[q] + 16], ALU.add))
                nc.vector.scalar_tensor_tensor(A[:], modT[:, SC[q]:SC[q] + KC], 1.0,
                                               colsB[:, G_PRE[q]:G_PRE[q] + KC], ALU.add, ALU.mult)\
                    .then_inc(ab_done, 1)
                if q:
                    normed(q)
                dve.wait_ge(xT_done, 4 * q + 4)
                dve.wait_ge(sq_done, C * (q + 1))
                dve.wait_ge(ab_done, q + 1)
                for k in range(KC):
                    src = bank[2 + k // 4][:, (k % 4) * P:(k % 4 + 1) * P]
                    nc.vector.tensor_scalar(h32[:, k, P:S], src, A[:, k:k + 1], modT[:, SH[q] + k:SH[q] + k + 1],
                                            ALU.mult, ALU.add).then_inc(h32b, 1)
                if q < 3:
                    for c in range(C):
                        dve.wait_ge(hhi_done, C * q + c + 1)
                        if c:
                            dve.wait_ge(h32b, KC * (q + 1))
                        nc.vector.tensor_tensor(hlo[:, :, c * P:(c + 1) * P], h32[:, :, c * P:(c + 1) * P],
                                                hhi[:, :, c * P:(c + 1) * P].bitcast(F32), ALU.subtract)\
                            .then_inc(hlo_done, 1)

            def gate_diag(q):
                link(nc.vector.tensor_tensor(gcol[:], modT[:, GT[q]:GT[q] + KC], colsM[:, GT[q]:GT[q] + KC], ALU.add))
                link(nc.vector.tensor_tensor(gcol[:], gcol[:], colsB[:, G_POST[q]:G_POST[q] + KC], ALU.mult))
                for k in range(KC):
                    nc.vector.tensor_scalar(gdiag[:, k * P:(k + 1) * P], ident[:], gcol[:, k:k + 1], None, ALU.mult)\
                        .then_inc(gd_done, 1)

            def gate_take(q):
                for half in range(2):
                    dve.wait_ge(gps_done, 2 * q + half + 1)
                    nc.vector.tensor_copy(gate[:, half * NB:(half + 1) * NB], bank[4 + half][:]).then_inc(gate_sb, 1)

            def residual(q):
                dve.wait_ge(gate_sb, 2 * (q + 1))
                for c in range(C):
                    dve.wait_ge(ry_done, C * q + c + 1)
                    tmp = [None] * 2
                    for half in range(2):
                        cols = slice(half * NB, (half + 1) * NB)
                        src = bank[2 * half + c][:] if q % 2 == 0 else yacc[:, c, cols]
                        if c == 0 and half == 0 and q % 2 == 0:
                            dve.wait_ge(ysq_done, [4, 0, 10][q])
                        if q == 3 and c == 0 and half == 0:
                            dve.wait_ge(ysq_done, 12)
                        links[0] += 1
                        nc.vector.scalar_tensor_tensor(mtmp[:, half, :], src, rstd[:, 4 + c:5 + c], gate[:, cols],
                                                       ALU.mult, ALU.mult).then_inc(dve_link, 1)
                        tmp[half] = links[0]
                    for half in range(2):
                        cols = slice(half * NB, (half + 1) * NB)
                        dve.wait_ge(dve_link, tmp[half])
                        nc.vector.tensor_tensor(x[:, c, cols], x[:, c, cols], mtmp[:, half, :], ALU.add)\
                            .then_inc(x_done, 1)
                    dve.wait_ge(x_done, 4 * q + 2 * c + 2)


            def mixer(l):
                base = MIX1 if l else MIX0
                q = 2 * l

                def after_scores(p):
                    for s in range(2):
                        n = 16 * l + 2 * p + s
                        z = bank[4 + s]
                        dve.wait_ge(z_done, n + 1)
                        if p < 4:
                            nc.vector.tensor_scalar(at[:, s, :], z[:, 0:384], 0.0, None, ALU.max).then_inc(z_relu, 1)
                            dve.wait_ge(z_relu, 8 * l + 2 * p + s + 1)
                            nc.vector.scalar_tensor_tensor(eb[:, s, :], at[:, s, :], -2.0, z[:, 0:384], ALU.mult,
                                                           ALU.add).then_inc(z_abs, 1)
                        else:
                            h = 2 * (p - 4) + s
                            links[0] += 2
                            nc.vector.tensor_tensor(eb[:, s, 0:S], z[:, 0:S], bias[:, h, :], ALU.add)\
                                .then_inc(dve_link, 1)
                            nc.vector.tensor_tensor(eb[:, s, S:384], z[:, S:384], bias[:, h, P:S], ALU.add)\
                                .then_inc(dve_link, 1)
                            dve.wait_ge(dve_link, links[0])
                            nc.vector.tensor_reduce(nmx[:, 2 * s:2 * s + 1], eb[:, s, 0:S], AX, ALU.max, negate=True)\
                                .then_inc(mo_max, 1)
                            nc.vector.tensor_reduce(nmx[:, 2 * s + 1:2 * s + 2], eb[:, s, S:384], AX, ALU.max,
                                                    negate=True).then_inc(mo_max, 1)
                    for s in range(2):
                        if p < 4:
                            nsb = 8 * l + 2 * p + s
                            dve.wait_ge(sb_ln, 4 * l + p + 1)
                            dve.wait_ge(z_relu, nsb + 1)
                            nc.vector.scalar_tensor_tensor(at[:, s, :], eb[:, s, :], -1.0, at[:, s, :], ALU.mult,
                                                           ALU.subtract).then_inc(sb_sum, 1)
                        else:
                            nmo = 8 * l + 2 * (p - 4) + s
                            dve.wait_ge(mo_exp, 2 * (nmo + 1))
                            link(nc.vector.reciprocal(rs[:, 2 * s:2 * s + 2], rs[:, 2 * s:2 * s + 2]))
                            nc.vector.tensor_scalar(eb[:, s, 0:S], eb[:, s, 0:S], rs[:, 2 * s:2 * s + 1], None,
                                                    ALU.mult).then_inc(mo_p, 1)
                            nc.vector.tensor_scalar(eb[:, s, S:384], eb[:, s, S:384], rs[:, 2 * s + 1:2 * s + 2],
                                                    None, ALU.mult).then_inc(mo_p, 1)

                def after_pv(p):
                    dve.wait_ge(ohi_done, 8 * l + p + 1)
                    nc.vector.tensor_tensor(olo[:, p, :], bank[6][:, 0:S], ohi[:, p, :].bitcast(F32), ALU.subtract)\
                        .then_inc(olo_done, 1)

                for u in range(MIX_UNITS):
                    split_lo(dve, base + u + LEAD)
                    if 7 <= u < 23 and (u - 7) % 2 == 0:
                        after_pv((u - 7) // 2)
                    if 5 <= u < 21 and (u - 5) % 2 == 0:
                        after_scores((u - 5) // 2)
                    for m in mods_of_step(l, u):
                        mod_product(dve, m, m % MRAW)
                    if u == 22:
                        first, end = [(MOD_FIRST, 42), (90, 96)][l]
                        mod_take(dve, first, end, end - MOD_FIRST)
                        dve.wait_ge(mod_evac, [2, 5][l])
                    if 20 <= u < 22:
                        half = u - 20
                        dve.wait_ge(sig_done, C * (l + 1))
                        for c in range(C):
                            dve.wait_ge(unit_used, base + u + 1)
                            nc.vector.tensor_tensor(merged[:, c, half * NB:(half + 1) * NB], bank[2 * half + c][:],
                                                    gates[:, c, half * NB:(half + 1) * NB], ALU.mult)\
                                .then_inc(mg_evac, 1)
                    if 22 <= u < 24:
                        half = u - 22
                        for c in range(C):
                            dve.wait_ge(unit_used, base + u + 1)
                            link(nc.vector.tensor_tensor(mtmp[:, c, :], bank[(4 if half == 0 else 0) + c][:],
                                                         gates[:, c, D + half * NB:D + (half + 1) * NB], ALU.mult))
                            dve.wait_ge(mg_evac, 8 * l + 2 * half + c + 1)
                            cols = slice(half * NB, (half + 1) * NB)
                            nc.vector.tensor_tensor(merged[:, c, cols], merged[:, c, cols], mtmp[:, c, :], ALU.add)\
                                .then_inc(mg_evac, 1)
                    if u == 23:
                        for i in range(4):
                            half, c = divmod(i, 2)
                            dve.wait_ge(mhi_done, 4 * l + i + 1)
                            nc.vector.tensor_tensor(hlo[:, 4 * half:4 * half + 4, c * P:(c + 1) * P],
                                                    bank[[2, 3, 6, 4][i]][:].rearrange("p (k t) -> p k t", k=4),
                                                    hhi[:, 4 * half:4 * half + 4, c * P:(c + 1) * P].bitcast(F32),
                                                    ALU.subtract).then_inc(mlo_done, 1)
                        gate_diag(q)
                    if u == 25:
                        gate_take(q)

            def ffn_g(n, t, units):
                for c in range(n):
                    dve.wait_ge(unit_used, units)
                    dve.wait_ge(silu_done, t * n + (base_of[n] + c + 1))
                    wait_at_least(dve, gT_done, t * n + base_of[n])
                    nc.vector.tensor_tensor(hid[:, c, :], silu[:, c, :], bank[(2 if n == 2 else 1) + c][:], ALU.mult)\
                        .then_inc(g_done, 1)

            def ffn_glo(n, t, c):
                dve.wait_ge(gh_done, t * n + (base_of[n] + c + 1))
                nc.vector.tensor_tensor(olo[:, 0:4, c * P:(c + 1) * P], bank[6][:].rearrange("p (k t) -> p k t", k=4),
                                        ohi[:, 0:4, c * P:(c + 1) * P].bitcast(F32), ALU.subtract)\
                    .then_inc(gl_done, 1)

            def dense_add(t, c, units):
                if True:
                    for half in range(2):
                        k = 2 * c + half
                        if k < 3:
                            dve.wait_ge(yp_done, t * 3 + (k + 1))
                        else:
                            dve.wait_ge(unit_used, units)
                        dve.wait_ge(yadd_done, t * 4 + 1)
                        cols = slice(half * NB, (half + 1) * NB)
                        nc.vector.tensor_tensor(yacc[:, c, cols], yacc[:, c, cols], bank[4 + half][:], ALU.add)\
                            .then_inc(yadd_done, 1)

            base_of = {2: FFN_BASE[0], 1: FFN_BASE[1]}

            nc.vector.memset(ones[:], 1.0).then_inc(const, 1)
            nc.vector.memset(posI[:], -1.0).then_inc(const, 1)
            nc.vector.memset(wI[:], 0.0).then_inc(const, 1)
            dve.wait_ge(cols_ps, 2)
            nc.vector.tensor_copy(colsM[:], bank[4][:, 0:DEPTH * MODS]).then_inc(cols_sb, 1)
            nc.vector.tensor_copy(colsB[:], bank[4][:, P:P + 72]).then_inc(cols_sb, 1)
            dve.wait_ge(dist_ps, 1)
            nc.vector.tensor_copy(distb[:, 0:DIST], bank[5][0:HEADS, 0:DIST]).then_inc(dist_sb, 1)
            dve.wait_ge(cond_done, 1)
            normed(0)
            for i in range(4):
                dve.wait_ge(flip_ps, i + 1)
                nc.vector.tensor_copy(bias[:, 2 * i:2 * i + 2, :].rearrange("p h j -> p (h j)"), bank[4 + i % 2][:])\
                    .then_inc(bias_sb, 1)
            dve.wait_ge(mod_first, 1)
            mod_take(dve, 0, MOD_FIRST, 0)
            dve.wait_ge(mod_evac, 1)
            norm(0)
            for s in range(LEAD):
                split_lo(dve, s)
            mixer(0)
            residual(0)
            norm(1)
            mod_take(dve, 42, MODS, MODS - MOD_FIRST)
            dve.wait_ge(mod_evac, 3)
            gate_diag(1)
            nc.vector.memset(yacc[:], 0.0).then_inc(yadd_done, 1)
            for j in range(4):
                split_lo(dve, FFN0 + j + LEAD)
                mod_product(dve, MODS + j, j % MRAW)
                if j == 3:
                    gate_take(1)
                    ffn_g(2, 0, FFN0 + 4)
            with dve.Fori(0, FBLK - 1) as t:
                for j in range(6):
                    split_lo(dve, FFN0 + 4 + j + LEAD, t)
                    if j == 1:
                        ffn_glo(2, t, 0)
                    if j == 2:
                        ffn_glo(2, t, 1)
                    mod_product(dve, t * 6 + (MODS + 4 + j), j % MRAW)
                    if j == 3:
                        ffn_g(2, t + 1, t * 6 + (FFN0 + 8))
                    if j == 4:
                        dense_add(t, 0, None)
                dense_add(t, 1, t * 6 + (FFN0 + 10))
            for c in range(C):
                ffn_glo(2, FBLK - 1, c)
            for j in range(2):
                split_lo(dve, MIX1 + j)
                m = MODS + 4 + 6 * (FBLK - 1) + j
                mod_product(dve, m, m % MRAW)
                dense_add(FBLK - 1, j, MIX1)
            mod_take(dve, MODS, 90, 90 - MOD_FIRST)
            dve.wait_ge(mod_evac, 4)
            residual(1)
            norm(2)
            mixer(1)
            residual(2)
            norm(3)
            gate_diag(3)

            lg, cand, oh1, oh2, t5, pos, comb, mem = (rt[:, i, :, :] for i in range(8))
            m1, m2, i1, w1, w2 = (rt[:, 10, :, i:i + 1] for i in range(5))
            dlt = rt[:, 8, :, 0:1]
            ex = rt[:, 9, :, 0:1]
            cnt = rt[:, 11, 0, :]

            def wide8(v):
                return v.broadcast_to([P, C, E])

            iota8 = iota[:, 0:E].rearrange("p (a e) -> p a e", a=1).broadcast_to([P, C, E])

            def first_of_largest(values, top, onehot_out):
                link(nc.vector.tensor_reduce(top, values, AX, ALU.max))
                link(nc.vector.tensor_tensor(cand, values, wide8(top), ALU.is_lt))
                link(nc.vector.tensor_scalar(cand, cand, 100.0, None, ALU.mult))
                link(nc.vector.tensor_tensor(cand, cand, iota8, ALU.add))
                link(nc.vector.tensor_reduce(i1, cand, AX, ALU.min))
                link(nc.vector.tensor_tensor(onehot_out, iota8, wide8(i1), ALU.is_equal))

            dve.wait_ge(lg_done, 1)
            link(nc.vector.tensor_copy(lg, bank[4][:, 0:C * E].rearrange("p (c e) -> p c e", c=C)))
            first_of_largest(lg, m1, oh1)
            link(nc.vector.tensor_scalar(t5, oh1, NEG, None, ALU.mult))
            link(nc.vector.tensor_tensor(t5, t5, lg, ALU.add))
            first_of_largest(t5, m2, oh2)
            nc.vector.tensor_tensor(dlt, m2, m1, ALU.subtract).then_inc(rexp_in, 1)
            nc.vector.tensor_tensor(mem, oh1, oh2, ALU.add).then_inc(mem_done, 1)
            dve.wait_ge(rexp, 1)
            link(nc.vector.tensor_scalar(w1, ex, 1.0, None, ALU.add))
            link(nc.vector.reciprocal(w1, w1))
            link(nc.vector.tensor_tensor(w2, ex, w1, ALU.mult))
            link(nc.vector.tensor_tensor(comb, oh1, wide8(w1), ALU.mult))
            link(nc.vector.tensor_tensor(t5, oh2, wide8(w2), ALU.mult))
            link(nc.vector.tensor_tensor(comb, comb, t5, ALU.add))
            link(nc.vector.tensor_copy(wI[:, :, 0:E], comb))
            dve.wait_ge(pos_done, 1)
            link(nc.vector.tensor_scalar(pos, bank[5][:, 0:C * E].rearrange("p (c e) -> p c e", c=C), 1.0, None, ALU.add))
            link(nc.vector.tensor_tensor(pos, pos, mem, ALU.mult))
            link(nc.vector.tensor_scalar(pos, pos, -1.0, None, ALU.add))
            link(nc.vector.tensor_copy(posI[:, :, 0:E], pos))
            nc.vector.tensor_copy(cnt, bank[5][:, C * E:C * E + E]).then_inc(cnt_sb, 1)

            def expert_slots(item):
                col = slice(item, item + 1) if isinstance(item, int) else bass.ds(item, 1)
                nc.vector.tensor_copy(cur[:, 0, :], posI[:, :, col].rearrange("p c o -> p (c o)")).then_inc(cur_done, 1)
                dve.wait_ge(cur_done, 1 if isinstance(item, int) else item * 2)
                for c in range(C):
                    nc.vector.tensor_scalar(gat[:, c, :], iota[:], cur[:, 0, c:c + 1], None, ALU.is_equal)\
                        .then_inc(gat_done, 1)

            def expert_lo(item):
                dve.wait_ge(ehi_done, item + 1)
                nc.vector.tensor_tensor(hlo[:, :, 0:P], h32e[:], hhi[:, :, 0:P].bitcast(F32), ALU.subtract)\
                    .then_inc(elo_done, 1)

            dve.wait_ge(lg_done, 1)
            expert_slots(0)
            gate_take(3)
            nc.vector.memset(yacc[:], 0.0).then_inc(comb_add, 1)
            expert_lo(0)
            dve.wait_ge(gatT_ps, 1)
            nc.vector.tensor_copy(gatT, bank[7][:, 0:S]).then_inc(gatT_sb, 1)

            def expert(i):
                dve.wait_ge(gate_sb, 8)
                for half in range(2):
                    nc.vector.memset(bank[4 + half][:], 0.0).then_inc(yzero, 1)
                for j in range(4):
                    split_lo(dve, MOE0 + j + LEAD, i * FBLK)
                    if j == 3:
                        ffn_g(1, i * FBLK, i * FFN_UNITS + (MOE0 + 4))
                with dve.Fori(0, FBLK - 1) as t:
                    for j in range(6):
                        split_lo(dve, MOE0 + 4 + j + LEAD, i * FBLK + t)
                        if j == 1:
                            ffn_glo(1, i * FBLK + t, 0)
                        if j == 3:
                            ffn_g(1, i * FBLK + t + 1, i * FFN_UNITS + t * 6 + (MOE0 + 8))
                dve.wait_ge(gatT_ps, i + 1)
                dve.wait_ge(ctl_done, 1)
                expert_slots(i + 1)
                ffn_glo(1, i * FBLK + (FBLK - 1), 0)
                expert_lo(i + 1)
                for j in range(2):
                    split_lo(dve, MOE0 + FFN_UNITS + j, i * FBLK)
                nc.vector.tensor_copy(cur[:, 1, :], wI[:, :, bass.ds(i, 1)].rearrange("p c o -> p (c o)"))\
                    .then_inc(cur_done, 1)
                dve.wait_ge(cur_done, i * 2 + 3)
                for c in range(C):
                    for half in range(2):
                        k = 2 * c + half
                        dve.wait_ge(comb_ps, i * 4 + (k + 1) + 1)
                        dve.wait_ge(comb_add, i * 4 + 1)
                        cols = slice(half * NB, (half + 1) * NB)
                        nc.vector.scalar_tensor_tensor(yacc[:, c, cols], bank[2 + half][:], cur[:, 1, c:c + 1],
                                                       yacc[:, c, cols], ALU.mult, ALU.add).then_inc(comb_add, 1)
                dve.wait_ge(gatT_ps, i + 2)
                nc.vector.tensor_copy(gatT, bank[7][:, 0:S]).then_inc(gatT_sb, 1)

            with dve.Fori(0, E) as i:
                expert(i)
            over = dve.value_load(ctli[0:1, 1:2], min_val=0, max_val=EXTRA)
            with dve.If(over > 0):
                with dve.Fori(0, over) as i:
                    expert(i + E)
            dve.wait_ge(comb_add, (over + E) * 4 + 1)
            residual(3)

        @block.gpsimd
        def _(pool):
            links = [0]

            def link(ins):
                links[0] += 1
                ins.then_inc(pool_link, 1)
                pool.wait_ge(pool_link, links[0])

            nc.gpsimd.memset(relx, NEG).then_inc(relx_set, 1)
            nc.gpsimd.iota(iota[:], pattern=[[1, P]], base=0, channel_multiplier=0,
                           allow_small_or_imprecise_dtypes=True).then_inc(const, 1)
            for tile in (ident, upper, lower):
                nc.gpsimd.memset(tile[:], 0.0 if tile is ident else 1.0).then_inc(pool_link, 1)
                links[0] += 1
            nc.gpsimd.memset(flip, 0.0).then_inc(pool_link, 1)
            nc.gpsimd.memset(nhalf[:], -0.5).then_inc(pool_link, 1)
            links[0] += 2
            pool.wait_ge(pool_link, links[0])

            def select(tile, op, step, channel, base, fill):
                return nc.gpsimd.affine_select(out=tile, in_=tile, compare_op=op, fill=fill, base=base,
                                               pattern=[[step, P]], channel_multiplier=channel)

            select(ident[:], ALU.not_equal, -1, 1, 0, 1.0).then_inc(const, 1)
            select(upper[:], ALU.is_gt, 1, -1, 0, 0.0).then_inc(const, 1)
            select(lower[:], ALU.is_ge, -1, 1, 0, 0.0).then_inc(const, 1)
            select(flip, ALU.not_equal, 1, 1, -(P - 1), 1.0).then_inc(const, 1)

            def inv_rms(done, wait_sem, wait_val, col, parts, at_col, free):
                pool.wait_ge(wait_sem, wait_val)
                src = ss[:, col:col + 1]
                if parts == 2:
                    link(nc.gpsimd.tensor_tensor(src, src, ss[:, col + 1:col + 2], ALU.add))
                link(nc.gpsimd.tensor_scalar(src, src, 1.0 / D, EPS, ALU.mult, ALU.add))
                nc.gpsimd.tensor_tensor(rstd[:, at_col:at_col + 1], src, nhalf[:, 0:1], ALU.pow).then_inc(done, 1)

            def norm(q):
                for c in range(C):
                    if q:
                        pool.wait_ge(xn_done, C * q)
                    inv_rms(rstd_done, sq_done, C * q + c + 1, c, 1, c, None)

            def after(q, count):
                for c in range(C):
                    if q:
                        pool.wait_ge(x_done, 4 * q)
                    if q % 2 == 0:
                        inv_rms(ry_done, ysq_done, count + 2 * c + 2, 2 * c, 2, 4 + c, None)
                    else:
                        inv_rms(ry_done, ysq_done, count + c + 1, c, 1, 4 + c, None)

            def keep_earlier(s, fill_done):
                select(at[:, s, 0:P], ALU.is_gt, 1, -1, 0, 0.0)
                select(at[:, s, S:384], ALU.is_gt, 1, -1, 0, 0.0).then_inc(fill_done, 1)

            def mixer(l):
                for u in range(MIX_UNITS):
                    if 5 <= u < 13:
                        p = (u - 5) // 2
                        for s in range(2):
                            if u % 2:
                                pool.wait_ge(sb_sum, 8 * l + 2 * p + s + 1)
                                keep_earlier(s, sb_lm)
                            else:
                                pool.wait_ge(sb_att, 8 * l + 2 * p + s + 1)
                                keep_earlier(s, at_done)
                    for m in mods_of_step(l, u):
                        mod_sum(pool, m, m % MRAW)

            def extra_items():
                pos, comb = rt[:, 5, :, :], rt[:, 6, :, :]
                cnt, pre = ex[:, 0, 0, :], ex[:, 0, 1, :]
                sel = ex[:, 1, 0, :]
                iota8 = iota[:, 0:E]
                a, b = ex[:, 2, :, :], ex[:, 3, :, :]

                def total(out, v):
                    link(nc.gpsimd.tensor_tensor(v[:, :, 0:4], v[:, :, 0:4], v[:, :, 4:8], ALU.add))
                    link(nc.gpsimd.tensor_tensor(v[:, :, 0:2], v[:, :, 0:2], v[:, :, 2:4], ALU.add))
                    link(nc.gpsimd.tensor_tensor(out, v[:, :, 0:1], v[:, :, 1:2], ALU.add))

                pool.wait_ge(cnt_sb, 1)
                link(nc.gpsimd.tensor_scalar(cnt, rt[:, 11, 0, :], float(P), None, ALU.is_gt))
                link(nc.gpsimd.memset(pre[:, 0:1], 0.0))
                for e in range(1, E):
                    link(nc.gpsimd.tensor_tensor(pre[:, e:e + 1], pre[:, e - 1:e], cnt[:, e - 1:e], ALU.add))
                link(nc.gpsimd.tensor_tensor(ctl[:, 1:2], pre[:, E - 1:E], cnt[:, E - 1:E], ALU.add))
                for i in range(EXTRA):
                    link(nc.gpsimd.tensor_scalar(sel, pre, float(i), None, ALU.is_equal))
                    link(nc.gpsimd.tensor_tensor(sel, sel, cnt, ALU.mult))
                    for c in range(C):
                        link(nc.gpsimd.tensor_tensor(a[:, c, :], pos[:, c, :], sel, ALU.mult))
                        link(nc.gpsimd.tensor_tensor(b[:, c, :], comb[:, c, :], sel, ALU.mult))
                    total(posI[:, :, E + i:E + i + 1], a)
                    link(nc.gpsimd.tensor_scalar(posI[:, :, E + i], posI[:, :, E + i], -float(P), None, ALU.add))
                    total(wI[:, :, E + i:E + i + 1], b)
                    link(nc.gpsimd.tensor_tensor(a[:, 0, :], sel, iota8, ALU.mult))
                    total(ctl[:, 2 + i:3 + i].rearrange("p (a b) -> p a b", a=1), a[:, 0:1, :])
                nc.gpsimd.tensor_copy(ctli[:, 1:5], ctl[:, 1:5]).then_inc(ctl_done, 1)

            norm(0)
            mixer(0)
            after(0, 0)
            norm(1)
            for j in range(4):
                mod_sum(pool, MODS + j, j % MRAW)
            with pool.Fori(0, FBLK - 1) as t:
                for j in range(6):
                    mod_sum(pool, t * 6 + (MODS + 4 + j), j % MRAW)
            for j in range(2):
                mod_sum(pool, 88 + j, j % MRAW)
            after(1, 4)
            norm(2)
            mixer(1)
            after(2, 6)
            norm(3)
            extra_items()
            after(3, 10)

        @block.tensor
        def _(pe):
            def three(out, a_hi, a_lo, b_hi, b_lo, first, last, check=True):
                kw = {} if check else {"skip_group_check": True}
                nc.tensor.matmul(out, a_hi, b_hi, start=first, stop=False, **kw)
                nc.tensor.matmul(out, a_lo, b_hi, start=False, stop=False, **kw)
                return nc.tensor.matmul(out, a_hi, b_lo, start=False, stop=last, **kw)

            def unit(s, n):
                hi = whi[:, s % SPLIT, :].rearrange("p (k n) -> p k n", n=n)
                lo = wlo[:, s % SPLIT, :].rearrange("p (k n) -> p k n", n=n)
                return hi, lo

            def use(s, r=0):
                pe.wait_ge(lo_done, number(s, r) + 1)

            def transposes(q):
                for c in range(C):
                    pe.wait_ge(xn_done, C * q + c + 1)
                    if q == 0 and c == 0:
                        pe.wait_ge(const, 8)
                    for half in range(2):
                        for k in range(4):
                            kk = 4 * half + k
                            ins = nc.tensor.transpose(bank[2 * c + half][:, k * P:(k + 1) * P],
                                                      xn[:, c, kk * P:(kk + 1) * P], ident[:])
                        ins.then_inc(xT_done, 1)

            def gate_rows(q):
                pe.wait_ge(gd_done, KC * (q + 1))
                for half in range(2):
                    nc.tensor.matmul(bank[4 + half][:], ones[:], gdiag[:, half * NB:(half + 1) * NB], start=True,
                                     stop=True).then_inc(gps_done, 1)

            def mixer(l):
                base = MIX1 if l else MIX0

                def rows_step(s, a_hi, a_lo, kcs, banks, first, last):
                    w_hi, w_lo = unit(s, NB)
                    for c in range(C):
                        cs = slice(c * P, (c + 1) * P)
                        for k in range(4):
                            ins = three(bank[banks[c]][:], a_hi[:, kcs + k, cs], a_lo[:, kcs + k, cs], w_hi[:, k, :],
                                        w_lo[:, k, :], first and k == 0, last and k == 3)
                    return ins

                def scores(p):
                    for s in range(2):
                        z = bank[4 + s]
                        rows = slice(s * DH, (s + 1) * DH)
                        b = 0 if p < 4 else 2
                        qT = qkT[rows, b, p % 4, :]
                        kT = qkT[rows, b + 1, p % 4, :]
                        if p or l:
                            pe.wait_ge(at_done, 16 * l + 2 * p)
                        if p < 4:
                            nc.tensor.matmul(z[:, 0:S], kT[:, 0:P], qT, start=True, stop=True)
                            nc.tensor.matmul(z[:, S:384], kT[:, P:S], qT[:, P:S], start=False, stop=True,
                                             skip_group_check=True).then_inc(z_done, 1)
                        else:
                            nc.tensor.matmul(z[:, 0:S], qT[:, P:S], kT, start=True, stop=True)
                            nc.tensor.matmul(z[:, S:384], qT[:, 0:P], kT[:, 0:P], start=True, stop=True)\
                                .then_inc(z_done, 1)

                def arguments(p):
                    for s in range(2):
                        z = bank[4 + s]
                        if p < 4:
                            pe.wait_ge(sb_lm, 8 * l + 2 * p + s + 1)
                            nc.tensor.matmul(z[:, 0:384], lower[:], at[:, s, :], start=False, stop=True,
                                             skip_group_check=True)
                            nc.tensor.matmul(z[:, P:S], ones[:], at[:, s, S:384], start=False, stop=True,
                                             skip_group_check=True).then_inc(arg_done, 1)
                        else:
                            pe.wait_ge(mo_p, 2 * (8 * l + 2 * (p - 4) + s + 1))
                            nc.tensor.transpose(z[:, 0:P], eb[:, s, S:384], ident[:])
                            nc.tensor.transpose(z[:, P:S], eb[:, s, 0:P], ident[:])
                            nc.tensor.transpose(z[:, S:384], eb[:, s, P:S], ident[:]).then_inc(arg_done, 1)

                def weighted(p):
                    if p or l:
                        pe.wait_ge(olo_done, 8 * l + p)
                    for s in range(2):
                        pe.wait_ge(at_done, 16 * l + 2 * p + s + 1)
                        out = bank[6][s * DH:(s + 1) * DH, :]
                        cols = slice((2 * (p % 4) + s) * DH, (2 * (p % 4) + s + 1) * DH)
                        nc.tensor.matmul(out[:, 0:S], vals[:, p // 4, 0, cols], at[:, s, 0:S], start=True, stop=True)
                        ins = nc.tensor.matmul(out[:, P:S], vals[:, p // 4, 1, cols], at[:, s, S:384], start=False,
                                               stop=True, skip_group_check=True)
                    ins.then_inc(pv_done, 1)

                for u in range(MIX_UNITS):
                    s = base + u
                    use(s)
                    if u == 0:
                        pe.wait_ge(hlo_done, C * (2 * l + 1))
                        pe.wait_ge(h32b, KC * (2 * l + 1))
                    if u < 20:
                        j, kh = divmod(u, 2)
                        if kh == 0 and (j >= 2):
                            pe.wait_ge(blk_evac, 2 * (BLK * l + j - 1))
                        if j in (0, 1, 3, 4):
                            w_hi, w_lo = unit(s, NB)
                            for cc in range(4):
                                out = bank[2 * (j % 2) + cc // 2][:, (cc % 2) * S:(cc % 2 + 1) * S]
                                cols = slice(cc * P, (cc + 1) * P)
                                for k in range(4):
                                    kk = 4 * kh + k
                                    ins = three(out, w_hi[:, k, cols], w_lo[:, k, cols], hhi[:, kk, :], hlo[:, kk, :],
                                                kh == 0 and k == 0 and cc % 2 == 0, kh == 1 and k == 3, check=False)
                        else:
                            b2 = 2 * (j % 2)
                            ins = rows_step(s, hhi, hlo, 4 * kh, (b2, b2 + 1), kh == 0, kh == 1)
                        ins.then_inc(unit_used, 1)
                    elif u < 24:
                        half = u % 2
                        branch = (u - 20) // 2
                        if u == 20:
                            pe.wait_ge(blk_evac, 2 * BLK * (l + 1))
                            pe.wait_ge(olo_done, 8 * l + 4)
                        if u == 22:
                            pe.wait_ge(olo_done, 8 * l + 8)
                        if u == 23:
                            pe.wait_ge(mg_evac, 8 * l + 2)
                        banks = [(0, 1), (2, 3), (4, 5), (0, 1)][u - 20]
                        rows_step(s, ohi, olo, 4 * branch, banks, True, True).then_inc(unit_used, 1)
                    else:
                        half, kh = divmod(u - 24, 2)
                        if u == 24:
                            pe.wait_ge(mlo_done, 4 * l + 2)
                            pe.wait_ge(mg_evac, 8 * (l + 1))
                        if u == 25:
                            pe.wait_ge(mlo_done, 4 * l + 4)
                        banks = [(0, 1), (2, 3)][half]
                        rows_step(s, hhi, hlo, 4 * kh, banks, kh == 0, kh == 1).then_inc(unit_used, 1)
                    if 7 <= u < 23 and (u - 7) % 2 == 0:
                        weighted((u - 7) // 2)
                    if 6 <= u < 22 and (u - 6) % 2 == 0:
                        arguments((u - 6) // 2)
                    if 5 <= u < 21 and (u - 5) % 2 == 0:
                        if u == 5:
                            pe.wait_ge(blk_evac, 2 * (BLK * l + 2))
                        if u == 7:
                            pass
                        if u == 13:
                            pe.wait_ge(blk_evac, 2 * (BLK * l + 5))
                        scores((u - 5) // 2)
                    if u in (6, 14):
                        pe.wait_ge(blk_evac, 2 * (BLK * l + (3 if u == 6 else 6)))
                    if l == 0 and u in (1, 23):
                        pe.wait_ge(mod_evac, 1 if u == 1 else 2)
                    if l == 1 and u == 1:
                        pe.wait_ge(mod_evac, 4)
                    if u:
                        for m in mods_of_step(l, u - 1):
                            mod_column(pe, m, m % MRAW)
                    if u == 23:
                        for i in range(4):
                            half, c = divmod(i, 2)
                            pe.wait_ge(mg_evac, 8 * l + 4 + 2 * half + c + 1)
                            for k in range(4):
                                kk = 4 * half + k
                                ins = nc.tensor.transpose(bank[[2, 3, 6, 4][i]][:, k * P:(k + 1) * P],
                                                          merged[:, c, kk * P:(kk + 1) * P], ident[:])
                            ins.then_inc(mT_done, 1)
                    if u == 25:
                        gate_rows(2 * l)
                if l == 0:
                    mod_column(pe, MODS - 1, 1)

            def up(n, s, r, kh, banks):
                use(s, r)
                w_hi, w_lo = unit(s, NB)
                for c in range(n):
                    cs = slice(c * P, (c + 1) * P)
                    for k in range(4):
                        ins = three(bank[banks + c][:], hhi[:, 4 * kh + k, cs], hlo[:, 4 * kh + k, cs], w_hi[:, k, :],
                                    w_lo[:, k, :], kh == 0 and k == 0, kh == 1 and k == 3)
                ins.then_inc(unit_used, 1)

            def hidden_T(n, t, c):
                pe.wait_ge(g_done, t * n + (base_of[n] + c + 1))
                wait_at_least(pe, gl_done, t * n + (base_of[n] + c))
                for k in range(4):
                    ins = nc.tensor.transpose(bank[6][:, k * P:(k + 1) * P], hid[:, c, k * P:(k + 1) * P], ident[:])
                ins.then_inc(gT_done, 1)

            def dense_down(t, s, r):
                pe.wait_ge(gl_done, t * 2 + 2)
                use(s + 1, r)
                for c in range(C):
                    cs = slice(c * P, (c + 1) * P)
                    for half in range(2):
                        if c:
                            pe.wait_ge(yadd_done, t * 4 + (half + 1) + 1)
                        else:
                            pe.wait_ge(yadd_done, t * 4 + 1)
                        for k in range(4):
                            w_hi, w_lo = unit(s + k // 2, D)
                            cols = slice(half * NB, (half + 1) * NB)
                            ins = three(bank[4 + half][:], ohi[:, k, cs], olo[:, k, cs], w_hi[:, k % 2, cols],
                                        w_lo[:, k % 2, cols], k == 0, k == 3)
                            if k % 2 and c and half:
                                ins.then_inc(unit_used, 1)
                        if not (c and half):
                            ins.then_inc(yp_done, 1)

            def expert_down(t, s, r, part, last=False):
                use(s, r)
                w_hi, w_lo = unit(s, D)
                for k in range(2):
                    kk = 2 * part + k
                    for half in range(2):
                        cols = slice(half * NB, (half + 1) * NB)
                        ins = three(bank[4 + half][:], ohi[:, kk, 0:P], olo[:, kk, 0:P], w_hi[:, k, cols],
                                    w_lo[:, k, cols], False, last and k == 1, check=False)
                ins.then_inc(unit_used, 1)

            base_of = {2: FFN_BASE[0], 1: FFN_BASE[1]}

            pe.wait_ge(const, 8)
            pe.wait_ge(small_in, 16 * 7)
            nc.tensor.transpose(bank[4][:, 0:DEPTH * MODS], rowsM, ident[0:DEPTH * MODS, 0:DEPTH * MODS])\
                .then_inc(cols_ps, 1)
            nc.tensor.transpose(bank[4][:, P:P + 72], rowsB, ident[0:72, 0:72]).then_inc(cols_ps, 1)
            pe.wait_ge(rel_in, 32)
            nc.tensor.matmul(bank[5][0:HEADS, 0:DIST], relx, onehot, start=True, stop=True).then_inc(dist_ps, 1)
            transposes(0)
            pe.wait_ge(cond_done, 1)
            for i in range(MOD_UNITS):
                cb, kh = divmod(i, 2)
                pe.wait_ge(raw_full[i % RAW], 16 * (i // RAW + 1))
                if cb >= 2 and kh == 0:
                    pe.wait_ge(mod_row, cb - 1)
                for k in range(4):
                    ins = nc.tensor.matmul(bank[6 + cb % 2][0:1, :], cond[:, 4 * kh + k:4 * kh + k + 1],
                                           raw[:, i % RAW, k * NB:(k + 1) * NB], start=kh == 0 and k == 0,
                                           stop=kh == 1 and k == 3)
                ins.then_inc(mod_unit, 1)
                if i in (5, 7):
                    pe.wait_ge(hank_in, 16)
                    pe.wait_ge(cols_sb, 2)
                    pe.wait_ge(dist_sb, 1)
                    if i == 7:
                        pe.wait_ge(bias_sb, 2)
                    for t in range(2):
                        h = 2 * (t + (i - 5))
                        nc.tensor.matmul(bank[4 + t][:], flip, hank[:, h:h + 2, :].rearrange("p h j -> p (h j)"),
                                         start=True, stop=True).then_inc(flip_ps, 1)
            for m in range(MOD_FIRST):
                if m == 0:
                    pe.wait_ge(mod_row, 4)
                ins = nc.tensor.matmul(MODB[:, m:m + 1], modrow[:, m * P:(m + 1) * P], ones[0:1, 0:1], start=True,
                                       stop=True)
            ins.then_inc(mod_first, 1)
            mixer(0)
            transposes(1)
            pe.wait_ge(hlo_done, C * 2)
            for j in range(4):
                up(2, FFN0 + j, 0, j % 2, 2 * (j // 2))
                if j == 2:
                    gate_rows(1)
                if j == 1:
                    pe.wait_ge(mod_evac, 3)
                if j:
                    mod_column(pe, MODS + j - 1, (j - 1) % MRAW)
            pe.wait_ge(gate_sb, 4)
            with pe.Fori(0, FBLK - 1) as t:
                for j in range(6):
                    if j == 0:
                        pe.wait_ge(silu_done, t * 2 + 2)
                    if j == 2:
                        pe.wait_ge(g_done, t * 2 + 2)
                    if j < 4:
                        up(2, FFN0 + 4 + j, t, j % 2, 2 * (j // 2))
                    if j == 1:
                        hidden_T(2, t, 0)
                    if j == 2:
                        hidden_T(2, t, 1)
                    if j == 4:
                        dense_down(t, FFN0 + 8, t)
                    mod_column(pe, t * 6 + (MODS + 3 + j), (j + 1) % MRAW)
            for c in range(C):
                hidden_T(2, FBLK - 1, c)
            dense_down(FBLK - 1, FFN0 + 4 + 6 * (FBLK - 1), 0)
            for j in range(-1, 2):
                mod_column(pe, MODS + 4 + 6 * (FBLK - 1) + j, j % MRAW)
            transposes(2)
            mixer(1)
            transposes(3)

            pe.wait_ge(h32a, KC * 4)
            pe.wait_ge(h32b, KC * 4)
            pe.wait_ge(gate_sb, 6)
            for c in range(C):
                for k in range(KC):
                    ins = nc.tensor.matmul(bank[4][:, c * E:(c + 1) * E], h32[:, k, c * P:(c + 1) * P], wr[:, k, :],
                                           start=k == 0, stop=k == KC - 1)
            ins.then_inc(lg_done, 1)
            pe.wait_ge(mem_done, 1)
            mem = rt[:, 7, :, :]
            b5 = bank[5]
            nc.tensor.matmul(b5[:, 0:E], upper[:], mem[:, 0, :], start=True, stop=True)
            nc.tensor.matmul(b5[:, E:2 * E], ones[:], mem[:, 0, :], start=True, stop=False)
            nc.tensor.matmul(b5[:, E:2 * E], upper[:], mem[:, 1, :], start=False, stop=True)
            nc.tensor.matmul(b5[:, 2 * E:3 * E], ones[:], mem[:, 0, :], start=True, stop=False)
            nc.tensor.matmul(b5[:, 2 * E:3 * E], ones[:], mem[:, 1, :], start=False, stop=True).then_inc(pos_done, 1)

            def gather(item):
                pe.wait_ge(gat_done, item * 2 + 2)
                for half in range(2):
                    for k in range(4):
                        kk = 4 * half + k
                        for c in range(C):
                            ins = nc.tensor.matmul(bank[2 + half][:, k * P:(k + 1) * P], xn[:, c, kk * P:(kk + 1) * P],
                                                   gat[:, c, :], start=c == 0, stop=c == C - 1)
                    ins.then_inc(gath_done, 1)

            def slots_T(item):
                for c in range(C):
                    ins = nc.tensor.transpose(bank[7][:, c * P:(c + 1) * P], gat[:, c, :], ident[:])
                ins.then_inc(gatT_ps, 1)

            gather(0)
            slots_T(0)
            pe.wait_ge(cnt_sb, 1)
            gate_rows(3)
            nc.tensor.matmul(bank[6][0:1, 0:1], ones[:, 0:1], ones[:, 0:1], start=True, stop=True).then_inc(comb_ps, 1)

            def expert(i):
                pe.wait_ge(elo_done, i + 1)
                pe.wait_ge(gatT_sb, i + 1)
                for j in range(4):
                    if j == 0:
                        pe.wait_ge(silu_done, i * FBLK + base_of[1])
                    if j == 2:
                        pe.wait_ge(g_done, i * FBLK + base_of[1])
                    up(1, MOE0 + j, i * FBLK, j % 2, j // 2)
                with pe.Fori(0, FBLK - 1) as t:
                    for j in range(6):
                        if j == 0:
                            pe.wait_ge(silu_done, i * FBLK + t + (base_of[1] + 1))
                        if j == 2:
                            pe.wait_ge(g_done, i * FBLK + t + (base_of[1] + 1))
                        if j < 4:
                            up(1, MOE0 + 4 + j, i * FBLK + t, j % 2, j // 2)
                        if j == 1:
                            hidden_T(1, i * FBLK + t, 0)
                        if j == 4:
                            pe.wait_ge(gl_done, i * FBLK + t + (base_of[1] + 1))
                            pe.wait_ge(yzero, i * 2 + 2)
                        if j >= 4:
                            expert_down(t, MOE0 + 4 + j, i * FBLK + t, j - 4)
                pe.wait_ge(comb_add, i * 4 + 1)
                gather(i + 1)
                hidden_T(1, i * FBLK + (FBLK - 1), 0)
                pe.wait_ge(gl_done, i * FBLK + (base_of[1] + FBLK))
                for j in range(2):
                    expert_down(None, MOE0 + FFN_UNITS - 2 + j, i * FBLK, j, last=j == 1)
                pe.wait_ge(h32e_done, i * KC + 2 * KC)
                for c in range(C):
                    for half in range(2):
                        pe.wait_ge(ysb_done, i * 2 + half + 1)
                        if c:
                            pe.wait_ge(comb_add, i * 4 + (half + 1) + 1)
                        nc.tensor.matmul(bank[2 + half][:], gatT[:, c * P:(c + 1) * P],
                                         ysb[:, half * NB:(half + 1) * NB], start=True, stop=True)\
                            .then_inc(comb_ps, 1)
                slots_T(i + 1)

            with pe.Fori(0, E) as i:
                expert(i)
            pe.wait_ge(ctl_done, 1)
            over = pe.value_load(ctli[0:1, 1:2], min_val=0, max_val=EXTRA)
            with pe.If(over > 0):
                with pe.Fori(0, over) as i:
                    expert(i + E)


def _bucket_onehot():
    import numpy as np
    table = np.zeros((BUCKETS + 1, DIST), np.float32)
    exact = BUCKETS // 2
    for i in range(DIST):
        dist = S - 1 - i
        if dist < 0:
            table[BUCKETS, i] = 1
        elif dist < exact:
            table[dist, i] = 1
        else:
            large = exact + int(np.float32(np.log(np.float32(dist) / np.float32(exact)))
                                / np.float32(np.log(128 / exact)) * np.float32(BUCKETS - exact))
            table[min(large, BUCKETS - 1), i] = 1
    return table


_INS = ["x", "c", "w_mod", "b_mod", "g_mix_pre", "g_mix_post", "g_ffn_pre", "g_ffn_post", "w_in", "w_proj_sb",
        "w_proj_moba", "w_out", "rel_bias", "w1_dense", "w3_dense", "w2_dense", "w_router", "w1_moe", "w3_moe",
        "w2_moe"]


def kernel(**inputs):
    import numpy as np
    import concourse.bacc as bacc
    from concourse.bass_utils import run_bass_kernel_spmd as run

    nc = bacc.Bacc("TRN2", target_bir_lowering=False, num_devices=1)
    arrays = {f"in_{name}": np.ascontiguousarray(inputs[name]) for name in _INS}
    arrays["in_bucket_onehot"] = _bucket_onehot()
    args = [nc.dram_tensor(k, a.shape, mybir.dt.from_np(a.dtype), kind="ExternalInput").ap()
            for k, a in arrays.items()]
    scratch = nc.dram_tensor("dist_scratch", (HEADS, 384), F32, kind="Internal").ap()
    out = nc.dram_tensor("out_0", (1, S, D), F32, kind="ExternalOutput").ap()
    build(nc, *args, scratch, out)
    r = run(nc, [arrays], core_ids=[0])
    return r.results[0]["out_0"]
```

```python
from contextlib import ExitStack

import concourse.bass as bass
from concourse import mybir

F32 = mybir.dt.float32
F32R = mybir.dt.float32r
I32 = mybir.dt.int32
ALU = mybir.AluOpType
ACT = mybir.ActivationFunctionType
AX = mybir.AxisListType.X

P = 128
D = 1024
KC = D // P
S = 256
C = S // P
DH = 64
HEADS = 8
DEPTH = 2
NB = 512
UNIT = 2048
FF = 3584
FBLK = FF // NB
E = 8
EXTRA = 3
ITEMS = E + EXTRA
BUCKETS = 32
BLK = 10
MIX_UNITS = 28
FFN_UNITS = 6 * FBLK
RAW = 6
SPLIT = 3
LEAD = 2
MODS = 48
MOD_FIRST = 16
MOD_UNITS = 8
MRAW = 2
MOD_LAG = 4
EPS = 1e-6
NEG = -1e30
DIST = S + P - 1

MIX0 = 0
FFN0 = MIX0 + MIX_UNITS
MIX1 = FFN0 + FFN_UNITS
MOE0 = MIX1 + MIX_UNITS
FFN_BASE = [0, 2 * FBLK]


def build(nc, x_d, c_d, w_mod, b_mod, g_mix_pre, g_mix_post, g_ffn_pre, g_ffn_post, w_in, w_psb, w_pmo, w_out,
          rel_bias, w1_d, w3_d, w2_d, w_router, w1_m, w3_m, w2_m, onehot_d, dist_scratch, out_d):
    with ExitStack() as ctx:
        def sb(name, shape, dt=F32):
            return ctx.enter_context(nc.sbuf_tensor(name, shape, dt))

        def sem(name):
            return ctx.enter_context(nc.semaphore(name))

        raw = sb("raw", [P, RAW, UNIT])
        whi = sb("whi", [P, SPLIT, UNIT], F32R)
        wlo = sb("wlo", [P, SPLIT, UNIT], F32R)
        mraw = sb("mraw", [P, MRAW, KC, P])
        macc = sb("macc", [P, 2, P])
        x = sb("x", [P, C, D])
        hhi = sb("hhi", [P, KC, S], F32R)
        hlo = sb("hlo", [P, KC, S], F32R)
        ohi = sb("ohi", [P, KC, S], F32R)
        olo = sb("olo", [P, KC, S], F32R)
        wide = sb("wide", [P, 2 * C * D])
        gates = wide[:].rearrange("p (c n) -> p c n", c=C)
        xn = wide[:, 0:C * D].rearrange("p (c n) -> p c n", c=C)
        yacc = wide[:, C * D:2 * C * D].rearrange("p (c n) -> p c n", c=C)
        vals = sb("vals", [P, 2, C, NB])
        h32 = vals[:].rearrange("p b c n -> p (b c n)").rearrange("p (k t) -> p k t", k=KC)
        gat = vals[:, 1, 0, 0:S].rearrange("p (c s) -> p c s", c=C)
        gatT = vals[:, 1, 0, S:2 * S]
        h32e = vals[:, 0, :, :].rearrange("p c n -> p (c n)").rearrange("p (k t) -> p k t", k=KC)
        qk = sb("qk", [P, 4 * 4 * S])
        qkT = qk[:].rearrange("p (b c t) -> p b c t", b=4, c=4)
        merged = qk[:, 0:C * D].rearrange("p (c n) -> p c n", c=C)
        mtmp = qk[:, 2048:3072].rearrange("p (c n) -> p c n", c=C)
        hid = qk[:, 0:C * NB].rearrange("p (c n) -> p c n", c=C)
        silu = qk[:, C * NB:2 * C * NB].rearrange("p (c n) -> p c n", c=C)
        ysb = qk[:, 2048:3072]
        gdiag = qk[:, 3072:4096]
        bias = sb("bias", [P, HEADS, S])
        gate = sb("gate", [P, D])
        eb = sb("eb", [P, 2, 384])
        at = sb("at", [P, 2, 384])
        ident = sb("ident", [P, P])
        upper = sb("upper", [P, P])
        lower = sb("lower", [P, P])
        ones = sb("ones", [P, P])
        iota = sb("iota", [P, P])
        modT = sb("modT", [P, DEPTH * MODS])
        colsB = sb("colsB", [P, 72])
        colsM = sb("colsM", [P, DEPTH * MODS])
        cond = sb("cond", [P, KC])
        wr = sb("wr", [P, KC, E])
        ss = sb("ss", [P, 8])
        rstd = sb("rstd", [P, 8])
        nhalf = sb("nhalf", [P, 8])
        A = sb("A", [P, KC])
        gcol = sb("gcol", [P, KC])
        nmx = sb("nmx", [P, 4])
        rs = sb("rs", [P, 4])
        rt = at[:, 1, 0:192].rearrange("p (n c e) -> p n c e", n=12, c=C)
        ex = at[:, 0, 0:64].rearrange("p (n c e) -> p n c e", n=4, c=C)
        posI = sb("posI", [P, C, ITEMS + 1])
        wI = sb("wI", [P, C, ITEMS + 1])
        cur = sb("cur", [P, 2, C])
        ctl = sb("ctl", [P, 8])
        ctli = sb("ctli", [P, 8], I32)
        rowsM = qk[0:DEPTH * MODS, 2048:2048 + P]
        rowsB = qk[0:72, 2176:2176 + P]
        onehot = qk[0:BUCKETS + 1, 2304:2304 + DIST]
        relx = qk[0:BUCKETS + 1, 2690:2690 + HEADS]
        distb = qk[0:HEADS, 2700:2700 + 384]
        modrow = wide[0:1, C * D:2 * C * D]
        flip = eb[:, 0, 0:P]
        hank = qk[:, 0:HEADS * S].rearrange("p (h j) -> p h j", h=HEADS)

        bank = [ctx.enter_context(nc.psum_tensor(f"bank{i}", [P, NB], F32)) for i in range(8)]
        MODB = bank[7]

        def hidden_half(b):
            return slice(4 * (b % 2), 4 * (b % 2) + 4)

        raw_full = [sem(f"raw_full{i}") for i in range(RAW)]
        mraw_full = [sem(f"mraw_full{i}") for i in range(MRAW)]
        hi_done = sem("hi_done")
        lo_done = sem("lo_done")
        unit_used = sem("unit_used")
        mod_link = sem("mod_link")
        mod_acc = sem("mod_acc")
        mod_col = sem("mod_col")
        mod_evac = sem("mod_evac")
        mod_prod = sem("mod_prod")
        mod_unit = sem("mod_unit")
        mod_row = sem("mod_row")
        mod_first = sem("mod_first")
        cnt_sb = sem("cnt_sb")
        small_in = sem("small_in")
        x_in = sem("x_in")
        rel_in = sem("rel_in")
        hank_in = sem("hank_in")
        dist_out = sem("dist_out")
        x_out = sem("x_out")
        const = sem("const")
        relx_set = sem("relx_set")
        cols_ps = sem("cols_ps")
        cols_sb = sem("cols_sb")
        cond_done = sem("cond_done")
        dist_ps = sem("dist_ps")
        dist_sb = sem("dist_sb")
        flip_ps = sem("flip_ps")
        bias_sb = sem("bias_sb")
        dve_link = sem("dve_link")
        pool_link = sem("pool_link")
        sq_done = sem("sq_done")
        rstd_done = sem("rstd_done")
        xn_done = sem("xn_done")
        xT_done = sem("xT_done")
        ab_done = sem("ab_done")
        h32a = sem("h32a")
        h32b = sem("h32b")
        hhi_done = sem("hhi_done")
        hlo_done = sem("hlo_done")
        blk_evac = sem("blk_evac")
        z_done = sem("z_done")
        z_abs = sem("z_abs")
        z_relu = sem("z_relu")
        sb_exp1 = sem("sb_exp1")
        sb_ln = sem("sb_ln")
        sb_sum = sem("sb_sum")
        sb_lm = sem("sb_lm")
        arg_done = sem("arg_done")
        sb_att = sem("sb_att")
        mo_max = sem("mo_max")
        mo_exp = sem("mo_exp")
        mo_p = sem("mo_p")
        at_done = sem("at_done")
        pv_done = sem("pv_done")
        ohi_done = sem("ohi_done")
        olo_done = sem("olo_done")
        sig_done = sem("sig_done")
        mg_evac = sem("mg_evac")
        mT_done = sem("mT_done")
        mhi_done = sem("mhi_done")
        mlo_done = sem("mlo_done")
        gd_done = sem("gd_done")
        gps_done = sem("gps_done")
        gate_sb = sem("gate_sb")
        ysq_done = sem("ysq_done")
        ry_done = sem("ry_done")
        x_done = sem("x_done")
        silu_done = sem("silu_done")
        g_done = sem("g_done")
        gT_done = sem("gT_done")
        gh_done = sem("gh_done")
        gl_done = sem("gl_done")
        yp_done = sem("yp_done")
        yadd_done = sem("yadd_done")
        lg_done = sem("lg_done")
        rexp_in = sem("rexp_in")
        rexp = sem("rexp")
        mem_done = sem("mem_done")
        pos_done = sem("pos_done")
        ctl_done = sem("ctl_done")
        cur_done = sem("cur_done")
        gat_done = sem("gat_done")
        gath_done = sem("gath_done")
        h32e_done = sem("h32e_done")
        ehi_done = sem("ehi_done")
        elo_done = sem("elo_done")
        gatT_ps = sem("gatT_ps")
        gatT_sb = sem("gatT_sb")
        ysb_done = sem("ysb_done")
        yzero = sem("yzero")
        comb_ps = sem("comb_ps")
        comb_add = sem("comb_add")
        wcur_done = sem("wcur_done")
        yg_done = sem("yg_done")

        def dma_value(s, r):
            return 16 * ((s + MOD_UNITS) // RAW + 1) + r * 16

        def slot(s):
            return (s + MOD_UNITS) % RAW

        def number(s, r):
            return s + r * 6

        def wait_at_least(eng, semaphore, value):
            if not isinstance(value, int) or value > 0:
                eng.wait_ge(semaphore, value)

        def split_hi(act, s, r=0):
            act.wait_ge(raw_full[slot(s)], dma_value(s, r))
            wait_at_least(act, unit_used, number(s, r) - SPLIT + 1)
            nc.scalar.activation(whi[:, s % SPLIT, :], raw[:, slot(s), :], ACT.Copy).then_inc(hi_done, 1)

        def split_lo(dve, s, r=0):
            dve.wait_ge(hi_done, number(s, r) + 1)
            wait_at_least(dve, unit_used, number(s, r) - SPLIT + 1)
            nc.vector.tensor_tensor(wlo[:, s % SPLIT, :], raw[:, slot(s), :], whi[:, s % SPLIT, :].bitcast(F32),
                                    ALU.subtract).then_inc(lo_done, 1)

        def mod_product(dve, m, ms):
            dve.wait_ge(mraw_full[ms], 16 * ((m - MOD_FIRST) // MRAW + 1) if isinstance(m, int)
                        else m * (16 // MRAW) + (16 - (MOD_FIRST + ms) * (16 // MRAW)))
            nc.vector.tensor_tensor(mraw[:, ms, :, :], mraw[:, ms, :, :],
                                    cond[:].rearrange("p (k a) -> p k a", a=1).broadcast_to([P, KC, P]), ALU.mult)\
                .then_inc(mod_prod, 1)

        def mod_sum(pool, m, ms):
            pool.wait_ge(mod_prod, m - (MOD_FIRST - 1))
            nc.gpsimd.tensor_tensor(mraw[:, ms, 0:4, :], mraw[:, ms, 0:4, :], mraw[:, ms, 4:8, :], ALU.add)\
                .then_inc(mod_link, 1)
            pool.wait_ge(mod_link, m * 2 - (2 * MOD_FIRST - 1))
            nc.gpsimd.tensor_tensor(mraw[:, ms, 0:2, :], mraw[:, ms, 0:2, :], mraw[:, ms, 2:4, :], ALU.add)\
                .then_inc(mod_link, 1)
            pool.wait_ge(mod_link, m * 2 - (2 * MOD_FIRST - 2))
            wait_at_least(pool, mod_col, m - (MOD_FIRST + 1))
            nc.gpsimd.tensor_tensor(macc[:, ms, :], mraw[:, ms, 0, :], mraw[:, ms, 1, :], ALU.add)\
                .then_inc(mod_acc, 1)

        def mod_column(pe, m, ms):
            pe.wait_ge(mod_acc, m - (MOD_FIRST - 1))
            out = MODB[:, m:m + 1] if isinstance(m, int) else MODB[:, bass.ds(m, 1)]
            nc.tensor.matmul(out, macc[:, ms, :], ones[:, 0:1], start=True, stop=True).then_inc(mod_col, 1)

        def mod_take(dve, first, end, col_count):
            wait_at_least(dve, mod_col, col_count)
            nc.vector.tensor_copy(modT[:, first:end], MODB[:, first:end]).then_inc(mod_evac, 1)

        def mods_of_step(phase, u):
            if phase == 0:
                first = 16 + (2 * u if u < 4 else 4 + u)
                return list(range(first, first + (2 if u < 4 else 1)))
            return [90 + u] if u < 6 else []

        G_PRE = [0, 32, 8, 40]
        G_POST = [16, 48, 24, 56]
        C_COL = 64
        SH = [0, 24, 48, 72]
        SC = [8, 32, 56, 80]
        GT = [16, 40, 64, 88]

        GATE_BANK = [4, 4, 4, 0]

        block = ctx.enter_context(nc.Block())

        @block.sync
        def _(sp):
            def load_mix(l, u):
                if u < 20:
                    j, kh = divmod(u, 2)
                    return w_in[l, kh * 512:(kh + 1) * 512, j * NB:(j + 1) * NB].rearrange("(k p) n -> p k n", p=P)
                if u < 24:
                    w = w_psb if u < 22 else w_pmo
                    half = u % 2
                    return w[l, :, half * NB:(half + 1) * NB].rearrange("(k p) n -> p k n", p=P)
                half, kh = divmod(u - 24, 2)
                return w_out[l, kh * 512:(kh + 1) * 512, half * NB:(half + 1) * NB].rearrange("(k p) n -> p k n", p=P)

            def load_up(w, kh, b):
                cols = slice(b * NB, (b + 1) * NB) if isinstance(b, int) else bass.ds(b * NB, NB)
                return w.rearrange("(k p) n -> p k n", p=P)[:, kh * 4:kh * 4 + 4, cols]

            def load_down(w, part, b):
                rows = w.rearrange("(b q k p) n -> b q p k n", q=2, k=2, p=P)
                return rows[b, part]

            def load(s, r, src):
                if isinstance(s, int) and isinstance(r, int) and s + 6 * r < RAW:
                    wait_at_least(sp, mod_unit, s + MOD_UNITS - RAW + 1)
                wait_at_least(sp, lo_done, number(s, r) - RAW + 1)
                n = src.shape[-1]
                sp.dma_start(raw[:, slot(s), :].rearrange("p (k n) -> p k n", n=n), src)\
                    .then_inc(raw_full[slot(s)], 16)

            def load_mod(m, ms, l, col):
                wait_at_least(sp, mod_acc, m - (MOD_FIRST + MRAW - 1))
                cols = slice(col * P, col * P + P) if isinstance(col, int) else bass.ds(col * P, P)
                sp.dma_start(mraw[:, ms, :, :], w_mod[l].rearrange("(k p) n -> p k n", p=P)[:, :, cols])\
                    .then_inc(mraw_full[ms], 16)

            def ffn_unit(ws, b, j):
                if j < 4:
                    return load_up(ws[j // 2], j % 2, b)
                return load_down(ws[2], j - 4, b - 1)

            sp.dma_start(rowsM, b_mod.rearrange("l (m p) -> (l m) p", p=P)).then_inc(small_in, 16)
            for i, g in enumerate([g_mix_pre, g_mix_post, g_ffn_pre, g_ffn_post]):
                sp.dma_start(rowsB[16 * i:16 * i + 16, :], g.rearrange("l (m p) -> (l m) p", p=P))\
                    .then_inc(small_in, 16)
            sp.dma_start(rowsB[64:72, :], c_d.rearrange("b (m p) -> (b m) p", p=P)).then_inc(small_in, 16)
            sp.dma_start(x[:], x_d.rearrange("b (c p) n -> p (b c) n", p=P)).then_inc(x_in, 16)
            sp.dma_start(onehot, onehot_d).then_inc(rel_in, 16)
            sp.wait_ge(relx_set, 1)
            sp.dma_start(relx[0:BUCKETS, :], rel_bias).then_inc(rel_in, 16)
            sp.dma_start(wr[:], w_router[0].rearrange("(k p) e -> p k e", p=P)).then_inc(small_in, 16)
            for i in range(MOD_UNITS):
                cb, kh = divmod(i, 2)
                if i >= RAW:
                    sp.wait_ge(mod_unit, i - RAW + 1)
                sp.dma_start(raw[:, i % RAW, :].rearrange("p (k n) -> p k n", n=NB),
                             w_mod[0, kh * 512:(kh + 1) * 512, cb * NB:(cb + 1) * NB]
                             .rearrange("(k p) n -> p k n", p=P)).then_inc(raw_full[i % RAW], 16)
                if i == 3:
                    sp.wait_ge(dist_sb, 1)
                    sp.dma_start(dist_scratch[:, 0:DIST], distb[:, 0:DIST]).then_inc(dist_out, 16)
                    sp.wait_ge(dist_out, 16)
                    sp.dma_start(hank, bass.AP(dist_scratch.tensor, 0, [[1, P], [384, HEADS], [1, S]]))\
                        .then_inc(hank_in, 16)

            def phase_unit(n):
                if n < FFN0:
                    return load_mix(0, n)
                if n < MIX1:
                    u = n - FFN0
                    return ffn_unit(dense, 0, u) if u < 4 else ffn_unit(dense, FBLK, u - FFN_UNITS + 6)
                return load_mix(1, n - MIX1)

            dense = (w1_d[0], w3_d[0], w2_d[0])

            for s in range(LEAD):
                load(s, 0, phase_unit(s))
            for u in range(MIX_UNITS):
                load(u + LEAD, 0, phase_unit(u + LEAD))
                if u >= MOD_LAG:
                    for m in mods_of_step(0, u - MOD_LAG):
                        load_mod(m, m % MRAW, 0, m)
            for j in range(4):
                s = FFN0 + j + LEAD
                load(s, 0, ffn_unit(dense, 0, j + LEAD) if j + LEAD < 4 else ffn_unit(dense, 1, j + LEAD - 4))
                m = MODS + j - MOD_LAG
                load_mod(m, m % MRAW, 0, m)
            with sp.Fori(0, FBLK - 2) as t:
                for j in range(6):
                    jj = j + LEAD
                    src = ffn_unit(dense, t + 1, jj) if jj < 6 else ffn_unit(dense, t + 2, jj - 6)
                    load(FFN0 + 4 + jj, t, src)
                    load_mod(t * 6 + (MODS + 4 + j - MOD_LAG), j % MRAW, 1, t * 6 + (4 + j - MOD_LAG))
            for j in range(6):
                jj = j + LEAD
                src = ffn_unit(dense, FBLK - 1, jj) if jj < 6 else ffn_unit(dense, FBLK, jj - 2)
                load(FFN0 + 4 + jj + 6 * (FBLK - 2), 0, src)
                m = MODS + 4 + 6 * (FBLK - 2) + j - MOD_LAG
                load_mod(m, m % MRAW, 1, m - MODS)
            for j in range(2):
                load(MIX1 + j, 0, load_mix(1, j))
                m = MODS + 4 + 6 * (FBLK - 1) + j - MOD_LAG
                load_mod(m, m % MRAW, 1, m - MODS)
            for u in range(MIX_UNITS - LEAD):
                load(MIX1 + u + LEAD, 0, load_mix(1, u + LEAD))
                m = 90 + u - MOD_LAG
                if m < DEPTH * MODS:
                    load_mod(m, m % MRAW, 1, m - MODS)

            def load_expert(e, item):
                ws = (w1_m[0, e], w3_m[0, e], w2_m[0, e])
                for j in range(4):
                    load(MOE0 + j, item * FBLK, ffn_unit(ws, 0, j))
                with sp.Fori(0, FBLK - 1) as t:
                    for j in range(6):
                        load(MOE0 + 4 + j, item * FBLK + t, ffn_unit(ws, t + 1, j))
                for j in range(2):
                    load(MOE0 + FFN_UNITS - 2 + j, item * FBLK, load_down(ws[2], j, FBLK - 1))

            with sp.Fori(0, E) as e:
                load_expert(e, e)
            sp.wait_ge(ctl_done, 1)
            over = sp.value_load(ctli[0:1, 1:2], min_val=0, max_val=EXTRA)
            with sp.If(over > 0):
                with sp.Fori(0, over) as i:
                    e = sp.value_load(ctli[0:1, bass.ds(i + 2, 1)], min_val=0, max_val=E - 1)
                    load_expert(e, i + E)
            items = over + E
            for j in range(LEAD):
                load(MOE0 + j, items * FBLK, load_mix(0, j))
            for j in range(LEAD):
                sp.wait_ge(raw_full[slot(MOE0 + j)], dma_value(MOE0 + j, items * FBLK))
            for c in range(C):
                sp.wait_ge(x_done, 4 * 3 + 2 * (c + 1))
                sp.dma_start(out_d[0, c * P:(c + 1) * P, :], x[:, c, :]).then_inc(x_out, 16)
            sp.wait_ge(x_out, 32)

        @block.scalar
        def _(act):
            def squares_of_x(q):
                for c in range(C):
                    if q:
                        act.wait_ge(x_done, 4 * (q - 1) + 2 * c + 2)
                        act.wait_ge(rstd_done, C * q)
                        act.wait_ge(xT_done, 4 * q)
                        act.wait_ge(ysq_done, squares[0])
                    elif c == 0:
                        act.wait_ge(x_in, 16)
                    scr = h32[:].rearrange("p k t -> p (k t)")[:, c * D:(c + 1) * D]
                    nc.scalar.activation(scr, x[:, c, :], ACT.Square, accum_out=ss[:, c:c + 1]).then_inc(sq_done, 1)

            def norm(q):
                if q:
                    squares_of_x(q)
                act.wait_ge(ab_done, q + 1)
                act.wait_ge(sq_done, C * (q + 1))
                for c in range(C):
                    act.wait_ge(xT_done, 4 * q + 2 * c + 1)
                    for k in range(4):
                        nc.scalar.activation(h32[:, k, c * P:(c + 1) * P], bank[2 * c][:, k * P:(k + 1) * P],
                                             ACT.Identity, scale=A[:, k:k + 1],
                                             bias=modT[:, SH[q] + k:SH[q] + k + 1]).then_inc(h32a, 1)
                if q < 3:
                    act.wait_ge(h32a, KC * (q + 1))
                    nc.scalar.activation(hhi[:, 0:4, :], h32[:, 0:4, :], ACT.Copy).then_inc(hhi_done, 1)
                    act.wait_ge(h32b, KC * (q + 1))
                    nc.scalar.activation(hhi[:, 4:8, :], h32[:, 4:8, :], ACT.Copy).then_inc(hhi_done, 1)

            def mixer(l):
                base = MIX1 if l else MIX0

                def block_out(j):
                    act.wait_ge(unit_used, base + 2 * j + 2)
                    for i in range(2):
                        src = bank[2 * (j % 2) + i]
                        if j in (0, 1, 3, 4):
                            b = [0, 1, None, 2, 3][j]
                            nc.scalar.activation(qkT[:, b, 2 * i:2 * i + 2, :].rearrange("p c t -> p (c t)"), src[:],
                                                 ACT.Copy, scale=DH ** -0.5 if b % 2 == 0 else 1.0)\
                                .then_inc(blk_evac, 1)
                        elif j in (2, 5):
                            nc.scalar.activation(vals[:, j // 4, i, :], src[:], ACT.Copy).then_inc(blk_evac, 1)
                        else:
                            nc.scalar.activation(gates[:, i, (j - 6) * NB:(j - 5) * NB], src[:], ACT.Copy)\
                                .then_inc(blk_evac, 1)

                def after_scores(p):
                    if p < 4:
                        pair = 4 * l + p
                        act.wait_ge(z_abs, 2 * pair + 2)
                        nc.scalar.activation(eb[:], eb[:], ACT.Exp).then_inc(sb_exp1, 1)
                        act.wait_ge(sb_exp1, pair + 1)
                        nc.scalar.activation(eb[:], eb[:], ACT.Ln, bias=1.0).then_inc(sb_ln, 1)
                        return
                    for s in range(2):
                        nmo = 8 * l + 2 * (p - 4) + s
                        act.wait_ge(mo_max, 2 * (nmo + 1))
                        nc.scalar.activation(eb[:, s, 0:S], eb[:, s, 0:S], ACT.Exp, bias=nmx[:, 2 * s:2 * s + 1],
                                             accum_out=rs[:, 2 * s:2 * s + 1]).then_inc(mo_exp, 1)
                        nc.scalar.activation(eb[:, s, S:384], eb[:, s, S:384], ACT.Exp,
                                             bias=nmx[:, 2 * s + 1:2 * s + 2],
                                             accum_out=rs[:, 2 * s + 1:2 * s + 2]).then_inc(mo_exp, 1)

                def after_arg(p):
                    for s in range(2):
                        n = 16 * l + 2 * p + s
                        act.wait_ge(arg_done, n + 1)
                        if p < 4:
                            nc.scalar.activation(at[:, s, :], bank[4 + s][:, 0:384], ACT.Exp).then_inc(sb_att, 1)
                        else:
                            nc.scalar.activation(at[:, s, :], bank[4 + s][:, 0:384], ACT.Copy).then_inc(at_done, 1)

                def after_pv(p):
                    act.wait_ge(pv_done, 8 * l + p + 1)
                    nc.scalar.activation(ohi[:, p, :], bank[6][:, 0:S], ACT.Copy).then_inc(ohi_done, 1)

                for u in range(MIX_UNITS):
                    split_hi(act, base + u + LEAD)
                    if u < 20 and u % 2 == 1:
                        block_out(u // 2)
                    if 7 <= u < 23 and (u - 7) % 2 == 0:
                        after_pv((u - 7) // 2)
                    if 5 <= u < 21 and (u - 5) % 2 == 0:
                        after_scores((u - 5) // 2)
                    if 6 <= u < 22 and (u - 6) % 2 == 0:
                        after_arg((u - 6) // 2)
                    if u in (18, 21):
                        act.wait_ge(blk_evac, 2 * (BLK * l + (8 if u == 18 else 10)))
                        cols = slice(0, D) if u == 18 else slice(D, 2 * D)
                        for c in range(C):
                            nc.scalar.activation(gates[:, c, cols], gates[:, c, cols], ACT.Sigmoid)\
                                .then_inc(sig_done, 1)
                    if u == 23:
                        for i in range(4):
                            half, c = divmod(i, 2)
                            act.wait_ge(mT_done, 4 * l + i + 1)
                            nc.scalar.activation(hhi[:, 4 * half:4 * half + 4, c * P:(c + 1) * P],
                                                 bank[[2, 3, 6, 4][i]][:].rearrange("p (k t) -> p k t", k=4),
                                                 ACT.Copy).then_inc(mhi_done, 1)

            def out_squares(q):
                act.wait_ge(rstd_done, C * (q + 1))
                if q % 2 == 0:
                    for i in range(4):
                        half, c = divmod(i, 2)
                        act.wait_ge(unit_used, (MIX1 if q else MIX0) + 26 + 2 * half)
                        scr = eb[:].rearrange("p a n -> p (a n)")[:, 0:NB]
                        act.wait_ge(at_done, 16 * (q // 2 + 1))
                        if i:
                            act.wait_ge(ysq_done, squares[0])
                        squares[0] += 1
                        nc.scalar.activation(scr, bank[i][:], ACT.Square,
                                             accum_out=ss[:, 2 * c + half:2 * c + half + 1]).then_inc(ysq_done, 1)
                    return
                for c in range(C):
                    if q == 1:
                        act.wait_ge(yadd_done, 4 * FBLK + 4)
                    else:
                        act.wait_ge(comb_add, items4[0])
                    if c:
                        act.wait_ge(ysq_done, squares[0])
                    squares[0] += 1
                    nc.scalar.activation(h32[:].rearrange("p k t -> p (k t)")[:, 0:D] if q == 1 else gdiag,
                                         yacc[:, c, :], ACT.Square, accum_out=ss[:, c:c + 1]).then_inc(ysq_done, 1)

            squares = [0]
            items4 = [0]

            def ffn_silu(n, t, units):
                for c in range(n):
                    act.wait_ge(unit_used, units)
                    wait_at_least(act, g_done, t * n + base_of[n])
                    nc.scalar.activation(silu[:, c, :], bank[c][:], ACT.Silu).then_inc(silu_done, 1)

            def ffn_ghi(n, t, c, half):
                act.wait_ge(gT_done, t * n + (base_of[n] + c + 1))
                nc.scalar.activation(ohi[:, half, c * P:(c + 1) * P], bank[6][:].rearrange("p (k t) -> p k t", k=4),
                                     ACT.Copy).then_inc(gh_done, 1)

            base_of = {2: FFN_BASE[0], 1: FFN_BASE[1]}

            act.wait_ge(cols_sb, 2)
            nc.scalar.activation(cond[:], colsB[:, C_COL:C_COL + KC], ACT.Silu).then_inc(cond_done, 1)
            squares_of_x(0)
            for cb in range(4):
                act.wait_ge(mod_unit, 2 * cb + 2)
                nc.scalar.activation(modrow[:, cb * NB:(cb + 1) * NB], bank[6 + cb % 2][0:1, :], ACT.Copy)\
                    .then_inc(mod_row, 1)
            for s in range(LEAD):
                split_hi(act, s)
            norm(0)
            mixer(0)
            out_squares(0)
            norm(1)
            for j in range(4):
                split_hi(act, FFN0 + j + LEAD)
                if j == 1:
                    ffn_silu(2, 0, FFN0 + 2)
            for c in range(C):
                ffn_ghi(2, 0, c, hidden_half(0))

            def block_steps(n, s0, r, t, half):
                for j in range(6):
                    if j == 5:
                        ffn_ghi(n, t, 0, half)
                    split_hi(act, s0 + j + LEAD, r)
                    if j == 1:
                        ffn_silu(n, t, number(s0, r) + 2)
                    if j == 5 and n == 2:
                        ffn_ghi(n, t, 1, half)

            with act.Fori(0, (FBLK - 1) // 2) as tt:
                for q in range(2):
                    block_steps(2, FFN0 + 4 + 6 * q, tt * 2, tt * 2 + (q + 1), hidden_half(q + 1))
            for j in range(2):
                split_hi(act, MIX1 + j)
            out_squares(1)
            norm(2)
            mixer(1)
            out_squares(2)
            norm(3)
            act.wait_ge(rexp_in, 1)
            nc.scalar.activation(rt[:, 9, :, 0], rt[:, 8, :, 0], ACT.Exp).then_inc(rexp, 1)

            def expert_tokens(item, half):
                wait_at_least(act, elo_done, item)
                act.wait_ge(gath_done, item * 2 + (half + 1))
                for k in range(4 * half, 4 * half + 4):
                    src = bank[2 + half][:, (k % 4) * P:(k % 4 + 1) * P]
                    nc.scalar.activation(h32e[:, k, :], src, ACT.Identity, scale=A[:, k:k + 1],
                                         bias=modT[:, SH[3] + k:SH[3] + k + 1]).then_inc(h32e_done, 1)

            def expert_hi(item):
                act.wait_ge(h32e_done, item * KC + KC)
                nc.scalar.activation(hhi[:, :, 0:P], h32e[:], ACT.Copy).then_inc(ehi_done, 1)

            act.wait_ge(lg_done, 1)
            for half in range(2):
                expert_tokens(0, half)
            expert_hi(0)

            zeros = ones[:].rearrange("p (a n) -> p a n", a=1).broadcast_to([P, 4, P])

            def clear_sums():
                for half in range(2):
                    nc.scalar.activation(bank[4 + half][:].rearrange("p (a n) -> p a n", a=4), zeros, ACT.Copy,
                                         scale=0.0).then_inc(yzero, 1)

            act.wait_ge(cnt_sb, 1)
            clear_sums()

            def expert(i):
                for j in range(4):
                    split_hi(act, MOE0 + j + LEAD, i * FBLK)
                    if j == 1:
                        ffn_silu(1, i * FBLK, i * FFN_UNITS + (MOE0 + 2))
                expert_tokens(i + 1, 0)
                ffn_ghi(1, i * FBLK, 0, hidden_half(0))
                expert_tokens(i + 1, 1)
                with act.Fori(0, (FBLK - 1) // 2) as tt:
                    for q in range(2):
                        block_steps(1, MOE0 + 4 + 6 * q, i * FBLK + tt * 2, i * FBLK + tt * 2 + (q + 1),
                                    hidden_half(q + 1))
                act.wait_ge(unit_used, i * FFN_UNITS + (MOE0 + FFN_UNITS - 4))
                expert_hi(i + 1)
                for j in range(2):
                    split_hi(act, MOE0 + FFN_UNITS + j, i * FBLK)
                act.wait_ge(unit_used, i * FFN_UNITS + (MOE0 + FFN_UNITS))
                act.wait_ge(comb_ps, i * 4 + 4)
                for half in range(2):
                    nc.scalar.activation(ysb[:, half * NB:(half + 1) * NB], bank[4 + half][:], ACT.Copy)\
                        .then_inc(ysb_done, 1)
                act.wait_ge(ysb_done, i * 2 + 4)
                clear_sums()

            with act.Fori(0, E) as i:
                expert(i)
            act.wait_ge(ctl_done, 1)
            over = act.value_load(ctli[0:1, 1:2], min_val=0, max_val=EXTRA)
            with act.If(over > 0):
                with act.Fori(0, over) as i:
                    expert(i + E)
            items4[0] = (over + E) * 4 + 5
            out_squares(3)

        @block.vector
        def _(dve):
            links = [0]

            def link(ins):
                links[0] += 1
                ins.then_inc(dve_link, 1)
                dve.wait_ge(dve_link, links[0])

            def normed(q):
                for c in range(C):
                    dve.wait_ge(rstd_done, C * q + c + 1)
                    nc.vector.tensor_scalar(xn[:, c, :], x[:, c, :], rstd[:, c:c + 1], None, ALU.mult)\
                        .then_inc(xn_done, 1)

            def norm(q):
                link(nc.vector.tensor_tensor(modT[:, SH[q]:SH[q] + 16], modT[:, SH[q]:SH[q] + 16],
                                             colsM[:, SH[q]:SH[q] + 16], ALU.add))
                nc.vector.scalar_tensor_tensor(A[:], modT[:, SC[q]:SC[q] + KC], 1.0,
                                               colsB[:, G_PRE[q]:G_PRE[q] + KC], ALU.add, ALU.mult)\
                    .then_inc(ab_done, 1)
                if q:
                    normed(q)
                dve.wait_ge(sq_done, C * (q + 1))
                dve.wait_ge(ab_done, q + 1)
                for c in range(C):
                    dve.wait_ge(xT_done, 4 * q + 2 * c + 2)
                    for k in range(4, KC):
                        nc.vector.tensor_scalar(h32[:, k, c * P:(c + 1) * P],
                                                bank[2 * c + 1][:, (k - 4) * P:(k - 3) * P], A[:, k:k + 1],
                                                modT[:, SH[q] + k:SH[q] + k + 1], ALU.mult, ALU.add)\
                            .then_inc(h32b, 1)
                if q < 3:
                    for half in range(2):
                        ks = slice(4 * half, 4 * half + 4)
                        dve.wait_ge(hhi_done, 2 * q + half + 1)
                        if half:
                            dve.wait_ge(h32b, KC * (q + 1))
                        nc.vector.tensor_tensor(hlo[:, ks, :], h32[:, ks, :], hhi[:, ks, :].bitcast(F32),
                                                ALU.subtract).then_inc(hlo_done, 1)

            def gate_diag(q):
                link(nc.vector.tensor_tensor(gcol[:], modT[:, GT[q]:GT[q] + KC], colsM[:, GT[q]:GT[q] + KC], ALU.add))
                link(nc.vector.tensor_tensor(gcol[:], gcol[:], colsB[:, G_POST[q]:G_POST[q] + KC], ALU.mult))
                for k in range(KC):
                    nc.vector.tensor_scalar(gdiag[:, k * P:(k + 1) * P], ident[:], gcol[:, k:k + 1], None, ALU.mult)\
                        .then_inc(gd_done, 1)

            def gate_take(q):
                for half in range(2):
                    dve.wait_ge(gps_done, 2 * q + half + 1)
                    nc.vector.tensor_copy(gate[:, half * NB:(half + 1) * NB], bank[GATE_BANK[q] + half][:])\
                        .then_inc(gate_sb, 1)

            def residual(q):
                dve.wait_ge(gate_sb, 2 * (q + 1))
                for i in range(4):
                    half, c = divmod(i, 2) if q % 2 == 0 else (i % 2, i // 2)
                    cols = slice(half * NB, (half + 1) * NB)
                    if q % 2 == 0:
                        dve.wait_ge(ysq_done, [0, None, 6][q] + i + 1)
                    src = bank[i][:] if q % 2 == 0 else yacc[:, c, cols]
                    nc.vector.tensor_tensor(merged[:, c, cols], src, gate[:, cols], ALU.mult).then_inc(yg_done, 1)
                dve.wait_ge(yg_done, 4 * q + 4)
                for c in range(C):
                    dve.wait_ge(ry_done, C * q + c + 1)
                    for half in range(2):
                        cols = slice(half * NB, (half + 1) * NB)
                        nc.vector.scalar_tensor_tensor(x[:, c, cols], merged[:, c, cols], rstd[:, 4 + c:5 + c],
                                                       x[:, c, cols], ALU.mult, ALU.add).then_inc(x_done, 1)
                dve.wait_ge(x_done, 4 * q + 4)

            def mixer(l):
                base = MIX1 if l else MIX0
                q = 2 * l

                def after_scores(p):
                    if p < 4:
                        for s in range(2):
                            dve.wait_ge(z_done, 16 * l + 2 * p + s + 1)
                            nc.vector.tensor_scalar(at[:, s, :], bank[4 + s][:, 0:384], 0.0, None, ALU.max)\
                                .then_inc(z_relu, 1)
                    for s in range(2):
                        z = bank[4 + s]
                        if p < 4:
                            dve.wait_ge(z_relu, 8 * l + 2 * p + s + 1)
                            nc.vector.scalar_tensor_tensor(eb[:, s, :], at[:, s, :], -2.0, z[:, 0:384], ALU.mult,
                                                           ALU.add).then_inc(z_abs, 1)
                        else:
                            h = 2 * (p - 4) + s
                            dve.wait_ge(z_done, 16 * l + 2 * p + s + 1)
                            links[0] += 2
                            nc.vector.tensor_tensor(eb[:, s, 0:S], z[:, 0:S], bias[:, h, :], ALU.add)\
                                .then_inc(dve_link, 1)
                            nc.vector.tensor_tensor(eb[:, s, S:384], z[:, S:384], bias[:, h, P:S], ALU.add)\
                                .then_inc(dve_link, 1)
                            dve.wait_ge(dve_link, links[0])
                            nc.vector.tensor_reduce(nmx[:, 2 * s:2 * s + 1], eb[:, s, 0:S], AX, ALU.max, negate=True)\
                                .then_inc(mo_max, 1)
                            nc.vector.tensor_reduce(nmx[:, 2 * s + 1:2 * s + 2], eb[:, s, S:384], AX, ALU.max,
                                                    negate=True).then_inc(mo_max, 1)
                    for s in range(2):
                        if p < 4:
                            nsb = 8 * l + 2 * p + s
                            dve.wait_ge(sb_ln, 4 * l + p + 1)
                            dve.wait_ge(z_relu, nsb + 1)
                            nc.vector.scalar_tensor_tensor(at[:, s, :], eb[:, s, :], -1.0, at[:, s, :], ALU.mult,
                                                           ALU.subtract).then_inc(sb_sum, 1)
                        else:
                            nmo = 8 * l + 2 * (p - 4) + s
                            dve.wait_ge(mo_exp, 2 * (nmo + 1))
                            link(nc.vector.reciprocal(rs[:, 2 * s:2 * s + 2], rs[:, 2 * s:2 * s + 2]))
                            nc.vector.tensor_scalar(eb[:, s, 0:S], eb[:, s, 0:S], rs[:, 2 * s:2 * s + 1], None,
                                                    ALU.mult).then_inc(mo_p, 1)
                            nc.vector.tensor_scalar(eb[:, s, S:384], eb[:, s, S:384], rs[:, 2 * s + 1:2 * s + 2],
                                                    None, ALU.mult).then_inc(mo_p, 1)

                def after_pv(p):
                    dve.wait_ge(ohi_done, 8 * l + p + 1)
                    nc.vector.tensor_tensor(olo[:, p, :], bank[6][:, 0:S], ohi[:, p, :].bitcast(F32), ALU.subtract)\
                        .then_inc(olo_done, 1)

                for u in range(MIX_UNITS):
                    split_lo(dve, base + u + LEAD)
                    for m in mods_of_step(l, u):
                        mod_product(dve, m, m % MRAW)
                    if 7 <= u < 23 and (u - 7) % 2 == 0:
                        after_pv((u - 7) // 2)
                    if 5 <= u < 21 and (u - 5) % 2 == 0:
                        after_scores((u - 5) // 2)
                    if u == 22:
                        first, end = [(MOD_FIRST, 42), (87, 96)][l]
                        mod_take(dve, first, end, end - MOD_FIRST)
                        dve.wait_ge(mod_evac, [2, 5][l])
                    if 20 <= u < 22:
                        half = u - 20
                        dve.wait_ge(sig_done, 2 * C * l + C)
                        for c in range(C):
                            dve.wait_ge(unit_used, base + u + 1)
                            nc.vector.tensor_tensor(merged[:, c, half * NB:(half + 1) * NB], bank[2 * half + c][:],
                                                    gates[:, c, half * NB:(half + 1) * NB], ALU.mult)\
                                .then_inc(mg_evac, 1)
                    if 22 <= u < 24:
                        half = u - 22
                        dve.wait_ge(sig_done, 2 * C * (l + 1))
                        for c in range(C):
                            dve.wait_ge(unit_used, base + u + 1)
                            link(nc.vector.tensor_tensor(mtmp[:, c, :], bank[(4 if half == 0 else 0) + c][:],
                                                         gates[:, c, D + half * NB:D + (half + 1) * NB], ALU.mult))
                            dve.wait_ge(mg_evac, 8 * l + 2 * half + c + 1)
                            cols = slice(half * NB, (half + 1) * NB)
                            nc.vector.tensor_tensor(merged[:, c, cols], merged[:, c, cols], mtmp[:, c, :], ALU.add)\
                                .then_inc(mg_evac, 1)
                    if u == 23:
                        for i in range(4):
                            half, c = divmod(i, 2)
                            dve.wait_ge(mhi_done, 4 * l + i + 1)
                            nc.vector.tensor_tensor(hlo[:, 4 * half:4 * half + 4, c * P:(c + 1) * P],
                                                    bank[[2, 3, 6, 4][i]][:].rearrange("p (k t) -> p k t", k=4),
                                                    hhi[:, 4 * half:4 * half + 4, c * P:(c + 1) * P].bitcast(F32),
                                                    ALU.subtract).then_inc(mlo_done, 1)
                        gate_diag(q)
                    if u == 25:
                        gate_take(q)

            def ffn_g(n, t, units):
                for c in range(n):
                    dve.wait_ge(unit_used, units)
                    dve.wait_ge(silu_done, t * n + (base_of[n] + c + 1))
                    wait_at_least(dve, gT_done, t * n + base_of[n])
                    nc.vector.tensor_tensor(hid[:, c, :], silu[:, c, :], bank[(2 if n == 2 else 1) + c][:], ALU.mult)\
                        .then_inc(g_done, 1)

            def ffn_glo(n, t, c, half):
                dve.wait_ge(gh_done, t * n + (base_of[n] + c + 1))
                nc.vector.tensor_tensor(olo[:, half, c * P:(c + 1) * P], bank[6][:].rearrange("p (k t) -> p k t", k=4),
                                        ohi[:, half, c * P:(c + 1) * P].bitcast(F32), ALU.subtract)\
                    .then_inc(gl_done, 1)

            def dense_add(t, c, units):
                for half in range(2):
                    if c == 1 or half == 0:
                        dve.wait_ge(yp_done, t * 3 + (1 + half if c else 3))
                    else:
                        dve.wait_ge(unit_used, units)
                    dve.wait_ge(yadd_done, t * 4 + 4)
                    cols = slice(half * NB, (half + 1) * NB)
                    nc.vector.tensor_tensor(yacc[:, c, cols], yacc[:, c, cols], bank[(0 if c else 4) + half][:],
                                            ALU.add).then_inc(yadd_done, 1)

            base_of = {2: FFN_BASE[0], 1: FFN_BASE[1]}

            nc.vector.memset(ones[:], 1.0).then_inc(const, 1)
            nc.vector.memset(posI[:], -1.0).then_inc(const, 1)
            nc.vector.memset(wI[:], 0.0).then_inc(const, 1)
            dve.wait_ge(cols_ps, 2)
            nc.vector.tensor_copy(colsM[:], bank[4][:, 0:DEPTH * MODS]).then_inc(cols_sb, 1)
            nc.vector.tensor_copy(colsB[:], bank[4][:, P:P + 72]).then_inc(cols_sb, 1)
            dve.wait_ge(dist_ps, 1)
            nc.vector.tensor_copy(distb[:, 0:DIST], bank[5][0:HEADS, 0:DIST]).then_inc(dist_sb, 1)
            dve.wait_ge(cond_done, 1)
            normed(0)
            for i in range(4):
                dve.wait_ge(flip_ps, i + 1)
                nc.vector.tensor_copy(bias[:, 2 * i:2 * i + 2, :].rearrange("p h j -> p (h j)"), bank[4 + i % 2][:])\
                    .then_inc(bias_sb, 1)
            dve.wait_ge(mod_first, 1)
            mod_take(dve, 0, MOD_FIRST, 0)
            dve.wait_ge(mod_evac, 1)
            for s in range(LEAD):
                split_lo(dve, s)
            norm(0)
            mixer(0)
            residual(0)
            norm(1)
            mod_take(dve, 42, MODS, MODS - MOD_FIRST)
            dve.wait_ge(mod_evac, 3)
            gate_diag(1)
            for j in range(4):
                split_lo(dve, FFN0 + j + LEAD)
                mod_product(dve, MODS + j, j % MRAW)
                if j == 3:
                    gate_take(1)
                    ffn_g(2, 0, FFN0 + 4)
            for c in range(C):
                ffn_glo(2, 0, c, hidden_half(0))
            with dve.Fori(0, (FBLK - 1) // 2) as tt:
                for q in range(2):
                    s0 = FFN0 + 4 + 6 * q
                    t = tt * 2 + q
                    for j in range(6):
                        split_lo(dve, s0 + j + LEAD, tt * 2)
                        if j >= 4:
                            ffn_glo(2, t + 1, j - 4, hidden_half(q + 1))
                        if j == 5:
                            dense_add(t, 1, None)
                        mod_product(dve, tt * 12 + (MODS + 4 + 6 * q + j), j % MRAW)
                        if j == 3:
                            ffn_g(2, t + 1, tt * 12 + (s0 + 4))
                    dense_add(t, 0, tt * 12 + (s0 + 6))
            split_lo(dve, MIX1)
            mod_product(dve, 88, 0)
            for c in (1, 0):
                dense_add(FBLK - 1, c, MIX1)
            mod_take(dve, MODS, 87, 87 - MOD_FIRST)
            dve.wait_ge(mod_evac, 4)
            residual(1)
            norm(2)
            split_lo(dve, MIX1 + 1)
            mod_product(dve, 89, 1)
            mixer(1)
            residual(2)
            norm(3)
            gate_diag(3)

            lg, cand, oh1, oh2, t5, pos, comb, mem = (rt[:, i, :, :] for i in range(8))
            m1, m2, i1, w1, w2 = (rt[:, 10, :, i:i + 1] for i in range(5))
            dlt = rt[:, 8, :, 0:1]
            ex = rt[:, 9, :, 0:1]
            cnt = rt[:, 11, 0, :]

            def wide8(v):
                return v.broadcast_to([P, C, E])

            iota8 = iota[:, 0:E].rearrange("p (a e) -> p a e", a=1).broadcast_to([P, C, E])

            def first_of_largest(values, top, onehot_out):
                link(nc.vector.tensor_reduce(top, values, AX, ALU.max))
                link(nc.vector.tensor_tensor(cand, values, wide8(top), ALU.is_lt))
                link(nc.vector.tensor_scalar(cand, cand, 100.0, None, ALU.mult))
                link(nc.vector.tensor_tensor(cand, cand, iota8, ALU.add))
                link(nc.vector.tensor_reduce(i1, cand, AX, ALU.min))
                link(nc.vector.tensor_tensor(onehot_out, iota8, wide8(i1), ALU.is_equal))

            dve.wait_ge(lg_done, 1)
            link(nc.vector.tensor_copy(lg, bank[4][:, 0:C * E].rearrange("p (c e) -> p c e", c=C)))
            first_of_largest(lg, m1, oh1)
            link(nc.vector.tensor_scalar(t5, oh1, NEG, None, ALU.mult))
            link(nc.vector.tensor_tensor(t5, t5, lg, ALU.add))
            first_of_largest(t5, m2, oh2)
            nc.vector.tensor_tensor(dlt, m2, m1, ALU.subtract).then_inc(rexp_in, 1)
            nc.vector.tensor_tensor(mem, oh1, oh2, ALU.add).then_inc(mem_done, 1)
            dve.wait_ge(rexp, 1)
            link(nc.vector.tensor_scalar(w1, ex, 1.0, None, ALU.add))
            link(nc.vector.reciprocal(w1, w1))
            link(nc.vector.tensor_tensor(w2, ex, w1, ALU.mult))
            link(nc.vector.tensor_tensor(comb, oh1, wide8(w1), ALU.mult))
            link(nc.vector.tensor_tensor(t5, oh2, wide8(w2), ALU.mult))
            link(nc.vector.tensor_tensor(comb, comb, t5, ALU.add))
            link(nc.vector.tensor_copy(wI[:, :, 1:E + 1], comb))
            dve.wait_ge(pos_done, 1)
            link(nc.vector.tensor_scalar(pos, bank[5][:, 0:C * E].rearrange("p (c e) -> p c e", c=C), 1.0, None,
                                         ALU.add))
            link(nc.vector.tensor_tensor(pos, pos, mem, ALU.mult))
            link(nc.vector.tensor_scalar(pos, pos, -1.0, None, ALU.add))
            link(nc.vector.tensor_copy(posI[:, :, 0:E], pos))
            nc.vector.tensor_copy(cnt, bank[5][:, C * E:C * E + E]).then_inc(cnt_sb, 1)

            def expert_slots(item):
                col = slice(item, item + 1) if isinstance(item, int) else bass.ds(item, 1)
                nc.vector.tensor_copy(cur[:, 0, :], posI[:, :, col].rearrange("p c o -> p (c o)")).then_inc(cur_done, 1)
                dve.wait_ge(cur_done, item + 1)
                for c in range(C):
                    nc.vector.tensor_scalar(gat[:, c, :], iota[:], cur[:, 0, c:c + 1], None, ALU.is_equal)\
                        .then_inc(gat_done, 1)

            def expert_lo(item):
                dve.wait_ge(ehi_done, item + 1)
                nc.vector.tensor_tensor(hlo[:, :, 0:P], h32e[:], hhi[:, :, 0:P].bitcast(F32), ALU.subtract)\
                    .then_inc(elo_done, 1)

            dve.wait_ge(lg_done, 1)
            expert_slots(0)
            gate_take(3)
            expert_lo(0)

            def combine(i, c):
                dve.wait_ge(wcur_done, i + 1)
                dve.wait_ge(comb_add, i * 4 + 1)
                for half in range(2):
                    dve.wait_ge(comb_ps, i * 4 + (2 * c + half + 1))
                    cols = slice(half * NB, (half + 1) * NB)
                    nc.vector.scalar_tensor_tensor(yacc[:, c, cols], bank[2 + half][:], cur[:, 1, c:c + 1],
                                                   yacc[:, c, cols], ALU.mult, ALU.add).then_inc(comb_add, 1)

            def expert(i):
                for j in range(4):
                    if j == 3:
                        dve.wait_ge(gatT_ps, i + 1)
                        dve.wait_ge(ctl_done, 1)
                        expert_slots(i + 1)
                        nc.vector.tensor_copy(gatT, bank[7][:, 0:S]).then_inc(gatT_sb, 1)
                    split_lo(dve, MOE0 + j + LEAD, i * FBLK)
                    if j < 2:
                        combine(i, j)
                    if j == 3:
                        ffn_g(1, i * FBLK, i * FFN_UNITS + (MOE0 + 4))
                        ffn_glo(1, i * FBLK, 0, hidden_half(0))
                with dve.Fori(0, (FBLK - 1) // 2) as tt:
                    for q in range(2):
                        s0 = MOE0 + 4 + 6 * q
                        t = i * FBLK + tt * 2 + q
                        for j in range(6):
                            if j == 5:
                                ffn_glo(1, t + 1, 0, hidden_half(q + 1))
                            split_lo(dve, s0 + j + LEAD, i * FBLK + tt * 2)
                            if j == 3:
                                ffn_g(1, t + 1, i * FFN_UNITS + tt * 12 + (s0 + 4))
                expert_lo(i + 1)
                for j in range(2):
                    split_lo(dve, MOE0 + FFN_UNITS + j, i * FBLK)

            with dve.Fori(0, E) as i:
                expert(i)
            over = dve.value_load(ctli[0:1, 1:2], min_val=0, max_val=EXTRA)
            with dve.If(over > 0):
                with dve.Fori(0, over) as i:
                    expert(i + E)
            for c in range(C):
                combine(over + E, c)
            dve.wait_ge(comb_add, (over + E) * 4 + 5)
            residual(3)

        @block.gpsimd
        def _(pool):
            links = [0]

            def link(ins):
                links[0] += 1
                ins.then_inc(pool_link, 1)
                pool.wait_ge(pool_link, links[0])

            nc.gpsimd.memset(relx, NEG).then_inc(relx_set, 1)
            nc.gpsimd.iota(iota[:], pattern=[[1, P]], base=0, channel_multiplier=0,
                           allow_small_or_imprecise_dtypes=True).then_inc(const, 1)
            for tile in (ident, upper, lower):
                nc.gpsimd.memset(tile[:], 0.0 if tile is ident else 1.0).then_inc(pool_link, 1)
                links[0] += 1
            nc.gpsimd.memset(flip, 0.0).then_inc(pool_link, 1)
            nc.gpsimd.memset(nhalf[:], -0.5).then_inc(pool_link, 1)
            links[0] += 2
            pool.wait_ge(pool_link, links[0])

            def select(tile, op, step, channel, base, fill):
                return nc.gpsimd.affine_select(out=tile, in_=tile, compare_op=op, fill=fill, base=base,
                                               pattern=[[step, P]], channel_multiplier=channel)

            select(ident[:], ALU.not_equal, -1, 1, 0, 1.0).then_inc(const, 1)
            select(upper[:], ALU.is_gt, 1, -1, 0, 0.0).then_inc(const, 1)
            select(lower[:], ALU.is_ge, -1, 1, 0, 0.0).then_inc(const, 1)
            select(flip, ALU.not_equal, 1, 1, -(P - 1), 1.0).then_inc(const, 1)

            def inv_rms(done, wait_sem, wait_val, col, parts, at_col):
                pool.wait_ge(wait_sem, wait_val)
                src = ss[:, col:col + 1]
                if parts == 2:
                    link(nc.gpsimd.tensor_tensor(src, src, ss[:, col + 1:col + 2], ALU.add))
                link(nc.gpsimd.tensor_scalar(src, src, 1.0 / D, EPS, ALU.mult, ALU.add))
                nc.gpsimd.tensor_tensor(rstd[:, at_col:at_col + 1], src, nhalf[:, 0:1], ALU.pow).then_inc(done, 1)

            def norm(q):
                for c in range(C):
                    if q:
                        pool.wait_ge(xn_done, C * q)
                    inv_rms(rstd_done, sq_done, C * q + c + 1, c, 1, c)

            def after(q, count):
                for c in range(C):
                    if q:
                        pool.wait_ge(x_done, 4 * q)
                    if q % 2 == 0:
                        inv_rms(ry_done, ysq_done, count + c + 3, 2 * c, 2, 4 + c)
                    else:
                        inv_rms(ry_done, ysq_done, count + c + 1, c, 1, 4 + c)

            def keep_earlier(s, fill_done):
                select(at[:, s, 0:P], ALU.is_gt, 1, -1, 0, 0.0)
                select(at[:, s, S:384], ALU.is_gt, 1, -1, 0, 0.0).then_inc(fill_done, 1)

            def mixer(l):
                for u in range(MIX_UNITS):
                    if l or u < MIX_UNITS - 1:
                        for m in mods_of_step(l, u):
                            mod_sum(pool, m, m % MRAW)
                    if 5 <= u < 13:
                        p = (u - 5) // 2
                        for s in range(2):
                            if u % 2:
                                pool.wait_ge(sb_sum, 8 * l + 2 * p + s + 1)
                                keep_earlier(s, sb_lm)
                            else:
                                pool.wait_ge(sb_att, 8 * l + 2 * p + s + 1)
                                keep_earlier(s, at_done)

            def extra_items():
                pos, comb = rt[:, 5, :, :], rt[:, 6, :, :]
                cnt, pre = ex[:, 0, 0, :], ex[:, 0, 1, :]
                sel = ex[:, 1, 0, :]
                iota8 = iota[:, 0:E]
                a, b = ex[:, 2, :, :], ex[:, 3, :, :]

                def total(out, v):
                    link(nc.gpsimd.tensor_tensor(v[:, :, 0:4], v[:, :, 0:4], v[:, :, 4:8], ALU.add))
                    link(nc.gpsimd.tensor_tensor(v[:, :, 0:2], v[:, :, 0:2], v[:, :, 2:4], ALU.add))
                    link(nc.gpsimd.tensor_tensor(out, v[:, :, 0:1], v[:, :, 1:2], ALU.add))

                pool.wait_ge(cnt_sb, 1)
                link(nc.gpsimd.tensor_scalar(cnt, rt[:, 11, 0, :], float(P), None, ALU.is_gt))
                link(nc.gpsimd.memset(pre[:, 0:1], 0.0))
                for e in range(1, E):
                    link(nc.gpsimd.tensor_tensor(pre[:, e:e + 1], pre[:, e - 1:e], cnt[:, e - 1:e], ALU.add))
                link(nc.gpsimd.tensor_tensor(ctl[:, 1:2], pre[:, E - 1:E], cnt[:, E - 1:E], ALU.add))
                for i in range(EXTRA):
                    link(nc.gpsimd.tensor_scalar(sel, pre, float(i), None, ALU.is_equal))
                    link(nc.gpsimd.tensor_tensor(sel, sel, cnt, ALU.mult))
                    for c in range(C):
                        link(nc.gpsimd.tensor_tensor(a[:, c, :], pos[:, c, :], sel, ALU.mult))
                        link(nc.gpsimd.tensor_tensor(b[:, c, :], comb[:, c, :], sel, ALU.mult))
                    total(posI[:, :, E + i:E + i + 1], a)
                    link(nc.gpsimd.tensor_scalar(posI[:, :, E + i], posI[:, :, E + i], -float(P), None, ALU.add))
                    total(wI[:, :, E + 1 + i:E + 2 + i], b)
                    link(nc.gpsimd.tensor_tensor(a[:, 0, :], sel, iota8, ALU.mult))
                    total(ctl[:, 2 + i:3 + i].rearrange("p (a b) -> p a b", a=1), a[:, 0:1, :])
                nc.gpsimd.tensor_copy(ctli[:, 1:5], ctl[:, 1:5]).then_inc(ctl_done, 1)

            norm(0)
            mixer(0)
            after(0, 0)
            norm(1)
            mod_sum(pool, MODS - 1, 1)
            pool.wait_ge(mg_evac, 8)
            for i in range(4):
                nc.gpsimd.memset(wide[:, C * D + i * NB:C * D + (i + 1) * NB], 0.0).then_inc(yadd_done, 1)
            for j in range(4):
                mod_sum(pool, MODS + j, j % MRAW)
            with pool.Fori(0, FBLK - 1) as t:
                for j in range(6):
                    mod_sum(pool, t * 6 + (MODS + 4 + j), j % MRAW)
            mod_sum(pool, 88, 0)
            after(1, 4)
            norm(2)
            mod_sum(pool, 89, 1)
            mixer(1)
            after(2, 6)
            norm(3)
            pool.wait_ge(mg_evac, 16)
            nc.gpsimd.memset(yacc[:], 0.0).then_inc(comb_add, 1)
            pool.wait_ge(x_done, 12)
            for half in range(2):
                nc.gpsimd.memset(ysb[:, half * NB:(half + 1) * NB], 0.0).then_inc(ysb_done, 1)
            pool.wait_ge(lg_done, 1)
            nc.gpsimd.memset(gatT, 0.0).then_inc(gatT_sb, 1)
            extra_items()

            def weights(i):
                pool.wait_ge(comb_add, i * 4 + 1)
                nc.gpsimd.tensor_copy(cur[:, 1, :], wI[:, :, bass.ds(i, 1)].rearrange("p c o -> p (c o)"))\
                    .then_inc(wcur_done, 1)

            def expert(i):
                pool.wait_ge(ctl_done, 1)
                weights(i)

            with pool.Fori(0, E) as i:
                expert(i)
            over = pool.value_load(ctli[0:1, 1:2], min_val=0, max_val=EXTRA)
            with pool.If(over > 0):
                with pool.Fori(0, over) as i:
                    expert(i + E)
            weights(over + E)
            after(3, 10)

        @block.tensor
        def _(pe):
            def three(out, a_hi, a_lo, b_hi, b_lo, first, last, check=True):
                kw = {} if check else {"skip_group_check": True}
                nc.tensor.matmul(out, a_hi, b_hi, start=first, stop=False, **kw)
                nc.tensor.matmul(out, a_lo, b_hi, start=False, stop=False, **kw)
                return nc.tensor.matmul(out, a_hi, b_lo, start=False, stop=last, **kw)

            def unit(s, n):
                hi = whi[:, s % SPLIT, :].rearrange("p (k n) -> p k n", n=n)
                lo = wlo[:, s % SPLIT, :].rearrange("p (k n) -> p k n", n=n)
                return hi, lo

            def use(s, r=0):
                pe.wait_ge(lo_done, number(s, r) + 1)

            def transposes(q):
                for c in range(C):
                    pe.wait_ge(xn_done, C * q + c + 1)
                    if q == 0 and c == 0:
                        pe.wait_ge(const, 8)
                    for half in range(2):
                        for k in range(4):
                            kk = 4 * half + k
                            ins = nc.tensor.transpose(bank[2 * c + half][:, k * P:(k + 1) * P],
                                                      xn[:, c, kk * P:(kk + 1) * P], ident[:])
                        ins.then_inc(xT_done, 1)

            def gate_rows(q):
                pe.wait_ge(gd_done, KC * (q + 1))
                for half in range(2):
                    nc.tensor.matmul(bank[GATE_BANK[q] + half][:], ones[:], gdiag[:, half * NB:(half + 1) * NB],
                                     start=True, stop=True).then_inc(gps_done, 1)

            def mixer(l):
                base = MIX1 if l else MIX0

                def rows_step(s, a_hi, a_lo, kcs, banks, first, last):
                    w_hi, w_lo = unit(s, NB)
                    for c in range(C):
                        cs = slice(c * P, (c + 1) * P)
                        for k in range(4):
                            ins = three(bank[banks[c]][:], a_hi[:, kcs + k, cs], a_lo[:, kcs + k, cs], w_hi[:, k, :],
                                        w_lo[:, k, :], first and k == 0, last and k == 3)
                    return ins

                def scores(p):
                    for s in range(2):
                        z = bank[4 + s]
                        rows = slice(s * DH, (s + 1) * DH)
                        b = 0 if p < 4 else 2
                        qT = qkT[rows, b, p % 4, :]
                        kT = qkT[rows, b + 1, p % 4, :]
                        if p or l:
                            pe.wait_ge(at_done, 16 * l + 2 * p)
                        if p < 4:
                            nc.tensor.matmul(z[:, 0:S], kT[:, 0:P], qT, start=True, stop=True)
                            nc.tensor.matmul(z[:, S:384], kT[:, P:S], qT[:, P:S], start=False, stop=True,
                                             skip_group_check=True).then_inc(z_done, 1)
                        else:
                            nc.tensor.matmul(z[:, 0:S], qT[:, P:S], kT, start=True, stop=True)
                            nc.tensor.matmul(z[:, S:384], qT[:, 0:P], kT[:, 0:P], start=True, stop=True)\
                                .then_inc(z_done, 1)

                def arguments(p):
                    for s in range(2):
                        z = bank[4 + s]
                        if p < 4:
                            pe.wait_ge(sb_lm, 8 * l + 2 * p + s + 1)
                            nc.tensor.matmul(z[:, 0:384], lower[:], at[:, s, :], start=False, stop=True,
                                             skip_group_check=True)
                            nc.tensor.matmul(z[:, P:S], ones[:], at[:, s, S:384], start=False, stop=True,
                                             skip_group_check=True).then_inc(arg_done, 1)
                        else:
                            pe.wait_ge(mo_p, 2 * (8 * l + 2 * (p - 4) + s + 1))
                            nc.tensor.transpose(z[:, 0:P], eb[:, s, S:384], ident[:])
                            nc.tensor.transpose(z[:, P:S], eb[:, s, 0:P], ident[:])
                            nc.tensor.transpose(z[:, S:384], eb[:, s, P:S], ident[:]).then_inc(arg_done, 1)

                def weighted(p):
                    if p or l:
                        pe.wait_ge(olo_done, 8 * l + p)
                    for s in range(2):
                        pe.wait_ge(at_done, 16 * l + 2 * p + s + 1)
                        out = bank[6][s * DH:(s + 1) * DH, :]
                        cols = slice((2 * (p % 4) + s) * DH, (2 * (p % 4) + s + 1) * DH)
                        nc.tensor.matmul(out[:, 0:S], vals[:, p // 4, 0, cols], at[:, s, 0:S], start=True, stop=True)
                        ins = nc.tensor.matmul(out[:, P:S], vals[:, p // 4, 1, cols], at[:, s, S:384], start=False,
                                               stop=True, skip_group_check=True)
                    ins.then_inc(pv_done, 1)

                for u in range(MIX_UNITS):
                    s = base + u
                    use(s)
                    if u < 2:
                        pe.wait_ge(hlo_done, 2 * (2 * l) + u + 1)
                    if u == 0:
                        pe.wait_ge(h32b, KC * (2 * l + 1))
                    if u < 20:
                        j, kh = divmod(u, 2)
                        if kh == 0 and (j >= 2):
                            pe.wait_ge(blk_evac, 2 * (BLK * l + j - 1))
                        if j in (0, 1, 3, 4):
                            w_hi, w_lo = unit(s, NB)
                            for cc in range(4):
                                out = bank[2 * (j % 2) + cc // 2][:, (cc % 2) * S:(cc % 2 + 1) * S]
                                cols = slice(cc * P, (cc + 1) * P)
                                for k in range(4):
                                    kk = 4 * kh + k
                                    ins = three(out, w_hi[:, k, cols], w_lo[:, k, cols], hhi[:, kk, :], hlo[:, kk, :],
                                                kh == 0 and k == 0 and cc % 2 == 0, kh == 1 and k == 3, check=False)
                        else:
                            b2 = 2 * (j % 2)
                            ins = rows_step(s, hhi, hlo, 4 * kh, (b2, b2 + 1), kh == 0, kh == 1)
                        ins.then_inc(unit_used, 1)
                    elif u < 24:
                        half = u % 2
                        branch = (u - 20) // 2
                        if u == 20:
                            pe.wait_ge(blk_evac, 2 * BLK * (l + 1))
                            pe.wait_ge(olo_done, 8 * l + 4)
                        if u == 22:
                            pe.wait_ge(olo_done, 8 * l + 8)
                        if u == 23:
                            pe.wait_ge(mg_evac, 8 * l + 2)
                        banks = [(0, 1), (2, 3), (4, 5), (0, 1)][u - 20]
                        rows_step(s, ohi, olo, 4 * branch, banks, True, True).then_inc(unit_used, 1)
                    else:
                        half, kh = divmod(u - 24, 2)
                        if u == 24:
                            pe.wait_ge(mlo_done, 4 * l + 2)
                            pe.wait_ge(mg_evac, 8 * (l + 1))
                        if u == 25:
                            pe.wait_ge(mlo_done, 4 * l + 4)
                        banks = [(0, 1), (2, 3)][half]
                        rows_step(s, hhi, hlo, 4 * kh, banks, kh == 0, kh == 1).then_inc(unit_used, 1)
                    if 7 <= u < 23 and (u - 7) % 2 == 0:
                        weighted((u - 7) // 2)
                    if 6 <= u < 22 and (u - 6) % 2 == 0:
                        arguments((u - 6) // 2)
                    if 5 <= u < 21 and (u - 5) % 2 == 0:
                        if u == 5:
                            pe.wait_ge(blk_evac, 2 * (BLK * l + 2))
                        if u == 13:
                            pe.wait_ge(blk_evac, 2 * (BLK * l + 5))
                        scores((u - 5) // 2)
                    if u in (6, 14):
                        pe.wait_ge(blk_evac, 2 * (BLK * l + (3 if u == 6 else 6)))
                    if l == 0 and u in (1, 23):
                        pe.wait_ge(mod_evac, 1 if u == 1 else 2)
                    if l and u == 0:
                        mod_column(pe, 89, 1)
                    if u:
                        for m in mods_of_step(l, u - 1):
                            mod_column(pe, m, m % MRAW)
                    if u == 23:
                        for i in range(4):
                            half, c = divmod(i, 2)
                            pe.wait_ge(mg_evac, 8 * l + 4 + 2 * half + c + 1)
                            for k in range(4):
                                kk = 4 * half + k
                                ins = nc.tensor.transpose(bank[[2, 3, 6, 4][i]][:, k * P:(k + 1) * P],
                                                          merged[:, c, kk * P:(kk + 1) * P], ident[:])
                            ins.then_inc(mT_done, 1)
                    if u == 25:
                        gate_rows(2 * l)
            def up(n, s, r, kh, banks):
                use(s, r)
                w_hi, w_lo = unit(s, NB)
                for c in range(n):
                    cs = slice(c * P, (c + 1) * P)
                    for k in range(4):
                        ins = three(bank[banks + c][:], hhi[:, 4 * kh + k, cs], hlo[:, 4 * kh + k, cs], w_hi[:, k, :],
                                    w_lo[:, k, :], kh == 0 and k == 0, kh == 1 and k == 3)
                ins.then_inc(unit_used, 1)

            def hidden_T(n, t, c):
                pe.wait_ge(g_done, t * n + (base_of[n] + c + 1))
                wait_at_least(pe, gl_done, t * n + (base_of[n] + c))
                for k in range(4):
                    ins = nc.tensor.transpose(bank[6][:, k * P:(k + 1) * P], hid[:, c, k * P:(k + 1) * P], ident[:])
                ins.then_inc(gT_done, 1)

            def dense_down(t, s, r, b, last=False):
                pe.wait_ge(gl_done, t * 2 + 2)
                pe.wait_ge(silu_done, t * 2 + (2 if last else 4))
                pe.wait_ge(yadd_done, t * 4 + 4)
                for part in range(2):
                    use(s + part, r)
                    w_hi, w_lo = unit(s + part, D)
                    for c in (1, 0) if part else (0, 1):
                        for half in range(2):
                            cols = slice(half * NB, (half + 1) * NB)
                            for k in range(2):
                                hk = hidden_half(b).start + 2 * part + k
                                cs = slice(c * P, (c + 1) * P)
                                ins = three(bank[(0 if c else 4) + half][:], ohi[:, hk, cs], olo[:, hk, cs],
                                            w_hi[:, k, cols], w_lo[:, k, cols], part == 0 and k == 0,
                                            part == 1 and k == 1)
                            if part and not (c == 0 and half):
                                ins.then_inc(yp_done, 1)
                            if not part and not last and (c, half) in ((0, 1), (1, 1)):
                                if c:
                                    ins.then_inc(unit_used, 1)
                                hidden_T(2, t + 1, c)
                            elif not part and c and half:
                                ins.then_inc(unit_used, 1)
                    if part:
                        ins.then_inc(unit_used, 1)

            def expert_down(s, r, part, b, last=False):
                use(s, r)
                w_hi, w_lo = unit(s, D)
                for k in range(2):
                    kk = hidden_half(b).start + 2 * part + k
                    for half in range(2):
                        cols = slice(half * NB, (half + 1) * NB)
                        ins = three(bank[4 + half][:], ohi[:, kk, 0:P], olo[:, kk, 0:P], w_hi[:, k, cols],
                                    w_lo[:, k, cols], False, last and k == 1, check=False)
                ins.then_inc(unit_used, 1)

            base_of = {2: FFN_BASE[0], 1: FFN_BASE[1]}

            pe.wait_ge(const, 8)
            pe.wait_ge(small_in, 16 * 7)
            nc.tensor.transpose(bank[4][:, 0:DEPTH * MODS], rowsM, ident[0:DEPTH * MODS, 0:DEPTH * MODS])\
                .then_inc(cols_ps, 1)
            nc.tensor.transpose(bank[4][:, P:P + 72], rowsB, ident[0:72, 0:72]).then_inc(cols_ps, 1)
            pe.wait_ge(rel_in, 32)
            nc.tensor.matmul(bank[5][0:HEADS, 0:DIST], relx, onehot, start=True, stop=True).then_inc(dist_ps, 1)
            transposes(0)
            pe.wait_ge(cond_done, 1)
            for i in range(MOD_UNITS):
                cb, kh = divmod(i, 2)
                pe.wait_ge(raw_full[i % RAW], 16 * (i // RAW + 1))
                if cb >= 2 and kh == 0:
                    pe.wait_ge(mod_row, cb - 1)
                for k in range(4):
                    ins = nc.tensor.matmul(bank[6 + cb % 2][0:1, :], cond[:, 4 * kh + k:4 * kh + k + 1],
                                           raw[:, i % RAW, k * NB:(k + 1) * NB], start=kh == 0 and k == 0,
                                           stop=kh == 1 and k == 3)
                ins.then_inc(mod_unit, 1)
                if i in (5, 7):
                    pe.wait_ge(hank_in, 16)
                    pe.wait_ge(cols_sb, 2)
                    pe.wait_ge(dist_sb, 1)
                    if i == 7:
                        pe.wait_ge(bias_sb, 2)
                    for t in range(2):
                        h = 2 * (t + (i - 5))
                        nc.tensor.matmul(bank[4 + t][:], flip, hank[:, h:h + 2, :].rearrange("p h j -> p (h j)"),
                                         start=True, stop=True).then_inc(flip_ps, 1)
            for m in range(MOD_FIRST):
                if m == 0:
                    pe.wait_ge(mod_row, 4)
                ins = nc.tensor.matmul(MODB[:, m:m + 1], modrow[:, m * P:(m + 1) * P], ones[0:1, 0:1], start=True,
                                       stop=True)
            ins.then_inc(mod_first, 1)
            mixer(0)
            transposes(1)
            mod_column(pe, MODS - 1, 1)
            for j in range(4):
                if j < 2:
                    pe.wait_ge(hlo_done, 2 + j + 1)
                up(2, FFN0 + j, 0, j % 2, 2 * (j // 2))
                if j == 2:
                    gate_rows(1)
                if j == 1:
                    pe.wait_ge(mod_evac, 3)
                if j:
                    mod_column(pe, MODS + j - 1, (j - 1) % MRAW)
            pe.wait_ge(gate_sb, 4)
            for c in range(C):
                hidden_T(2, 0, c)
            with pe.Fori(0, (FBLK - 1) // 2) as tt:
                for q in range(2):
                    s0 = FFN0 + 4 + 6 * q
                    t = tt * 2 + q
                    for j in range(6):
                        if j == 0:
                            pe.wait_ge(silu_done, t * 2 + 2)
                            pe.wait_ge(yadd_done, t * 4 + 2)
                        if j == 2:
                            pe.wait_ge(g_done, t * 2 + 2)
                        if j < 4:
                            up(2, s0 + j, tt * 2, j % 2, 2 * (j // 2))
                        if j == 4:
                            dense_down(t, s0 + 4, tt * 2, q)
                        mod_column(pe, tt * 12 + (MODS + 3 + 6 * q + j), (j + 1) % MRAW)
            dense_down(FBLK - 1, FFN0 + 4 + 6 * (FBLK - 1), 0, FBLK - 1, last=True)
            transposes(2)
            pe.wait_ge(mod_evac, 4)
            for m in range(87, 89):
                mod_column(pe, m, m % MRAW)
            mixer(1)
            transposes(3)

            pe.wait_ge(gate_sb, 6)
            for c in range(C):
                for k in range(KC):
                    pe.wait_ge(h32b if k >= 4 else h32a, KC * 3 + 4 * c + k % 4 + 1)
                    ins = nc.tensor.matmul(bank[4][:, c * E:(c + 1) * E], h32[:, k, c * P:(c + 1) * P], wr[:, k, :],
                                           start=k == 0, stop=k == KC - 1)
            ins.then_inc(lg_done, 1)
            gate_rows(3)
            pe.wait_ge(mem_done, 1)
            mem = rt[:, 7, :, :]
            b5 = bank[5]
            nc.tensor.matmul(b5[:, 0:E], upper[:], mem[:, 0, :], start=True, stop=True)
            nc.tensor.matmul(b5[:, E:2 * E], ones[:], mem[:, 0, :], start=True, stop=False)
            nc.tensor.matmul(b5[:, E:2 * E], upper[:], mem[:, 1, :], start=False, stop=True)
            nc.tensor.matmul(b5[:, 2 * E:3 * E], ones[:], mem[:, 0, :], start=True, stop=False)
            nc.tensor.matmul(b5[:, 2 * E:3 * E], ones[:], mem[:, 1, :], start=False, stop=True).then_inc(pos_done, 1)

            def gather(item, half):
                pe.wait_ge(gat_done, item * 2 + 2)
                for k in range(4):
                    kk = 4 * half + k
                    for c in range(C):
                        ins = nc.tensor.matmul(bank[2 + half][:, k * P:(k + 1) * P], xn[:, c, kk * P:(kk + 1) * P],
                                               gat[:, c, :], start=c == 0, stop=c == C - 1)
                ins.then_inc(gath_done, 1)

            def slots_T(item):
                for c in range(C):
                    ins = nc.tensor.transpose(bank[7][:, c * P:(c + 1) * P], gat[:, c, :], ident[:])
                ins.then_inc(gatT_ps, 1)

            for half in range(2):
                gather(0, half)
            pe.wait_ge(gate_sb, 8)

            def combine(i, c):
                pe.wait_ge(gatT_sb, i + 1)
                pe.wait_ge(h32e_done, i * KC + KC)
                for half in range(2):
                    pe.wait_ge(ysb_done, i * 2 + half + 1)
                    if c:
                        pe.wait_ge(comb_add, i * 4 + (half + 2))
                    nc.tensor.matmul(bank[2 + half][:], gatT[:, c * P:(c + 1) * P], ysb[:, half * NB:(half + 1) * NB],
                                     start=True, stop=True).then_inc(comb_ps, 1)

            def expert(i):
                pe.wait_ge(elo_done, i + 1)
                for j in range(4):
                    if j == 0:
                        pe.wait_ge(silu_done, i * FBLK + base_of[1])
                    if j == 2:
                        pe.wait_ge(g_done, i * FBLK + base_of[1])
                    up(1, MOE0 + j, i * FBLK, j % 2, j // 2)
                    if j < 2:
                        combine(i, j)
                    if j == 2:
                        slots_T(i)
                pe.wait_ge(comb_add, i * 4 + 5)
                gather(i + 1, 0)
                hidden_T(1, i * FBLK, 0)
                gather(i + 1, 1)
                with pe.Fori(0, (FBLK - 1) // 2) as tt:
                    for q in range(2):
                        s0 = MOE0 + 4 + 6 * q
                        t = i * FBLK + tt * 2 + q
                        for j in range(6):
                            if j == 0:
                                pe.wait_ge(silu_done, t + (base_of[1] + 1))
                            if j == 2:
                                pe.wait_ge(g_done, t + (base_of[1] + 1))
                            if j < 4:
                                up(1, s0 + j, i * FBLK + tt * 2, j % 2, j // 2)
                            if j == 4:
                                pe.wait_ge(gl_done, t + (base_of[1] + 1))
                                pe.wait_ge(yzero, i * 2 + 2)
                            if j >= 4:
                                expert_down(s0 + j, i * FBLK + tt * 2, j - 4, q)
                            if j == 4:
                                hidden_T(1, t + 1, 0)
                pe.wait_ge(gl_done, i * FBLK + (base_of[1] + FBLK))
                for j in range(2):
                    expert_down(MOE0 + FFN_UNITS - 2 + j, i * FBLK, j, FBLK - 1, last=j == 1)

            with pe.Fori(0, E) as i:
                expert(i)
            pe.wait_ge(ctl_done, 1)
            over = pe.value_load(ctli[0:1, 1:2], min_val=0, max_val=EXTRA)
            with pe.If(over > 0):
                with pe.Fori(0, over) as i:
                    expert(i + E)
            for c in range(C):
                combine(over + E, c)


def _bucket_onehot():
    import numpy as np
    table = np.zeros((BUCKETS + 1, DIST), np.float32)
    exact = BUCKETS // 2
    for i in range(DIST):
        dist = S - 1 - i
        if dist < 0:
            table[BUCKETS, i] = 1
        elif dist < exact:
            table[dist, i] = 1
        else:
            large = exact + int(np.float32(np.log(np.float32(dist) / np.float32(exact)))
                                / np.float32(np.log(128 / exact)) * np.float32(BUCKETS - exact))
            table[min(large, BUCKETS - 1), i] = 1
    return table


_INS = ["x", "c", "w_mod", "b_mod", "g_mix_pre", "g_mix_post", "g_ffn_pre", "g_ffn_post", "w_in", "w_proj_sb",
        "w_proj_moba", "w_out", "rel_bias", "w1_dense", "w3_dense", "w2_dense", "w_router", "w1_moe", "w3_moe",
        "w2_moe"]


def kernel(**inputs):
    import numpy as np
    import concourse.bacc as bacc
    from concourse.bass_utils import run_bass_kernel_spmd as run

    nc = bacc.Bacc("TRN2", target_bir_lowering=False, num_devices=1)
    arrays = {f"in_{name}": np.ascontiguousarray(inputs[name]) for name in _INS}
    arrays["in_bucket_onehot"] = _bucket_onehot()
    args = [nc.dram_tensor(k, a.shape, mybir.dt.from_np(a.dtype), kind="ExternalInput").ap()
            for k, a in arrays.items()]
    scratch = nc.dram_tensor("dist_scratch", (HEADS, 384), F32, kind="Internal").ap()
    out = nc.dram_tensor("out_0", (1, S, D), F32, kind="ExternalOutput").ap()
    build(nc, *args, scratch, out)
    r = run(nc, [arrays], core_ids=[0])
    return r.results[0]["out_0"]
```
